# Optimizing a Trainium2 kernel written in Bass

```python
import jax, jax.numpy as jnp
from jax import lax
import numpy as np
import math

D_MODEL = 1024
BATCH = 1
SEQ = 2048
DEPTH = 1

EXPAND = 2
D_MIX = EXPAND * D_MODEL
D_CONV = D_MIX // 2
D_GMLP = D_MIX - D_CONV
CONV_GROUPS = 8
CONV_GROUP_DIM = D_CONV // CONV_GROUPS
GMLP_HEADS = 8
GMLP_HEAD_DIM = D_GMLP // GMLP_HEADS
CONV_WIDTH = 31
CONV_HALF = CONV_WIDTH // 2
CHUNK = 128
EPS = 1e-6
D_IN = 3 * D_CONV + 3 * D_GMLP
SPLITS = (D_CONV, 2 * D_CONV, 3 * D_CONV, 3 * D_CONV + D_GMLP, 3 * D_CONV + 2 * D_GMLP)


def rms_norm(x, g):
    xf = x.astype(jnp.float32)
    xf = xf * lax.rsqrt(jnp.mean(xf * xf, axis=-1, keepdims=True) + EPS)
    return (xf * g.astype(jnp.float32)).astype(x.dtype)

def layer_norm(x, g, b):
    xf = x.astype(jnp.float32)
    mu = jnp.mean(xf, axis=-1, keepdims=True)
    var = jnp.mean(jnp.square(xf - mu), axis=-1, keepdims=True)
    y = (xf - mu) * lax.rsqrt(var + EPS) * g.astype(jnp.float32) + b.astype(jnp.float32)
    return y.astype(x.dtype)

def first_inputs(seed: int = 0) -> dict:
    key = jax.random.key(seed)
    ks = jax.random.split(key, 16)
    L = DEPTH
    nrm = jax.random.normal
    return {
        "x": nrm(ks[0], (BATCH, SEQ, D_MODEL), jnp.float32),
        "c": nrm(ks[1], (BATCH, D_MODEL), jnp.float32),
        "w_ada": nrm(ks[2], (L, D_MODEL, 3 * D_MODEL), jnp.float32) * D_MODEL ** -0.5,
        "b_ada": nrm(ks[3], (L, 3 * D_MODEL), jnp.float32) * 0.02,
        "norm_g": 1.0 + 0.02 * nrm(ks[4], (L, D_MODEL), jnp.float32),
        "w_in": nrm(ks[5], (L, D_MODEL, D_IN), jnp.float32) * D_MODEL ** -0.5,
        "conv_w": nrm(ks[6], (L, CONV_WIDTH, 1, D_CONV), jnp.float32) * CONV_WIDTH ** -0.5,
        "conv_b": nrm(ks[7], (L, D_CONV), jnp.float32) * 0.02,
        "conv_ln_g": 1.0 + 0.02 * nrm(ks[8], (L, D_CONV), jnp.float32),
        "conv_ln_b": nrm(ks[9], (L, D_CONV), jnp.float32) * 0.02,
        "sg_ln_g": 1.0 + 0.02 * nrm(ks[10], (L, D_GMLP), jnp.float32),
        "sg_ln_b": nrm(ks[11], (L, D_GMLP), jnp.float32) * 0.02,
        "w_s": nrm(ks[12], (L, GMLP_HEADS, CHUNK, CHUNK), jnp.float32) * CHUNK ** -0.5,
        "b_s": 1.0 + 0.02 * nrm(ks[13], (L, GMLP_HEADS, CHUNK), jnp.float32),
        "w_out": nrm(ks[14], (L, D_MIX, D_MODEL), jnp.float32) * D_MIX ** -0.5,
        "final_g": 1.0 + 0.02 * nrm(ks[15], (D_MODEL,), jnp.float32),
    }

def conv_group(a, a_glu, a_gate, conv_w, conv_b, ln_g, ln_b):
    a = a * jax.nn.sigmoid(a_glu)
    a = lax.conv_general_dilated(
        a, conv_w.astype(a.dtype), window_strides=(1,),
        padding=[(CONV_HALF, CONV_HALF)],
        dimension_numbers=("NWC", "WIO", "NWC"),
        feature_group_count=D_CONV) + conv_b
    a = jax.nn.silu(layer_norm(a, ln_g, ln_b))
    return a * jax.nn.silu(a_gate)

def gmlp_group(u, v, b_gate, ln_g, ln_b, w_s, b_s):
    B, S, _ = v.shape
    v = layer_norm(v, ln_g, ln_b)
    v = v.reshape(B, S // CHUNK, CHUNK, GMLP_HEADS, GMLP_HEAD_DIM)
    v = jnp.einsum("hpq,bnqhd->bnphd", w_s.astype(v.dtype), v) \
        + jnp.transpose(b_s)[None, None, :, :, None]
    v = v.reshape(B, S, D_GMLP)
    return u * v * jax.nn.silu(b_gate)

def first_block(x, c, w_ada, b_ada, norm_g, w_in, conv_w, conv_b, conv_ln_g, conv_ln_b,
              sg_ln_g, sg_ln_b, w_s, b_s, w_out, final_g):
    c_act = jax.nn.silu(c)
    for l in range(DEPTH):
        mod = jnp.einsum("bd,de->be", c_act, w_ada[l]) + b_ada[l]
        shift, scale, gate = jnp.split(mod, 3, axis=-1)
        h = rms_norm(x, norm_g[l]) * (1.0 + scale[:, None, :]) + shift[:, None, :]
        z = jnp.einsum("bsd,de->bse", h, w_in[l])
        a, a_glu, a_gate, u, v, b_gate = jnp.split(z, SPLITS, axis=-1)
        y_a = conv_group(a, a_glu, a_gate, conv_w[l], conv_b[l], conv_ln_g[l], conv_ln_b[l])
        y_b = gmlp_group(u, v, b_gate, sg_ln_g[l], sg_ln_b[l], w_s[l], b_s[l])
        y = jnp.einsum("bse,ed->bsd", jnp.concatenate([y_a, y_b], axis=-1), w_out[l])
        x = x + gate[:, None, :] * y
    return rms_norm(x, final_g)


_first_inputs = first_inputs


def first_inputs(seed=0):
    import zlib

    import numpy as np

    out = dict(_first_inputs(seed))
    spreads = {}
    factors = {'norm_g': 3.44,
     'conv_b': 53.164,
     'conv_ln_g': 64.0,
     'conv_ln_b': 64.0,
     'sg_ln_g': 29.133,
     'sg_ln_b': 26.972,
     'b_s': 28.127,
     'final_g': 8.09}
    for name, (base, spread) in spreads.items():
        noise = np.random.default_rng([zlib.crc32(name.encode()), seed]).standard_normal(out[name].shape)
        drawn = base * np.exp(spread * noise) if base else spread * noise
        out[name] = __import__('jax').numpy.asarray(drawn.astype(out[name].dtype))
    for name, factor in factors.items():
        out[name] = (out[name] * factor).astype(out[name].dtype)
    return out


_narrow_inputs = first_inputs


def first_inputs(seed=0):

    out = dict(_narrow_inputs(seed))
    wider = {'conv_ln_g': 12.0,
     'conv_ln_b': 12.0,
     'sg_ln_g': 4.75,
     'sg_ln_b': 4.76,
     'b_s': 4.74,
     'final_g': 3.19}
    for name, times in wider.items():
        mean = out[name].mean()
        out[name] = (mean + times * (out[name] - mean)).astype(out[name].dtype)
    return out


D_MIX_2 = D_MODEL
HYENA_WIDTH = D_MIX_2 // 2
POOL_WIDTH = D_MIX_2 - HYENA_WIDTH
HYENA_ORDER = 2
N_DIRECTIONS = 2
SHORT_CONV = 3
FILTER_EMB = 33
FILTER_BANDS = (FILTER_EMB - 1) // 2
FILTER_HIDDEN = 64
FAST_DECAY_PCT = 0.3
SLOW_DECAY_PCT = 1.5
DECAY_TARGET = 1e-2
POOL_WINDOWS = (2, 4, 8, 16)
POOL_GROUP = POOL_WIDTH // len(POOL_WINDOWS)
HYENA_IN = (HYENA_ORDER + 1) * HYENA_WIDTH
PROJ_WIDTH = HYENA_IN + HYENA_WIDTH + 2 * POOL_WIDTH


def rms_norm_2(x, g):
    xf = x.astype(jnp.float32)
    y = xf * lax.rsqrt(jnp.mean(xf * xf, axis=-1, keepdims=True) + EPS)
    return (y * g.astype(jnp.float32)).astype(x.dtype)

def short_conv(u, w, b):
    L = u.shape[1]
    up = jnp.pad(u, ((0, 0), (1, 1), (0, 0)))
    return up[:, :L] * w[0] + up[:, 1:L + 1] * w[1] + up[:, 2:] * w[2] + b

def hyena_filters(L, w1, b1, w2, b2, w3, b3, freq, w_proj):
    f32 = jnp.float32
    w1, b1, w2, b2, w3, b3, freq, w_proj = [a.astype(f32) for a in (w1, b1, w2, b2, w3, b3, freq, w_proj)]
    t = jnp.linspace(0.0, 1.0, L, dtype=f32)[:, None]
    pos = jnp.arange(L, dtype=f32)[:, None]
    ang = 2.0 * math.pi * pos / L
    bands = jnp.linspace(1e-4, FILTER_BANDS - 1, FILTER_BANDS, dtype=f32)[None, :]
    z = jnp.concatenate([t, jnp.cos(bands * ang), -jnp.sin(bands * ang)], axis=-1)
    h = jnp.sin(freq * (z @ w1 + b1))
    h = jnp.sin(freq * (h @ w2 + b2))
    h = jnp.sin(freq * (h @ w3 + b3))
    h = (h @ w_proj).reshape(L, HYENA_ORDER, N_DIRECTIONS, HYENA_WIDTH)
    max_decay = math.log(DECAY_TARGET) / FAST_DECAY_PCT
    min_decay = math.log(DECAY_TARGET) / SLOW_DECAY_PCT
    deltas = jnp.linspace(min_decay, max_decay, HYENA_WIDTH, dtype=f32)
    decay = jnp.exp(-t * jnp.abs(deltas)[None, :])
    return h * decay[:, None, None, :]

def two_sided_spectrum(h):
    L = h.shape[0]
    k_fwd = h[:, :, 0]
    k_bwd = h[:, :, 1]
    k_full = jnp.concatenate([k_fwd, jnp.zeros_like(k_fwd[:1]), k_bwd[:0:-1]], axis=0)
    return jnp.fft.rfft(k_full, n=2 * L, axis=0)

def fft_conv(u, k_f, d):
    L = u.shape[1]
    uf = u.astype(jnp.float32)
    u_f = jnp.fft.rfft(uf, n=2 * L, axis=1)
    y = jnp.fft.irfft(u_f * k_f[None], n=2 * L, axis=1)[:, :L]
    return (y + uf * d.astype(jnp.float32)).astype(u.dtype)

def multiscale_pool(u, pool_w, pool_scale):
    B, L, C = u.shape
    uf = u.astype(jnp.float32)
    S = jnp.concatenate([jnp.zeros((B, 1, C), jnp.float32), jnp.cumsum(uf, axis=1)], axis=1)
    pos = jnp.arange(L)
    outs = []
    for g, w in enumerate(POOL_WINDOWS):
        sl = slice(g * POOL_GROUP, (g + 1) * POOL_GROUP)
        lo = jnp.clip(pos - w // 2, 0, L - 1)
        hi = jnp.clip(pos + (w - 1 - w // 2), 0, L - 1)
        total = jnp.take(S[..., sl], hi + 1, axis=1) - jnp.take(S[..., sl], lo, axis=1)
        cnt = (hi - lo + 1).astype(jnp.float32)[None, :, None]
        pooled = total / cnt - uf[..., sl]
        outs.append(jnp.einsum('blc,cd->bld', pooled, pool_w[g].astype(jnp.float32)))
    y = jnp.concatenate(outs, axis=-1) * pool_scale.astype(jnp.float32)
    return y.astype(u.dtype)

def hybrid_layer(x, pre_g, w_in, conv_w, conv_b, fw1, fb1, fw2, fb2, fw3, fb3, ffreq, fw_out,
                 hyena_d, pool_w, pool_scale, norm_h_g, norm_p_g, w_out, post_g):
    L = x.shape[1]
    h = rms_norm_2(x, pre_g)
    p = jnp.einsum('bld,dk->blk', h, w_in)
    hy = short_conv(p[..., :HYENA_IN], conv_w, conv_b)
    v = hy[..., :HYENA_WIDTH]
    gates = (hy[..., HYENA_WIDTH:2 * HYENA_WIDTH], hy[..., 2 * HYENA_WIDTH:])
    z_h = p[..., HYENA_IN:HYENA_IN + HYENA_WIDTH]
    u_p = p[..., HYENA_IN + HYENA_WIDTH:HYENA_IN + HYENA_WIDTH + POOL_WIDTH]
    z_p = p[..., HYENA_IN + HYENA_WIDTH + POOL_WIDTH:]
    k_f = two_sided_spectrum(hyena_filters(L, fw1, fb1, fw2, fb2, fw3, fb3, ffreq, fw_out))
    y = v
    for o in range(HYENA_ORDER):
        y = gates[o] * fft_conv(y, k_f[:, o], hyena_d[o])
    y_h = rms_norm_2(y * jax.nn.silu(z_h), norm_h_g)
    y_p = rms_norm_2(multiscale_pool(u_p, pool_w, pool_scale) * jax.nn.silu(z_p), norm_p_g)
    out = jnp.einsum('blk,kd->bld', jnp.concatenate([y_h, y_p], axis=-1), w_out)
    return x + rms_norm_2(out, post_g)

def second_inputs(seed: int = 0) -> dict:
    key = jax.random.key(seed)
    ks = jax.random.split(key, 24)

    def nrm(k, shape, scale):
        return jax.random.normal(k, shape, jnp.float32) * scale

    n_filt_out = HYENA_ORDER * N_DIRECTIONS * HYENA_WIDTH
    return {
        'x': nrm(ks[0], (BATCH, SEQ, D_MODEL), 1.0),
        'pre_norm_g': 1.0 + nrm(ks[1], (DEPTH, D_MODEL), 0.02),
        'w_in': nrm(ks[2], (DEPTH, D_MODEL, PROJ_WIDTH), D_MODEL ** -0.5),
        'conv_w': nrm(ks[3], (DEPTH, SHORT_CONV, HYENA_IN), SHORT_CONV ** -0.5),
        'conv_b': nrm(ks[4], (DEPTH, HYENA_IN), 0.01),
        'filt_w1': nrm(ks[5], (DEPTH, FILTER_EMB, FILTER_HIDDEN), FILTER_EMB ** -0.5),
        'filt_b1': nrm(ks[6], (DEPTH, FILTER_HIDDEN), 0.1),
        'filt_w2': nrm(ks[7], (DEPTH, FILTER_HIDDEN, FILTER_HIDDEN), FILTER_HIDDEN ** -0.5),
        'filt_b2': nrm(ks[8], (DEPTH, FILTER_HIDDEN), 0.1),
        'filt_w3': nrm(ks[9], (DEPTH, FILTER_HIDDEN, FILTER_HIDDEN), FILTER_HIDDEN ** -0.5),
        'filt_b3': nrm(ks[10], (DEPTH, FILTER_HIDDEN), 0.1),
        'filt_freq': 1.0 + nrm(ks[11], (DEPTH, FILTER_HIDDEN), 0.02),
        'filt_w_out': nrm(ks[12], (DEPTH, FILTER_HIDDEN, n_filt_out), 0.5 * FILTER_HIDDEN ** -0.5),
        'hyena_d': nrm(ks[13], (DEPTH, HYENA_ORDER, HYENA_WIDTH), 0.5),
        'pool_w': nrm(ks[14], (DEPTH, len(POOL_WINDOWS), POOL_GROUP, POOL_GROUP), POOL_GROUP ** -0.5),
        'pool_scale': 1.0 + nrm(ks[15], (DEPTH, POOL_WIDTH), 0.02),
        'norm_h_g': 1.0 + nrm(ks[16], (DEPTH, HYENA_WIDTH), 0.02),
        'norm_p_g': 1.0 + nrm(ks[17], (DEPTH, POOL_WIDTH), 0.02),
        'w_out': nrm(ks[18], (DEPTH, D_MIX_2, D_MODEL), D_MIX_2 ** -0.5),
        'post_norm_g': 1.0 + nrm(ks[19], (DEPTH, D_MODEL), 0.02),
    }

def second_block(x, pre_norm_g, w_in, conv_w, conv_b, filt_w1, filt_b1, filt_w2, filt_b2, filt_w3, filt_b3,
              filt_freq, filt_w_out, hyena_d, pool_w, pool_scale, norm_h_g, norm_p_g, w_out, post_norm_g):
    for i in range(DEPTH):
        x = hybrid_layer(x, pre_norm_g[i], w_in[i], conv_w[i], conv_b[i],
                         filt_w1[i], filt_b1[i], filt_w2[i], filt_b2[i], filt_w3[i], filt_b3[i],
                         filt_freq[i], filt_w_out[i], hyena_d[i], pool_w[i], pool_scale[i],
                         norm_h_g[i], norm_p_g[i], w_out[i], post_norm_g[i])
    return x


_first_inputs_2 = second_inputs


def second_inputs(seed=0):
    import zlib

    import numpy as np

    out = dict(_first_inputs_2(seed))
    spreads = {}
    factors = {}
    for name, (base, spread) in spreads.items():
        noise = np.random.default_rng([zlib.crc32(name.encode()), seed]).standard_normal(out[name].shape)
        drawn = base * np.exp(spread * noise) if base else spread * noise
        out[name] = __import__('jax').numpy.asarray(drawn.astype(out[name].dtype))
    for name, factor in factors.items():
        out[name] = (out[name] * factor).astype(out[name].dtype)
    return out


_narrow_inputs_2 = second_inputs


def second_inputs(seed=0):

    out = dict(_narrow_inputs_2(seed))
    wider = {'pool_scale': 6.53, 'norm_h_g': 6.72, 'norm_p_g': 6.79, 'post_norm_g': 4.5}
    for name, times in wider.items():
        mean = out[name].mean()
        out[name] = (mean + times * (out[name] - mean)).astype(out[name].dtype)
    return out


GRID_W = 64
D_MIX_3 = D_MODEL
D_ATT = D_MIX_3 // 2
D_HG = D_MIX_3 - D_ATT
ATT_HEADS = 8
ATT_HEAD_DIM = D_ATT // ATT_HEADS
HG_HEADS = 4
HG_HEAD_DIM = D_HG // HG_HEADS
WIN_ROWS_MAX = 8
WIN_COLS = 16
Q_BLOCK_W = 16
K_BLOCK_W = 32
HG_CHUNK = 64
IN_WIDTHS = (D_ATT, D_ATT, D_ATT, D_ATT, D_HG, D_HG, D_HG, D_HG, D_HG)
D_IN_3 = sum(IN_WIDTHS)
LN_EPS = 1e-5
RMS_EPS = 1e-6
DEEPNORM_ALPHA = (2.0 * DEPTH) ** 0.25
DEEPNORM_BETA = (8.0 * DEPTH) ** -0.25


def neighbourhood_attention(q, k, v, rpb):
    B, T, H, dh = q.shape
    rows = T // GRID_W
    kr = min(WIN_ROWS_MAX, rows)
    q = q.reshape(B, rows, GRID_W, H, dh)
    k = k.reshape(B, rows, GRID_W, H, dh)
    v = v.reshape(B, rows, GRID_W, H, dh)
    r = np.arange(rows)
    row_start = np.clip(r - kr // 2, 0, rows - kr)
    row_idx = row_start[:, None] + np.arange(kr)[None, :]
    dr = row_idx - r[:, None] + (WIN_ROWS_MAX - 1)
    k_rows = k[:, row_idx]
    v_rows = v[:, row_idx]
    scale = dh ** -0.5
    outs = []
    for j in range(GRID_W // Q_BLOCK_W):
        qc = np.arange(j * Q_BLOCK_W, (j + 1) * Q_BLOCK_W)
        kc0 = int(np.clip(j * Q_BLOCK_W - WIN_COLS // 2, 0, GRID_W - K_BLOCK_W))
        kc = np.arange(kc0, kc0 + K_BLOCK_W)
        col_start = np.clip(qc - WIN_COLS // 2, 0, GRID_W - WIN_COLS)
        in_win = (kc[None, :] >= col_start[:, None]) & (kc[None, :] < col_start[:, None] + WIN_COLS)
        dc = np.clip(kc[None, :] - qc[:, None], -(WIN_COLS - 1), WIN_COLS - 1) + (WIN_COLS - 1)
        q_blk = q[:, :, j * Q_BLOCK_W:(j + 1) * Q_BLOCK_W]
        k_blk = k_rows[:, :, :, kc0:kc0 + K_BLOCK_W]
        v_blk = v_rows[:, :, :, kc0:kc0 + K_BLOCK_W]
        s = jnp.einsum('brqhd,brakhd->bhrqak', q_blk, k_blk,
                       preferred_element_type=jnp.float32) * scale
        bias = rpb[:, dr[:, None, :, None], dc[None, :, None, :]]
        s = jnp.where(in_win[None, None, None, :, None, :], s + bias[None].astype(jnp.float32), -jnp.inf)
        p = jax.nn.softmax(s.reshape(B, H, rows, Q_BLOCK_W, kr * K_BLOCK_W), axis=-1)
        p = p.reshape(B, H, rows, Q_BLOCK_W, kr, K_BLOCK_W).astype(v.dtype)
        outs.append(jnp.einsum('bhrqak,brakhd->brqhd', p, v_blk))
    o = jnp.concatenate(outs, axis=2)
    return o.reshape(B, T, H * dh)

def hgrn2_chunk_scan(q, k, v, log_f):
    B, H, T, dk = q.shape
    dv = v.shape[-1]
    n = T // HG_CHUNK
    causal = np.tril(np.ones((HG_CHUNK, HG_CHUNK), dtype=bool))

    def to_chunks(a):
        return jnp.moveaxis(a.reshape(B, H, n, HG_CHUNK, a.shape[-1]), 2, 0)

    def step(S, inp):
        qc, kc, vc, gc = inp
        b = jnp.cumsum(gc, axis=2)
        b_last = b[:, :, -1:, :]
        o_inter = jnp.einsum('bhtd,bhde->bhte', qc * jnp.exp(b), S)
        diff = jnp.where(causal[:, :, None], b[:, :, :, None, :] - b[:, :, None, :, :], -jnp.inf)
        a = jnp.einsum('bhtd,bhtsd,bhsd->bhts', qc, jnp.exp(diff), kc)
        o_intra = jnp.einsum('bhts,bhse->bhte', a, vc)
        S = jnp.exp(b_last[:, :, 0, :, None]) * S + jnp.einsum('bhsd,bhse->bhde', kc * jnp.exp(b_last - b), vc)
        return S, o_inter + o_intra

    S0 = jnp.zeros((B, H, dk, dv), jnp.float32)
    _, o = lax.scan(step, S0, (to_chunks(q), to_chunks(k), to_chunks(v), to_chunks(log_f)))
    return jnp.moveaxis(o, 0, 2).reshape(B, H, T, dv)

def hgrn2_forget(z, lb_logits, layer):
    lb = jnp.cumsum(jax.nn.softmax(lb_logits.astype(jnp.float32), axis=0), axis=0)[layer]
    lb = lb.reshape(HG_HEADS, 1, HG_HEAD_DIM)
    f = lb + (1.0 - lb) * jax.nn.sigmoid(z)
    return jnp.log(f), 1.0 - f

def hybrid_layer_3(x, layer, w_in, b_in, rpb, lb_fwd_logits, lb_bwd_logits, hg_norm_gain,
                 w_out, b_out, ln_gain, ln_bias):
    B, T, _ = x.shape
    h = jnp.einsum('btd,de->bte', x, w_in) + b_in
    split_at = list(np.cumsum(IN_WIDTHS)[:-1])
    q_a, k_a, v_a, g_a, q_h, z_fwd, z_bwd, i_h, g_h = jnp.split(h, split_at, axis=-1)

    heads_a = lambda t: t.reshape(B, T, ATT_HEADS, ATT_HEAD_DIM)
    o_a = neighbourhood_attention(heads_a(q_a), heads_a(k_a), heads_a(v_a), rpb)
    o_a = o_a * jax.nn.silu(g_a)

    heads_h = lambda t: t.reshape(B, T, HG_HEADS, HG_HEAD_DIM).transpose(0, 2, 1, 3).astype(jnp.float32)
    qh, ih = heads_h(q_h), heads_h(i_h)
    logf_f, k_f = hgrn2_forget(heads_h(z_fwd), lb_fwd_logits, layer)
    logf_b, k_b = hgrn2_forget(heads_h(z_bwd), lb_bwd_logits, layer)
    o_fwd = hgrn2_chunk_scan(qh, k_f, ih, logf_f)
    flip = lambda t: jnp.flip(t, axis=2)
    o_bwd = flip(hgrn2_chunk_scan(flip(qh), flip(k_b), flip(ih), flip(logf_b)))
    o_h = (o_fwd + o_bwd).transpose(0, 2, 1, 3)
    o_h = o_h * lax.rsqrt(jnp.mean(jnp.square(o_h), axis=-1, keepdims=True) + RMS_EPS)
    o_h = o_h.reshape(B, T, D_HG) * hg_norm_gain.astype(jnp.float32)
    o_h = o_h.astype(x.dtype) * jax.nn.silu(g_h)

    y = jnp.einsum('bte,ed->btd', jnp.concatenate([o_a, o_h], axis=-1), w_out) + b_out
    r = (DEEPNORM_ALPHA * x + y).astype(jnp.float32)
    mu = jnp.mean(r, axis=-1, keepdims=True)
    var = jnp.mean(jnp.square(r - mu), axis=-1, keepdims=True)
    r = (r - mu) * lax.rsqrt(var + LN_EPS) * ln_gain.astype(jnp.float32) + ln_bias.astype(jnp.float32)
    return r.astype(x.dtype)

def third_inputs(seed: int = 0) -> dict:
    key = jax.random.key(seed)
    ks = jax.random.split(key, 12)
    x = jax.random.normal(ks[0], (BATCH, SEQ, D_MODEL), jnp.float32)
    col_scale = np.ones((D_IN_3,), np.float32)
    off = np.cumsum((0,) + IN_WIDTHS)
    col_scale[off[2]:off[3]] = DEEPNORM_BETA
    col_scale[off[7]:off[8]] = DEEPNORM_BETA
    w_in = jax.random.normal(ks[1], (DEPTH, D_MODEL, D_IN_3), jnp.float32) * (D_MODEL ** -0.5) * jnp.asarray(col_scale)
    b_in = 0.02 * jax.random.normal(ks[2], (DEPTH, D_IN_3), jnp.float32)
    rpb = 0.1 * jax.random.normal(ks[3], (DEPTH, ATT_HEADS, 2 * WIN_ROWS_MAX - 1, 2 * WIN_COLS - 1), jnp.float32)
    lb_fwd_logits = 0.5 * jax.random.normal(ks[4], (DEPTH + 1, D_HG), jnp.float32)
    lb_bwd_logits = 0.5 * jax.random.normal(ks[5], (DEPTH + 1, D_HG), jnp.float32)
    hg_norm_gain = 1.0 + 0.02 * jax.random.normal(ks[6], (DEPTH, D_HG), jnp.float32)
    w_out = jax.random.normal(ks[7], (DEPTH, D_MIX_3, D_MODEL), jnp.float32) * (D_MIX_3 ** -0.5) * DEEPNORM_BETA
    b_out = 0.02 * jax.random.normal(ks[8], (DEPTH, D_MODEL), jnp.float32)
    ln_gain = 1.0 + 0.02 * jax.random.normal(ks[9], (DEPTH, D_MODEL), jnp.float32)
    ln_bias = 0.02 * jax.random.normal(ks[10], (DEPTH, D_MODEL), jnp.float32)
    return {"x": x, "w_in": w_in, "b_in": b_in, "rpb": rpb,
            "lb_fwd_logits": lb_fwd_logits, "lb_bwd_logits": lb_bwd_logits,
            "hg_norm_gain": hg_norm_gain, "w_out": w_out, "b_out": b_out,
            "ln_gain": ln_gain, "ln_bias": ln_bias}

def third_block(x, w_in, b_in, rpb, lb_fwd_logits, lb_bwd_logits, hg_norm_gain,
              w_out, b_out, ln_gain, ln_bias):
    for layer in range(DEPTH):
        x = hybrid_layer_3(x, layer, w_in[layer], b_in[layer], rpb[layer],
                         lb_fwd_logits, lb_bwd_logits, hg_norm_gain[layer],
                         w_out[layer], b_out[layer], ln_gain[layer], ln_bias[layer])
    return x


_first_inputs_3 = third_inputs


def third_inputs(seed=0):
    import zlib

    import numpy as np

    out = dict(_first_inputs_3(seed))
    spreads = {}
    factors = {'b_in': 2.67,
     'rpb': 8.0,
     'hg_norm_gain': 8.0,
     'b_out': 3.635,
     'ln_gain': 2.849,
     'ln_bias': 2.921}
    for name, (base, spread) in spreads.items():
        noise = np.random.default_rng([zlib.crc32(name.encode()), seed]).standard_normal(out[name].shape)
        drawn = base * np.exp(spread * noise) if base else spread * noise
        out[name] = __import__('jax').numpy.asarray(drawn.astype(out[name].dtype))
    for name, factor in factors.items():
        out[name] = (out[name] * factor).astype(out[name].dtype)
    return out


_narrow_inputs_3 = third_inputs


def third_inputs(seed=0):

    out = dict(_narrow_inputs_3(seed))
    wider = {'rpb': 8.38, 'hg_norm_gain': 3.69, 'ln_gain': 3.2, 'ln_bias': 3.2}
    for name, times in wider.items():
        mean = out[name].mean()
        out[name] = (mean + times * (out[name] - mean)).astype(out[name].dtype)
    return out


def setup_inputs(seed=0):
    out = dict(first_inputs(seed))
    for name, value in second_inputs(seed + 1).items():
        if name != "x":
            out[name + "_2"] = value
    for name, value in third_inputs(seed + 2).items():
        if name != "x":
            out[name + "_3"] = value
    return out


def reference(
    x, c, w_ada, b_ada, norm_g, w_in, conv_w, conv_b, conv_ln_g, conv_ln_b, sg_ln_g, sg_ln_b,
    w_s, b_s, w_out, final_g, pre_norm_g_2, w_in_2, conv_w_2, conv_b_2, filt_w1_2, filt_b1_2,
    filt_w2_2, filt_b2_2, filt_w3_2, filt_b3_2, filt_freq_2, filt_w_out_2, hyena_d_2, pool_w_2,
    pool_scale_2, norm_h_g_2, norm_p_g_2, w_out_2, post_norm_g_2, w_in_3, b_in_3, rpb_3,
    lb_fwd_logits_3, lb_bwd_logits_3, hg_norm_gain_3, w_out_3, b_out_3, ln_gain_3, ln_bias_3,
):
    x = first_block(
        x, c, w_ada, b_ada, norm_g, w_in, conv_w, conv_b, conv_ln_g, conv_ln_b, sg_ln_g,
        sg_ln_b, w_s, b_s, w_out, final_g,
    )
    x = second_block(
        x, pre_norm_g_2, w_in_2, conv_w_2, conv_b_2, filt_w1_2, filt_b1_2, filt_w2_2, filt_b2_2,
        filt_w3_2, filt_b3_2, filt_freq_2, filt_w_out_2, hyena_d_2, pool_w_2, pool_scale_2,
        norm_h_g_2, norm_p_g_2, w_out_2, post_norm_g_2,
    )
    return third_block(
        x, w_in_3, b_in_3, rpb_3, lb_fwd_logits_3, lb_bwd_logits_3, hg_norm_gain_3, w_out_3,
        b_out_3, ln_gain_3, ln_bias_3,
    )


_drawn_inputs = setup_inputs


def setup_inputs(seed=0):
    import zlib

    import numpy as np

    out = dict(_drawn_inputs(seed))
    spreads = {}
    factors = {'b_out_3': 8.0}
    for name, (base, spread) in spreads.items():
        noise = np.random.default_rng([zlib.crc32(name.encode()), seed]).standard_normal(out[name].shape)
        drawn = base * np.exp(spread * noise) if base else spread * noise
        out[name] = __import__('jax').numpy.asarray(drawn.astype(out[name].dtype))
    for name, factor in factors.items():
        out[name] = (out[name] * factor).astype(out[name].dtype)
    return out
```

```python
import math
from contextlib import ExitStack

import numpy as np

import concourse.bass as bass
from concourse import mybir

F32 = mybir.dt.float32
ACT = mybir.ActivationFunctionType
ALU = mybir.AluOpType
AXX = mybir.AxisListType.X

S_LEN = 2048
D = 1024
NT = 16
EPS = 1e-6


class Engine:

    def __init__(self, sem):
        self.sem, self.n, self.queue, self.seen = sem, 0, [], {}

    def wait(self, *after):
        for t in after:
            if t is None:
                continue
            if isinstance(t, list):
                self.wait(*t)
                continue
            sem, v = t
            if self.seen.get(sem.name, 0) < v:
                self.seen[sem.name] = v
                self.queue.append((0, sem, v))

    def do(self, f, *after, sig=True):
        self.wait(*after)
        if sig:
            self.n += 1
            self.queue.append((1, f, self.sem))
            return (self.sem, self.n)
        self.queue.append((1, f, None))
        return None

    def last(self):
        return (self.sem, self.n)

    def emit(self, eng):
        for kind, a, b in self.queue:
            if kind == 0:
                eng.wait_ge(a, b)
            elif kind == 1:
                i = a(eng)
                if b is not None:
                    i.then_inc(b, 1)
            else:
                a(eng).then_inc(b, 16)


class DmaSem:

    def __init__(self, sem):
        self.sem, self.n = sem, 0

    def last(self):
        return (self.sem, 16 * self.n)


class Ring:

    def __init__(self, n):
        self.n, self.at, self.free = n, 0, [None] * n

    def take(self):
        i = self.at % self.n
        self.at += 1
        f = self.free[i]
        return i, f

    def align(self, m):
        while self.at % m:
            self.at += 1

    def give(self, i, *tokens):
        self.free[i] = list(tokens)


class Ctx:
    pass


def setup(nc, ctx):
    c = Ctx()
    c.nc = nc
    c.nsem = 0

    def sem(name):
        return ctx.enter_context(nc.semaphore(name))

    def dsem():
        c.nsem += 1
        d = DmaSem(sem(f"d{c.nsem}"))
        c.dsems.append(d)
        return d

    c.dsems = []
    c.dsem = dsem
    c.pe, c.act, c.dve, c.pool, c.sp = (Engine(sem(n)) for n in ("s_pe", "s_act", "s_dve", "s_pool", "s_sp"))
    c.NF = 52688
    c.S = ctx.enter_context(nc.sbuf_tensor("arena", [128, c.NF], F32))
    c.pair = ctx.enter_context(nc.sbuf_tensor("pair", [128, 2, 128], mybir.dt.int32))
    c.zb = ctx.enter_context(nc.sbuf_tensor("zeros", [128, 512], mybir.dt.bfloat16))
    c.P = [ctx.enter_context(nc.psum_tensor(f"ps{i}", [128, 512], F32)) for i in range(8)]
    c.banks = Ring(8)

    def dma(eng, out, in_, ds, *after, slow=False):
        prev = ds.last() if ds.n else None
        eng.wait(*after)
        eng.wait(prev)
        ds.n += 1
        eng.queue.append((2, lambda e: e.dma_start(out, in_, allow_slow_non_contiguous=slow), ds.sem))
        return ds.last()

    def mm(out, lhsT, rhs, start, stop, *after, sig=False):
        return c.pe.do(lambda e: e.matmul(out, lhsT, rhs, start=start, stop=stop), *after, sig=sig)

    def tr(out, in_, ident, *after, sig=False):
        return c.pe.do(lambda e: e.transpose(out, in_, ident), *after, sig=sig)

    def act(out, in_, func, *after, scale=None, bias=None, accum=None):
        kw = {}
        if scale is not None:
            kw["scale"] = scale
        if bias is not None:
            kw["bias"] = bias
        if accum is not None:
            kw["accum_out"] = accum
        return c.act.do(lambda e: e.activation(out, in_, func, **kw), *after)

    def tt(eng, out, a, b, op, *after):
        return eng.do(lambda e: e.tensor_tensor(out, a, b, op), *after)

    def ts(eng, out, a, s1, s2, op0, op1, *after):
        if op1 is None:
            return eng.do(lambda e: e.tensor_scalar(out, a, s1, None, op0), *after)
        return eng.do(lambda e: e.tensor_scalar(out, a, s1, s2, op0, op1), *after)

    def stt(out, a, s, b, op0, op1, *after):
        return c.dve.do(lambda e: e.scalar_tensor_tensor(out, a, s, b, op0, op1), *after)

    def cp(eng, out, a, *after):
        return eng.do(lambda e: e.tensor_copy(out, a), *after)

    def ms(eng, out, v, *after):
        return eng.do(lambda e: e.memset(out, v), *after)

    def recip(out, a, *after):
        return c.dve.do(lambda e: e.reciprocal(out, a), *after)

    c.dma, c.mm, c.tr, c.act_, c.tt, c.ts, c.stt, c.cp, c.ms, c.recip = dma, mm, tr, act, tt, ts, stt, cp, ms, recip

    def view(off, *dims):
        n = 1
        for d in dims:
            n *= d
        assert off + n <= c.NF, (off, dims)
        v = c.S[:, off:off + n]
        if len(dims) == 2:
            return v.rearrange("p (a b) -> p a b", b=dims[1])
        if len(dims) == 3:
            return v.rearrange("p (a b c) -> p a b c", b=dims[1], c=dims[2])
        return v

    c.view = view

    def fence():
        toks = [e.last() for e in (c.pe, c.act, c.dve, c.pool, c.sp) if e.n] + [d.last() for d in c.dsems if d.n]
        for e in (c.pe, c.act, c.dve, c.pool, c.sp):
            e.wait(*toks)

    c.fence = fence
    return c


def rsqrt(c, out, in_, scale, *after):
    t = c.act_(out, in_, ACT.Ln, *after, scale=scale, bias=c.eps[:in_.shape[0], :])
    return c.act_(out, out, ACT.Exp, t, scale=-0.5)


class WRing:

    def __init__(self, c, off, n):
        self.c, self.ring, self.n = c, Ring(n), n
        self.sems = [c.wsems[i] for i in range(n)]
        self.W = c.view(off, n, 1024)

    def load(self, dram, col):
        i, free = self.ring.take()
        kt = dram.shape[0] // 128
        dst = self.W[:, i, 0:kt * 128].rearrange("p (k n) -> p k n", k=kt)
        src = dram[:, col:col + 128].rearrange("(k p) n -> p k n", p=128)
        t = self.c.dma(self.c.sp, dst, src, self.sems[i], free)
        return i, t


def proj_cm(c, wr, slot, wtok, HT, tb, htok):
    b, free = c.banks.take()
    for k in range(8):
        t = c.mm(c.P[b][:, :], wr.W[:, slot, k * 128:(k + 1) * 128], HT[:, k, tb * 512:(tb + 1) * 512],
                 k == 0, k == 7, free, wtok, htok, sig=(k == 7))
    return b, t


def transposed_in(c, HT, XH, xtoks, g, scale, bias, *after):
    out = []
    rel = []
    for k in range(8):
        b, free = c.banks.take()
        for j in range(4):
            t = c.tr(c.P[b][:, j * 128:(j + 1) * 128], XH[:, j, k * 128:(k + 1) * 128], c.ident, free, xtoks,
                     sig=(j == 3))
        dst = HT[:, k, g * 512:(g + 1) * 512]
        kw = dict(scale=1.0 if scale is None else scale[:, k:k + 1])
        if k % 2 == 0:
            kw2 = {} if bias is None else dict(bias=bias[:, k:k + 1])
            e = c.act_(dst, c.P[b][:, :], ACT.Identity, t, *after, **kw, **kw2)
        elif scale is None:
            e = c.cp(c.dve, dst, c.P[b][:, :], t, *after)
        elif bias is None:
            e = c.ts(c.dve, dst, c.P[b][:, :], scale[:, k:k + 1], None, ALU.mult, None, t, *after)
        else:
            e = c.ts(c.dve, dst, c.P[b][:, :], scale[:, k:k + 1], bias[:, k:k + 1], ALU.mult, ALU.add, t, *after)
        c.banks.give(b, e)
        out.append(e)
        rel.append(t)
    return out, rel


def transposed_tile(c, HT, xh, i, scale, tok, *after):
    ev = []
    for h in range(2):
        b, free = c.banks.take()
        for j in range(4):
            k = 4 * h + j
            t = c.tr(c.P[b][:, j * 128:(j + 1) * 128], xh[:, k * 128:(k + 1) * 128], c.ident, free, tok, sig=(j == 3))
        dst = HT[:, 4 * h:4 * h + 4, i * 128:(i + 1) * 128]
        src = c.P[b][:, :].rearrange("p (a b) -> p a b", b=128)
        if scale is None:
            e = c.act_(dst, src, ACT.Copy, t, *after)
        else:
            s = scale[:, 4 * h:4 * h + 4].unsqueeze(2).to_broadcast([128, 4, 128])
            e = c.tt(c.dve, dst, src, s, ALU.mult, t, *after)
        c.banks.give(b, e)
        ev.append(e)
    return ev, t


def out_stage(c, KT, lhs, ltoks, WO, wtok, epilogue, lrel, HT, scale, xh):
    pending = None
    ring = Ring(2)
    for i in range(NT):
        bb = []
        for h in range(2):
            b, free = c.banks.take()
            for k in range(KT):
                t = c.mm(c.P[b][:, :], lhs(i, k), WO[:, k, h * 512:(h + 1) * 512], k == 0, k == KT - 1,
                         free, ltoks(i), wtok, sig=(k == KT - 1))
            bb.append(b)
        lrel(i, t)
        r, rf = ring.take()
        e = epilogue(i, bb, t, rf)
        if HT is None:
            continue
        if pending is not None:
            pi, pe_, pt, pr = pending
            ev, tl = transposed_tile(c, HT, xh(pi), pi, scale, pe_, pt)
            ring.give(pr, tl)
        pending = (i, e, t, r)
    if HT is not None:
        pi, pe_, pt, pr = pending
        transposed_tile(c, HT, xh(pi), pi, scale, pe_, pt)


PROWS1 = [("c", 8), ("norm_g", 8), ("conv_b", 8), ("conv_ln_g", 8), ("conv_ln_b", 8), ("pre_norm_g_2", 8),
          ("conv_b_2", 12), ("pool_scale_2", 4), ("norm_h_g_2", 4), ("norm_p_g_2", 4), ("conv_w_2", 36)]
PROWS2 = [("b_in_3", 36), ("hg_norm_gain_3", 4), ("lb_fwd_logits_3", 8), ("lb_bwd_logits_3", 8)]


def parameters(c, A, off):
    raw = c.view(off, 4, 128)
    c.pcol = c.view(c.take(512), 4, 128)
    c.cols = {}
    toks = [c.ms(c.dve, raw[:, :, :], 0.0)]
    tk = []

    def rows(tile, at, ap):
        n = ap.shape[0]
        tk.append(c.dma(c.act, raw[at:at + n, tile, :], ap, c.dsem(), *toks))

    at = 0
    for name, n in PROWS1:
        a = A[name]
        while len(a.shape) > 1:
            letters = " ".join("abcd"[:len(a.shape)])
            a = a.rearrange(f"{letters} -> ({letters})")
        rows(0, at, a.rearrange("(r p) -> r p", p=128))
        c.cols[name] = (0, at, n)
        at += n
    at = 0
    for name, n in PROWS2:
        a = A[name]
        while len(a.shape) > 1:
            letters = " ".join("abcd"[:len(a.shape)])
            a = a.rearrange(f"{letters} -> ({letters})")
        rows(1, at, a.rearrange("(r p) -> r p", p=128))
        c.cols[name] = (1, at, n)
        at += n
    cw = A["conv_w"].rearrange("l w o (t p) -> (l w o t) p", p=128)
    rows(2, 0, cw[0:124, :])
    rows(3, 0, cw[124:248, :])
    b, free = c.banks.take()
    for t in range(4):
        last = c.tr(c.P[b][:, t * 128:(t + 1) * 128], raw[:, t, :], c.ident, free, tk, c.t_const, sig=(t == 3))
    done = c.cp(c.dve, c.pcol[:, :, :].rearrange("p a b -> p (a b)"), c.P[b][:, :], last)
    c.banks.give(b, done)
    c.t_par = done

    def col(name):
        t, a, n = c.cols[name]
        return c.pcol[:, t, a:a + n]

    def convw(j, ch):
        r = j * 8 + ch
        return c.pcol[:, 2 + r // 124, r % 124:r % 124 + 1]

    c.col, c.convw = col, convw


def rows_of(A, name):
    a = A[name]
    if len(a.shape) == 2:
        return a[0, :]
    return a


def bcast_row(c, dst, row, *after):
    return c.dma(c.act, dst, row.partition_broadcast(128), c.dsem(), *after)


def block1(c, A, X1, Y, GD, dbg):
    R0, R1, R2 = c.R0, c.R1, c.R2
    w_in = A["w_in"][0]
    HT = c.view(R0, 8, 2048)
    XT = c.view(R1, 16, 1024)
    x = A["x"][0]
    small = c.take(16 * 6 + 64)
    ss = c.view(small, 16)
    rstd = c.view(small + 16, 16)
    st = c.view(small + 32, 128)
    XQ = R2
    xt = []
    for i in range(16):
        xt.append(c.dma(c.sp, XT[:, i, :], x[i * 128:(i + 1) * 128, :], c.dsem()))
    parameters(c, A, R2 + 15368)
    w_ada = A["w_ada"][0]
    wa = c.view(R2, 2, 8, 512)
    mod = c.view(R2 + 8192, 3072)
    cs = c.view(R2 + 11264, 8)
    one = c.ms(c.pool, st[:, 0:16], 0.0)
    tcs = c.act_(cs[:, :], c.col("c"), ACT.Silu, c.t_par)
    crep = c.view(R2 + 11272, 8, 128)
    for k in range(8):
        trep = c.cp(c.dve, crep[:, k, :], cs[:, k:k + 1].to_broadcast([128, 128]), tcs)
    b_ada = c.view(R2 + 12296, 3072)
    tb = bcast_row(c, b_ada[:, :], rows_of(A, "b_ada"))
    wr = Ring(2)
    wsem = [c.dsem() for _ in range(2)]
    tm = []
    for n in range(6):
        s, free = wr.take()
        tw = c.dma(c.sp, wa[:, s, :, :], w_ada[:, n * 512:(n + 1) * 512].rearrange("(k p) n -> p k n", p=128),
                   wsem[s], free)
        b, bf = c.banks.take()
        for k in range(8):
            t = c.mm(c.P[b][:, :], crep[:, k, :], wa[:, s, k, :], k == 0, k == 7, bf, tw, trep, sig=(k == 7))
        wr.give(s, t)
        e = c.tt(c.dve, mod[:, n * 512:(n + 1) * 512], c.P[b][:, :], b_ada[:, n * 512:(n + 1) * 512], ALU.add, t, tb)
        c.banks.give(b, e)
        tm.append(e)
    gate = c.gate
    tg = c.cp(c.pool, gate, mod[:, 2048:3072], tm)
    b, bf = c.banks.take()
    for k in range(16):
        t = c.mm(c.P[b][:, k:k + 1], mod[0:1, k * 128:(k + 1) * 128], c.ones[0:1, 0:1], True, True, bf, tm,
                 sig=(k == 15))
    ms = c.view(c.take(16), 16)
    t0 = c.cp(c.dve, ms[:, 0:8], c.P[b][:, 0:8], t)
    t1 = c.stt(ms[:, 8:16], c.P[b][:, 8:16], 1.0, c.col("norm_g"), ALU.add, ALU.mult, t, c.t_par)
    c.banks.give(b, t1)
    junk = c.view(R2 + 15880, 1024)
    tj = None
    ta = []
    for i in range(16):
        tj = c.act_(junk[:, :], XT[:, i, :], ACT.Square, xt[i], tj, accum=ss[:, i:i + 1])
    tr_ = rsqrt(c, rstd[:, :], ss[:, :], 1.0 / D, tj)
    ht = []
    for g in range(4):
        tx = []
        for j in range(4):
            i = 4 * g + j
            tx.append(c.ts(c.dve, XT[:, i, :], XT[:, i, :], rstd[:, i:i + 1], None, ALU.mult, None, tr_))
        o, r = transposed_in(c, HT, XT[:, 4 * g:4 * g + 4, :], tx, g, ms[:, 8:16], ms[:, 0:8], t0, t1)
        ht.append(o)
    c.fence()
    if dbg == "h":
        return HT

    wr = WRing(c, R2, 8)
    V = c.view(R1, 16, 1024)
    base = R2 + 8192
    tv = []
    vt = [[] for _ in range(16)]
    for h in range(2):
        wr.ring.align(4)
        sl = [wr.load(w_in, 4096 + h * 512 + q * 128) for q in range(4)]
        s0 = sl[0][0]
        wt = [t for _, t in sl]
        for i in range(16):
            b, bf = c.banks.take()
            for k in range(8):
                t = c.mm(c.P[b][:, :], HT[:, k, i * 128:(i + 1) * 128], wr.W[:, s0:s0 + 4, k * 128:(k + 1) * 128],
                         k == 0, k == 7, bf, wt, sig=(k == 7))
            e = c.act_(V[:, i, h * 512:(h + 1) * 512], c.P[b][:, :], ACT.Copy, t)
            c.banks.give(b, e)
            vt[i].append(e)
        for s, _ in sl:
            wr.ring.give(s, t)
    lg, lb = c.view(base, 1024), c.view(base + 1024, 1024)
    tlg = bcast_row(c, lg[:, :], rows_of(A, "sg_ln_g"))
    tlb = bcast_row(c, lb[:, :], rows_of(A, "sg_ln_b"))
    bs = c.view(base + 2048, 8, 128)
    tbs = c.dma(c.act, bs[:, :, :], A["b_s"][0].partition_broadcast(128), c.dsem())
    wsr = c.view(base + 3072, 8, 128)
    wsT = c.view(base + 4096, 8, 128)
    tws = c.dma(c.act, wsr[:, :, :], A["w_s"][0].rearrange("h p q -> p h q"), c.dsem())
    twt = []
    for g in range(2):
        b, bf = c.banks.take()
        for j in range(4):
            t = c.tr(c.P[b][:, j * 128:(j + 1) * 128], wsr[:, 4 * g + j, :], c.ident, bf, tws, sig=(j == 3))
        e = c.act_(wsT[:, 4 * g:4 * g + 4, :].rearrange("p a b -> p (a b)"), c.P[b][:, :], ACT.Copy, t)
        c.banks.give(b, e)
        twt.append(e)
    bst = c.view(base + 5120, 16, 12)
    mv = c.view(base + 5312, 16, 2)
    rs = c.view(base + 5344, 16)
    for i in range(16):
        for h in range(2):
            o = bst[:, i, h * 6:h * 6 + 6]
            a = V[:, i, h * 512:(h + 1) * 512]
            tb_ = c.dve.do(lambda e, o=o, a=a: e.bn_stats(o, a), vt[i])
        o, a = mv[:, i, :], bst[:, i, :]
        tmv = c.dve.do(lambda e, o=o, a=a: e.bn_aggr(o, a), tb_)
        if i % 4 == 3:
            trs = rsqrt(c, rs[:, i - 3:i + 1], mv[:, i - 3:i + 1, 1:2].rearrange("p a b -> p (a b)"), 1.0, tmv)
            for j in range(i - 3, i + 1):
                t1 = c.ts(c.dve, V[:, j, :], V[:, j, :], mv[:, j, 0:1], rs[:, j:j + 1], ALU.subtract, ALU.mult, trs)
                t2 = c.tt(c.dve, V[:, j, :], V[:, j, :], lg[:, :], ALU.mult, t1, tlg)
                tv.append(c.tt(c.pool, V[:, j, :], V[:, j, :], lb[:, :], ALU.add, t2, tlb))
    tmp = c.view(base + 5400, 6, 512)
    ring = Ring(6)
    ysem = [c.dsem() for _ in range(6)]
    ytok = []
    for h in range(8):
        su, tu = wr.load(w_in, 3072 + h * 128)
        sg, tg_ = wr.load(w_in, 5120 + h * 128)
        for tb in range(4):
            b1, bf = c.banks.take()
            for j in range(4):
                n = 4 * tb + j
                t = c.mm(c.P[b1][:, j * 128:(j + 1) * 128], V[:, n, h * 128:(h + 1) * 128], wsT[:, h, :], True, True,
                         bf, tv[n], twt, sig=(j == 3))
            r, rf = ring.take()
            r2, rf2 = ring.take()
            e1 = c.tt(c.dve, tmp[:, r, :].rearrange("p (a b) -> p a b", b=128),
                      c.P[b1][:, :].rearrange("p (a b) -> p a b", b=128),
                      bs[:, h:h + 1, :].to_broadcast([128, 4, 128]), ALU.add, t, rf, tbs)
            c.banks.give(b1, e1)
            b2, t = proj_cm(c, wr, sg, tg_, HT, tb, None)
            e2 = c.act_(tmp[:, r2, :], c.P[b2][:, :], ACT.Silu, t, rf2)
            c.banks.give(b2, e2)
            b3, t = proj_cm(c, wr, su, tu, HT, tb, None)
            e3 = c.tt(c.dve, tmp[:, r, :], tmp[:, r, :], c.P[b3][:, :], ALU.mult, t, e1)
            c.banks.give(b3, e3)
            e4 = c.tt(c.dve, tmp[:, r, :], tmp[:, r, :], tmp[:, r2, :], ALU.mult, e3, e2)
            d = c.dma(c.act, Y[8 + h][:, tb * 512:(tb + 1) * 512], tmp[:, r, :], ysem[r], e4)
            ytok.append(d)
            ring.give(r, d)
            ring.give(r2, e4)
        wr.ring.give(su, t)
        wr.ring.give(sg, t)
    c.fence()

    CV = c.view(R1, 8, 2048)
    wr = WRing(c, R2, 5)
    o = R2 + 5120
    AP = [c.view(o, 2080), c.view(o + 2080, 2080)]
    o += 4160
    SUM, SQ = c.view(o, 2048), c.view(o + 2048, 2048)
    o += 4096
    sqt = c.view(o, 2, 512)
    o += 1024
    sgt = c.view(o, 3, 512)
    o += 1536
    gst = c.view(o, 2, 512)
    o += 1024
    sring, gring, qring = Ring(3), Ring(2), Ring(2)
    gsem = [c.dsem() for _ in range(2)]
    pads = [c.ms(c.pool, AP[q][:, a:b], 0.0) for q in range(2) for a, b in ((0, 15), (2063, 2080))]
    aptok = [None, None]
    gtok = {}
    cvt = []
    tsum = tsq = None
    cb = c.col("conv_b")

    def gates(ch):
        s, tw = wr.load(w_in, 2048 + ch * 128)
        for tb in range(4):
            b, t = proj_cm(c, wr, s, tw, HT, tb, None)
            r, rf = gring.take()
            e = c.act_(gst[:, r, :], c.P[b][:, :], ACT.Silu, t, rf)
            c.banks.give(b, e)
            d = c.dma(c.act, GD[ch][:, tb * 512:(tb + 1) * 512], gst[:, r, :], gsem[r], e)
            gtok[(ch, tb)] = d
            gring.give(r, d)
        wr.ring.give(s, t)

    for ch in range(8):
        sg, tg_ = wr.load(w_in, 1024 + ch * 128)
        sa, ta_ = wr.load(w_in, ch * 128)
        a = AP[ch % 2]
        parts = []
        for tb in range(4):
            b, t = proj_cm(c, wr, sg, tg_, HT, tb, None)
            r, rf = sring.take()
            e = c.act_(sgt[:, r, :], c.P[b][:, :], ACT.Sigmoid, t, rf)
            c.banks.give(b, e)
            b, t = proj_cm(c, wr, sa, ta_, HT, tb, None)
            e = c.tt(c.dve, a[:, 15 + tb * 512:15 + (tb + 1) * 512], c.P[b][:, :], sgt[:, r, :], ALU.mult,
                     t, e, aptok[ch % 2], pads)
            c.banks.give(b, e)
            sring.give(r, e)
            parts.append(e)
        wr.ring.give(sg, t)
        wr.ring.give(sa, t)
        tc_ = c.ts(c.dve, CV[:, ch, :], a[:, 0:2048], c.convw(0, ch), cb[:, ch:ch + 1], ALU.mult, ALU.add, parts)
        for j in range(1, 31):
            tc_ = c.stt(CV[:, ch, :], a[:, j:j + 2048], c.convw(j, ch), CV[:, ch, :], ALU.mult, ALU.add, tc_)
        aptok[ch % 2] = tc_
        cvt.append(tc_)
        for tb in range(4):
            sl = slice(tb * 512, (tb + 1) * 512)
            r, rf = qring.take()
            tq = c.act_(sqt[:, r, :], CV[:, ch, sl], ACT.Square, tc_, rf)
            if ch == 0:
                c.cp(c.pool, SUM[:, sl], CV[:, ch, sl], tc_)
                e = c.cp(c.pool, SQ[:, sl], sqt[:, r, :], tq)
            else:
                c.tt(c.pool, SUM[:, sl], SUM[:, sl], CV[:, ch, sl], ALU.add, tc_, tsum)
                e = c.tt(c.pool, SQ[:, sl], SQ[:, sl], sqt[:, r, :], ALU.add, tq, tsum)
            qring.give(r, e)
        tsum = tsq = c.pool.last()
        if ch >= 1:
            gates(ch - 1)
    gates(7)
    pe_done = c.pe.last()
    WO = c.view(R0, 16, 1024)
    tpe = pe_done
    two = []
    for k in range(16):
        two.append(c.dma(c.sp, WO[:, k, :], A["w_out"][0][k * 128:(k + 1) * 128, :], c.dsem(), tpe))
    mu, rsd = c.view(R2, 2, 512), c.view(R2 + 1024, 2, 512)
    gld, tp = c.view(R2 + 2048, 3, 512), c.view(R2 + 3584, 3, 512)
    lring, tring = Ring(3), Ring(3)
    lsem = [c.dsem() for _ in range(3)]
    glg, glb = c.col("conv_ln_g"), c.col("conv_ln_b")
    first = [c.pe.last(), c.dve.last(), c.pool.last(), c.act.last()]
    fg = c.view(R2 + 8192, 1024)
    tfg = bcast_row(c, fg[:, :], A["final_g"], first)
    yat = []
    for tb in range(4):
        sl = slice(tb * 512, (tb + 1) * 512)
        q = tb % 2
        if tb >= 2:
            wm = yat[tb - 2]
        else:
            wm = first
        bm, f1 = c.banks.take()
        t1 = c.mm(c.P[bm][:, :], c.ones, SUM[:, sl], True, True, f1, tsum, sig=True)
        bq, f2 = c.banks.take()
        t2 = c.mm(c.P[bq][:, :], c.ones, SQ[:, sl], True, True, f2, tsq, sig=True)
        e1 = c.ts(c.dve, mu[:, q, :], c.P[bm][:, :], 1.0 / D, None, ALU.mult, None, t1, wm)
        c.banks.give(bm, e1)
        e2 = c.act_(rsd[:, q, :], mu[:, q, :], ACT.Square, e1)
        e3 = c.stt(rsd[:, q, :], c.P[bq][:, :], 1.0 / D, rsd[:, q, :], ALU.mult, ALU.subtract, e2, t2)
        c.banks.give(bq, e3)
        e4 = c.ts(c.dve, rsd[:, q, :], rsd[:, q, :], 0.0, None, ALU.max, None, e3)
        e5 = rsqrt(c, rsd[:, q, :], rsd[:, q, :], 1.0, e4)
        last = []
        for ch in range(8):
            v = CV[:, ch, sl]
            r, rf = lring.take()
            tl = c.dma(c.sp, gld[:, r, :], GD[ch][:, sl], lsem[r], rf, gtok[(ch, tb)], first)
            eng = c.pool if ch % 2 else c.dve
            a1 = c.tt(eng, v, v, mu[:, q, :], ALU.subtract, e1, cvt[ch])
            a2 = c.tt(eng, v, v, rsd[:, q, :], ALU.mult, a1, e5)
            r2, rf2 = tring.take()
            a3 = c.act_(tp[:, r2, :], v, ACT.Silu, a2, rf2, scale=glg[:, ch:ch + 1], bias=glb[:, ch:ch + 1])
            a4 = c.tt(eng, v, tp[:, r2, :], gld[:, r, :], ALU.mult, a3, tl)
            lring.give(r, a4)
            tring.give(r2, a4)
            last.append(a4)
        yat.append(last)
    yb = c.view(R2 + 5120, 2, 8, 128)
    T = c.view(R2 + 7168, 1024)
    X = c.view(R2 + 13376, 2, 1024)
    XH = c.view(R2 + 15424, 2, 1024)
    st = c.view(c.take(64), 64)
    xring, xsem = Ring(2), [c.dsem() for _ in range(2)]
    bring, bsem = Ring(2), [c.dsem() for _ in range(2)]
    x1sem = [c.dsem() for _ in range(2)]
    lt, x1tok, tfree = {}, {}, [None]

    def ltoks(i):
        if i not in lt:
            r, rf = bring.take()
            t = c.dma(c.sp, yb[:, r, :, :], Y[8:16, :, i * 128:(i + 1) * 128].rearrange("k p t -> p k t"), bsem[r],
                      rf, ytok, first)
            lt[i] = (r, t)
        return [lt[i][1], yat[i // 4], two]

    def lhs(i, k):
        if k < 8:
            return CV[:, k, i * 128:(i + 1) * 128]
        return yb[:, i % 2, k - 8, :]

    def epilogue(i, bb, t, rf):
        r, xf = xring.take()
        X_ = X[:, r, :]
        tx = c.dma(c.sp, X_, A["x"][0, i * 128:(i + 1) * 128, :], xsem[r], xf, first)
        for h in range(2):
            e = c.tt(c.dve, T[:, h * 512:(h + 1) * 512], c.P[bb[h]][:, :], c.gate[:, h * 512:(h + 1) * 512],
                     ALU.mult, t, tfree[0], first)
            c.banks.give(bb[h], e)
        e = c.tt(c.pool, X_, X_, T[:, :], ALU.add, e, tx)
        tfree[0] = e
        xh = XH[:, r, :]
        s = st[:, 4 * r:4 * r + 1]
        e1 = c.act_(xh, X_, ACT.Square, e, rf, accum=s)
        e1 = rsqrt(c, s, s, 1.0 / D, e1)
        e = c.stt(X_, X_, s, fg[:, :], ALU.mult, ALU.mult, e1, tfg)
        x1tok[i] = c.dma(c.act, X1[i * 128:(i + 1) * 128, :], X_, x1sem[r], e)
        s2 = st[:, 4 * r + 1:4 * r + 2]
        e1 = c.act_(xh, X_, ACT.Square, e, accum=s2)
        e1 = rsqrt(c, s2, s2, 1.0 / D, e1)
        e = c.ts(c.dve, xh, X_, s2, None, ALU.mult, None, e1)
        xring.give(r, e, x1tok[i])
        return e

    out_stage(c, 16, lhs, ltoks, WO, None, epilogue, lambda i, t: bring.give(lt[i][0], t), CV,
              c.col("pre_norm_g_2"), lambda i: XH[:, i % 2, :])
    c.x1tok = [x1tok[i] for i in range(16)]
    c.fence()
    return CV


TWO_PI = 2 * math.pi
MAGIC = 12582912.0


def transform_constants():
    k = {}
    n1 = np.arange(128)[:, None]
    wk = np.zeros((128, 128))
    wai = np.zeros((128, 64))
    m1 = np.arange(64)
    for j in range(64):
        a = TWO_PI * ((n1[:, 0] * j) % 128) / 128
        b = TWO_PI * ((m1 * j) % 128) / 128
        if j == 0:
            wk[:, 0] = 1.0
            wk[:, 1] = np.where(n1[:, 0] % 2 == 0, 1.0, -1.0)
            wai[0] = 1.0 / 4096
            wai[1] = np.where(m1 % 2 == 0, 1.0, -1.0) / 4096
        else:
            wk[:, 2 * j] = np.cos(a)
            wk[:, 2 * j + 1] = -np.sin(a)
            wai[2 * j] = 2 * np.cos(b) / 4096
            wai[2 * j + 1] = -2 * np.sin(b) / 4096
    k["k_wk"] = wk
    wa = np.zeros((128, 2, 128))
    wb = np.zeros((128, 2, 128))
    for e in range(2):
        wa[e::2, e, :] = wk[:64]
        wb[:, e, e::2] = wai
    k["k_wa"] = wa.reshape(128, 256)
    k["k_wai"] = wb.reshape(128, 256)
    wx = np.zeros((128, 32, 3, 2, 32))
    wi = np.zeros((2, 2, 32, 32, 2, 2, 32))
    n2 = np.arange(32)[:, None]
    k2 = np.arange(32)[None, :]
    for b in range(32):
        for q in range(2):
            j = 2 * b + q
            re, im = slice(64 * q, 64 * q + 32), slice(64 * q + 32, 64 * q + 64)
            if j:
                th = TWO_PI * ((n2 * (j + 128 * k2)) % 4096) / 4096
                cs, sn = np.cos(th), np.sin(th)
                wx[re, b, 0, q], wx[im, b, 0, q] = cs, sn
                wx[re, b, 1, q], wx[im, b, 1, q] = -sn, cs
                wi[0, q, :, b, q, 0, :], wi[1, q, :, b, q, 0, :] = cs.T, -sn.T
                wi[0, q, :, b, q, 1, :], wi[1, q, :, b, q, 1, :] = sn.T, cs.T
                continue
            n = np.arange(32)
            alt = np.where(n % 2 == 0, 1.0, -1.0)
            wx[re, 0, 0, 0, 0] = 1.0
            wx[re, 0, 1, 0, 0] = alt
            wi[0, 0, 0, 0, 0, 0, :] = 1.0
            wi[1, 0, 0, 0, 0, 0, :] = alt
            for v in range(1, 32):
                f = 128 * v if v < 16 else 64 + 128 * (v - 16)
                row, cc = (re, 0) if v < 16 else (im, 1)
                th = TWO_PI * ((n * f) % 4096) / 4096
                wx[row, 0, 0, 0, v] = np.cos(th)
                wx[row, 0, 1, 0, v] = -np.sin(th)
                wi[0, 0, v, 0, 0, cc, :] = 2 * np.cos(th)
                wi[1, 0, v, 0, 0, cc, :] = -2 * np.sin(th)
    wx[:, :, 2] = wx[:, :, 0]
    k["k_wx"] = wx.reshape(128, 6144)
    k["k_wi"] = wi.reshape(128, 4096)
    sg = np.ones((128, 1))
    sg[0:64] = -1.0
    k["k_sg"] = sg
    L = S_LEN
    f32 = np.float32
    t = np.linspace(0.0, 1.0, L, dtype=f32)[:, None]
    ang = f32(2.0 * math.pi) * np.arange(L, dtype=f32)[:, None] / f32(L)
    bands = np.linspace(1e-4, 15, 16, dtype=f32)[None, :]
    z = np.concatenate([t, np.cos(bands * ang), -np.sin(bands * ang)], axis=-1).astype(f32)
    i = np.arange(64)
    tf = np.stack([32 * i + n for n in range(32)])
    tb = np.stack([2048 - n - 32 * i for n in range(32)])
    k["k_z"] = np.concatenate([z[tf.reshape(-1)].T, z[np.minimum(tb, L - 1).reshape(-1)].T], 0)
    max_decay = math.log(1e-2) / 0.3
    min_decay = math.log(1e-2) / 1.5
    deltas = np.linspace(min_decay, max_decay, 512, dtype=f32)
    dec = np.exp(-t * np.abs(deltas)[None, :]).astype(f32)
    dec = np.concatenate([dec, np.zeros((1, 512), f32)], 0)
    k["k_dec"] = np.concatenate([dec[tf.T], dec[tb.T]], 0)
    ec = np.ones((4, 16))
    for g, w in enumerate((2, 4, 8, 16)):
        for q in range(8):
            if q < w // 2:
                ec[g, q] = w / (q + w // 2)
            tt_ = L - 8 + q
            cnt = min(tt_ + w // 2 - 1, L - 1) - (tt_ - w // 2) + 1
            ec[g, 8 + q] = w / cnt
    k["k_ec"] = ec
    return {n: np.ascontiguousarray(v, dtype=np.float32) for n, v in k.items()}


def block2(c, A, HT, X1, X2, Y, GD, dbg, dump):
    R0, R1, R2 = c.R0, c.R1, c.R2
    w_in = A["w_in_2"][0]
    wr = WRing(c, R2, 8)
    U = [c.view(R0, 2064), c.view(R0 + 2064, 2064)]
    Sa, Sb = c.view(R0 + 4128, 2064), c.view(R0 + 6192, 2064)
    zst = c.view(R0 + 8256, 4, 512)
    yst = c.view(R0 + 10304, 4, 512)
    pw = c.view(R0 + 12352, 4, 128)
    ec = c.view(R0 + 12864, 4, 16)
    tpw = c.dma(c.act, pw[:, :, :], A["pool_w_2"][0].rearrange("g c d -> c g d"), c.dsem())
    tec = c.dma(c.act, ec[:, :, :], A["k_ec"].partition_broadcast(128), c.dsem())
    pads = [c.ms(c.pool, u[:, a:b], 0.0) for u in U for a, b in ((0, 8), (2056, 2064))]
    zring, yring = Ring(4), Ring(4)
    ysem = [c.dsem() for _ in range(4)]
    zsem = [c.dsem() for _ in range(4)]
    ufree = [None, None]
    ytok, ztok = {}, {}
    ps = c.col("pool_scale_2")
    pend = None

    def pool_out(g, tp_):
        s, tw = wr.load(w_in, 2560 + g * 128)
        ytok[4 + g] = []
        for tb in range(4):
            b, t = proj_cm(c, wr, s, tw, HT, tb, None)
            r, rf = zring.take()
            e = c.act_(zst[:, r, :], c.P[b][:, :], ACT.Silu, t, rf)
            c.banks.give(b, e)
            b, bf = c.banks.take()
            t2 = c.mm(c.P[b][:, :], pw[:, g, :], U[g % 2][:, 8 + tb * 512:8 + (tb + 1) * 512], True, True, bf, tp_,
                      tpw, sig=True)
            r2, rf2 = yring.take()
            e = c.stt(yst[:, r2, :], c.P[b][:, :], ps[:, g:g + 1], zst[:, r, :], ALU.mult, ALU.mult, t2, e, rf2)
            c.banks.give(b, e)
            zring.give(r, e)
            d = c.dma(c.act, Y[4 + g][:, tb * 512:(tb + 1) * 512], yst[:, r2, :], ysem[r2], e)
            ytok[4 + g].append(d)
            yring.give(r2, d)
        wr.ring.give(s, t)
        ufree[g % 2] = t2

    for g in range(4):
        w = 2 << g
        u = U[g % 2]
        s, tw = wr.load(w_in, 2048 + g * 128)
        tu = []
        for tb in range(4):
            b, t = proj_cm(c, wr, s, tw, HT, tb, None)
            e = c.act_(u[:, 8 + tb * 512:8 + (tb + 1) * 512], c.P[b][:, :], ACT.Copy, t, ufree[g % 2], pads)
            c.banks.give(b, e)
            tu.append(e)
        wr.ring.give(s, t)
        t = c.tt(c.dve, Sa[:, 1:2064], u[:, 0:2063], u[:, 1:2064], ALU.add, tu, c.dve.last())
        cur, nxt, lo, hi, d = Sa, Sb, 1, 2063, 1
        for _ in range(g):
            t = c.tt(c.dve, nxt[:, lo + d:hi - d + 1], cur[:, lo:hi - 2 * d + 1], cur[:, lo + 2 * d:hi + 1], ALU.add, t)
            cur, nxt, lo, hi, d = nxt, cur, lo + d, hi - d, 2 * d
        t = c.tt(c.dve, cur[:, 8:16], cur[:, 8:16], ec[:, g, 0:8], ALU.mult, t, tec)
        t = c.tt(c.dve, cur[:, 2048:2056], cur[:, 2048:2056], ec[:, g, 8:16], ALU.mult, t)
        t = c.stt(u[:, 8:2056], cur[:, 8:2056], 1.0 / w, u[:, 8:2056], ALU.mult, ALU.subtract, t)
        if pend is not None:
            pool_out(*pend)
        pend = (g, t)
    for q in range(4):
        s, tw = wr.load(w_in, 1536 + q * 128)
        ztok[q] = []
        for tb in range(4):
            b, t = proj_cm(c, wr, s, tw, HT, tb, None)
            r, rf = zring.take()
            e = c.act_(zst[:, r, :], c.P[b][:, :], ACT.Silu, t, rf)
            c.banks.give(b, e)
            d = c.dma(c.act, GD[q][:, tb * 512:(tb + 1) * 512], zst[:, r, :], zsem[r], e)
            ztok[q].append(d)
            zring.give(r, d)
        wr.ring.give(s, t)
        if q == 0:
            pool_out(*pend)
    c.fence()
    PP = [c.view(R0, 2052), c.view(R0 + 2052, 2052)]
    TT = [c.view(R0 + 4104, 2048), c.view(R0 + 6152, 2048)]
    ST = [c.view(R0 + 8200, 16, 128), c.view(R0 + 10248, 16, 128)]
    pads = [c.ms(c.pool, p[:, a:b], 0.0) for p in PP for a, b in ((0, 1), (2049, 2052))]
    pfree, tfree, sfree = [None, None], [None, None], [None, None]
    ssem = [c.dsem(), c.dsem()]
    stok = {}
    cb2 = c.col("conv_b_2")
    cw2 = c.col("conv_w_2")
    pend = None

    def to_time(n, tc_):
        q = n % 2
        tv = TT[q].rearrange("p (n j) -> p n j", j=16)
        ev = []
        for jg in range(4):
            b, bf = c.banks.take()
            for jj in range(4):
                t = c.tr(c.P[b][:, jj * 128:(jj + 1) * 128], tv[:, :, 4 * jg + jj], c.ident, bf, tc_, sig=(jj == 3))
            e = c.act_(ST[q][:, 4 * jg:4 * jg + 4, :].rearrange("p a b -> p (a b)"), c.P[b][:, :], ACT.Copy, t, sfree[q])
            c.banks.give(b, e)
            ev.append(e)
        tfree[q] = t
        stok[n] = c.dma(c.act, GD[8 + n], ST[q][:, :, :].rearrange("p a b -> p (a b)"), ssem[q], ev)
        sfree[q] = stok[n]

    for n in range(12):
        q = n % 2
        s, tw = wr.load(w_in, n * 128)
        ev, ew = [], []
        for tb in range(4):
            b, t = proj_cm(c, wr, s, tw, HT, tb, None)
            e = c.act_(PP[q][:, 1 + tb * 512:1 + (tb + 1) * 512], c.P[b][:, :], ACT.Copy, t, pfree[q], pads)
            e2 = c.ts(c.dve, TT[q][:, tb * 512:(tb + 1) * 512], PP[q][:, 1 + tb * 512:1 + (tb + 1) * 512],
                      cw2[:, 12 + n:13 + n], cb2[:, n:n + 1], ALU.mult, ALU.add, e, tfree[q])
            c.banks.give(b, e)
            ev.append(e)
            ew.append(e2)
        wr.ring.give(s, t)
        t = c.stt(TT[q][:, :], PP[q][:, 0:2048], cw2[:, n:n + 1], TT[q][:, :], ALU.mult, ALU.add, ev, ew)
        t = c.stt(TT[q][:, :], PP[q][:, 2:2050], cw2[:, 24 + n:25 + n], TT[q][:, :], ALU.mult, ALU.add, t)
        pfree[q] = t
        if pend is not None:
            to_time(*pend)
        pend = (n, t)
    to_time(*pend)
    c.fence()
    if dbg == "b2a":
        dump(Y[4:8], "o0")
        dump(GD[8:20], "o1")
        return
    hyena(c, A, Y, GD, ztok, stok)
    YT = c.view(R1, 8, 2048)
    UT, ZT = c.view(R2, 2, 2048), c.view(R2 + 4096, 2, 2048)
    ycm = []
    for q in range(4):
        r = q % 2
        rf = ycm[q - 2] if q >= 2 else None
        t1 = c.dma(c.sp, UT[:, r, :], GD[4 + q], c.dsem_of(40 + r), rf)
        t2 = c.dma(c.act, ZT[:, r, :], GD[q], c.dsem_of(42 + r), rf)
        es = []
        for jg in range(4):
            b, bf = c.banks.take()
            for jj in range(4):
                j = 4 * jg + jj
                t = c.tr(c.P[b][:, jj * 128:(jj + 1) * 128], UT[:, r, j * 128:(j + 1) * 128], c.ident, bf, t1,
                         sig=(jj == 3))
            a3 = "p (n j) -> p j n"
            e = c.tt(c.dve, YT[:, q, :].rearrange(a3, j=16)[:, 4 * jg:4 * jg + 4, :],
                     c.P[b][:, :].rearrange("p (j n) -> p j n", j=4),
                     ZT[:, r, :].rearrange(a3, j=16)[:, 4 * jg:4 * jg + 4, :], ALU.mult, t, t2)
            c.banks.give(b, e)
            es.append(e)
        ycm.append(es)
    if dbg == "b2b":
        dump(YT[:, 0:4, :], "o0")
        return
    WO = c.view(R0, 8, 1024)
    o = R0 + 8192
    sq = c.view(o, 4, 512)
    sm = c.view(o + 2048, 2, 512)
    rs = c.view(o + 3072, 2, 512)
    o = R2
    X = c.view(o + 8192, 2, 1024)
    T = c.view(o + 10240, 1024)
    pg = c.view(o + 11264, 1024)
    st = c.view(c.take(16), 16)
    ly = {}
    for tb in range(4):
        for k in range(4):
            ly[(k, tb)] = ycm[k]
        for k in range(4, 8):
            ly[(k, tb)] = c.dma(c.sp if k % 2 else c.act, YT[:, k, tb * 512:(tb + 1) * 512],
                                Y[k][:, tb * 512:(tb + 1) * 512], c.dsem_of(tb * 8 + k))
    two = [c.dma(c.sp, WO[:, k, :], A["w_out_2"][0][k * 128:(k + 1) * 128, :], c.dsem_of(32 + k)) for k in range(8)]
    tpg = bcast_row(c, pg[:, :], rows_of(A, "post_norm_g_2"))
    qring, mring = Ring(4), Ring(2)
    yat = []
    for tb in range(4):
        sl = slice(tb * 512, (tb + 1) * 512)
        last = []
        for grp in range(2):
            m, mf = mring.take()
            gain = c.col("norm_h_g_2" if grp == 0 else "norm_p_g_2")
            tp = None
            for k in range(4):
                r, rf = qring.take()
                e = c.act_(sq[:, r, :], YT[:, 4 * grp + k, sl], ACT.Square, ly[(4 * grp + k, tb)], rf)
                if k == 0:
                    tp = c.cp(c.pool, sm[:, m, :], sq[:, r, :], e, mf)
                else:
                    tp = c.tt(c.pool, sm[:, m, :], sm[:, m, :], sq[:, r, :], ALU.add, e, tp)
                qring.give(r, tp)
            b, bf = c.banks.take()
            t = c.mm(c.P[b][:, :], c.ones, sm[:, m, :], True, True, bf, tp, sig=True)
            e = rsqrt(c, rs[:, m, :], c.P[b][:, :], 1.0 / 512, t)
            c.banks.give(b, e)
            for k in range(4):
                v = YT[:, 4 * grp + k, sl]
                e2 = c.stt(v, v, gain[:, k:k + 1], rs[:, m, :], ALU.mult, ALU.mult, e, ly[(4 * grp + k, tb)])
                last.append(e2)
            mring.give(m, t, e2)
        yat.append(last)
    xring, xsem = Ring(2), [c.dsem() for _ in range(2)]
    x2sem = [c.dsem() for _ in range(2)]
    x2tok, tf = {}, [None]

    def lhs(i, k):
        return YT[:, k, i * 128:(i + 1) * 128]

    def epilogue(i, bb, t, rf):
        r, xf = xring.take()
        X_ = X[:, r, :]
        tx = c.dma(c.sp, X_, X1[i * 128:(i + 1) * 128, :], xsem[r], xf, rf, c.x1tok[i])
        s = st[:, 4 * r:4 * r + 2]
        e1 = c.act_(T[:, 0:512], c.P[bb[0]][:, :], ACT.Square, t, tf[0], accum=s[:, 0:1])
        e1 = c.act_(T[:, 512:1024], c.P[bb[1]][:, :], ACT.Square, t, accum=s[:, 1:2])
        s1 = st[:, 4 * r + 2:4 * r + 3]
        e1 = c.tt(c.dve, s1, s[:, 0:1], s[:, 1:2], ALU.add, e1)
        e1 = rsqrt(c, s1, s1, 1.0 / D, e1)
        for h in range(2):
            e = c.stt(T[:, h * 512:(h + 1) * 512], c.P[bb[h]][:, :], s1, pg[:, h * 512:(h + 1) * 512], ALU.mult,
                      ALU.mult, e1, tpg)
            c.banks.give(bb[h], e)
        e = c.tt(c.pool, X_, X_, T[:, :], ALU.add, e, tx)
        tf[0] = e
        x2tok[i] = c.dma(c.act, X2[i * 128:(i + 1) * 128, :], X_, x2sem[r], e)
        xring.give(r, e, x2tok[i])
        return e

    out_stage(c, 8, lhs, lambda i: [yat[i // 4], two], WO, None, epilogue, lambda i, t: None, YT, None,
              lambda i: X[:, i % 2, :])
    c.x2tok = [x2tok[i] for i in range(16)]
    c.fence()
    if dbg == "b2":
        dump(X2, "o0")
        dump(YT, "o1")


def hyena(c, A, Y, GD, ztok, stok):
    o = [c.R0]
    flat = lambda v: v.rearrange("p a b -> p (a b)")

    def al(n):
        o[0] += n
        return o[0] - n

    G = c.view(al(2048), 32, 64)
    KT = c.view(al(4096), 32, 128)
    AK = c.view(al(4096), 32, 128)
    KR = c.view(al(4096), 32, 128)
    KI = c.view(al(4096), 32, 128)
    AD = c.view(al(4096), 32, 128)
    DD = c.view(al(4096), 32, 128)
    T2 = c.view(al(4096), 32, 128)
    WX = c.view(al(6144), 32, 192)
    WI = c.view(al(4096), 32, 128)
    WP = c.view(al(1024), 2, 512)
    DEC = c.view(al(1024), 2, 512)
    U = c.view(al(4096), 2, 2048)
    GT = c.view(al(2048), 2048)
    WK, WA = c.view(al(128), 128), c.view(al(256), 2, 128)
    WAI = c.view(al(256), 2, 128)
    dr = c.view(al(128), 128)
    sg = c.view(al(1), 1)
    fc = c.view(al(8), 8)
    ld = []
    n_ = [0]

    def load(dst, src):
        n_[0] += 1
        ld.append(c.dma(c.sp if n_[0] % 2 else c.act, dst, src, c.dsem_of(n_[0] - 1), slow=True))

    Z = c.view(c.R0 + 2048, 2048)
    H = [c.view(c.R0 + 2048 + 4096, 2048), c.view(c.R0 + 2048 + 8192, 2048)]
    Q = c.view(c.R0 + 2048 + 12288, 2048)
    WF = c.view(c.R0 + 2048 + 16384, 3, 128)
    z0 = c.ms(c.pool, WF[:, :, :], 0.0)
    c.sp.wait(z0)
    c.act.wait(z0)
    load(Z[0:66, :], A["k_z"])
    for h in range(2):
        load(WF[33 * h:33 * h + 33, 0, 64 * h:64 * h + 64], A["filt_w1_2"][0])
        load(WF[64 * h:64 * h + 64, 1, 64 * h:64 * h + 64], A["filt_w2_2"][0])
        load(WF[64 * h:64 * h + 64, 2, 64 * h:64 * h + 64], A["filt_w3_2"][0])
        for q, nm in enumerate(("filt_freq_2", "filt_b1_2", "filt_b2_2", "filt_b3_2")):
            load(fc[64 * h:64 * h + 64, q:q + 1], A[nm].rearrange("l n -> n l"))
        load(WP[64 * h:64 * h + 64, :, :],
             A["filt_w_out_2"][0].rearrange("k (o d n) -> k o d n", o=2, d=2)[:, :, h, :])
    load(WK, A["k_wk"])
    load(flat(WA), A["k_wa"])
    load(flat(WAI), A["k_wai"])
    load(sg, A["k_sg"])
    load(WX[:, :, :].rearrange("p a b -> p (a b)"), A["k_wx"])
    load(WI[:, :, :].rearrange("p a b -> p (a b)"), A["k_wi"])
    c.pe.wait(ld)
    c.dve.wait(ld)
    c.act.wait(ld)
    tfb = c.ts(c.dve, fc[:, 4:7], fc[:, 1:4], fc[:, 0:1], None, ALU.mult, None, ld)
    src, kk, th = Z, 66, None
    tg = None
    for layer in range(3):
        dst = H[layer % 2]
        new = []
        for tb in range(4):
            sl = slice(tb * 512, (tb + 1) * 512)
            b, bf = c.banks.take()
            t = c.mm(c.P[b][:, :], WF[0:kk, layer, :], src[0:kk, sl], True, True, bf, th, sig=True)
            d = dst[:, sl]
            q = Q[:, sl]
            e = c.ts(c.dve, d, c.P[b][:, :], fc[:, 0:1], fc[:, 4 + layer:5 + layer], ALU.mult, ALU.add, t, tfb, th)
            c.banks.give(b, e)
            e2 = c.ts(c.dve, q, d, 1.0 / TWO_PI, MAGIC, ALU.mult, ALU.add, e)
            e2 = c.ts(c.dve, q, q, MAGIC, None, ALU.subtract, None, e2)
            hi = float(np.float32(6.28125))
            mid = float(np.float32(TWO_PI - 6.28125))
            lo = float(np.float32(TWO_PI - 6.28125 - float(np.float32(TWO_PI - 6.28125))))
            for v in (hi, mid, lo):
                e2 = c.stt(d, q, -v, d, ALU.mult, ALU.add, e2)
            e2 = c.ts(c.dve, d, d, 3.1415925, -3.1415925, ALU.min, ALU.max, e2)
            if layer < 2:
                new.append(c.act_(d, d, ACT.Sin, e2))
            else:
                new.append(c.act_(G[:, tb * 8:(tb + 1) * 8, :].rearrange("p a b -> p (a b)"), d, ACT.Sin, e2))
        src, kk, th = dst, 128, new
    tg = th
    c.fence()

    jobs = [(0, 0), (0, 1), (1, 0), (1, 1), (0, 2), (0, 3), (1, 2), (1, 3)]
    dring = Ring(2)
    dsem_ = [c.dsem_of(i) for i in range(2)]
    usem = [c.dsem_of(2 + i) for i in range(2)]
    gsem, rsem, osem, dup = c.dsem_of(4), c.dsem_of(5), [c.dsem_of(6 + i) for i in range(2)], [c.dsem_of(8 + i) for i in range(2)]
    ksh = [c.dsem_of(10 + i) for i in range(8)]
    ash = [c.dsem_of(18 + i) for i in range(8)]
    bsh = [c.dsem_of(26 + i) for i in range(8)]
    F = {n: None for n in ("KT", "AK", "K", "AD", "DD", "T2", "dr", "GT")}
    ufree = [None, None]
    utok = {}
    SH = [c.nc.dram_tensor(f"sh{i}", (32, 128, 128), F32, kind="Internal").ap() for i in range(3)]

    def shuffle(dram, dst, src, sems, out, *after):
        rows = dram.rearrange("b q n -> (b q) n").rearrange("(p m) n -> p m n", m=32)
        w = [c.dma(c.act, rows[:, 8 * g:8 * g + 8, :], src[:, 8 * g:8 * g + 8, :], sems[g], out[2 * g:2 * g + 2], F[dram.name])
             for g in range(4)]
        sh = [c.dma(c.sp, dst[:, 8 * g:8 * g + 8, :], dram[8 * g:8 * g + 8, :, :].rearrange("b q n -> q b n"),
                    sems[4 + g], w, *after) for g in range(4)]
        F[dram.name] = sh
        return w, sh

    def unshuffle(dram, dst, src, sems, out, *after):
        rows = dram.rearrange("b q n -> (b q) n").rearrange("(p m) n -> p m n", m=32)
        w = [c.dma(c.act, dram[8 * g:8 * g + 8, :, :].rearrange("b q n -> q b n"), src[:, 8 * g:8 * g + 8, :], sems[g],
                   out[2 * g:2 * g + 2], F[dram.name]) for g in range(4)]
        sh = [c.dma(c.sp, dst[:, 8 * g:8 * g + 8, :], rows[:, 8 * g:8 * g + 8, :], sems[4 + g], w, *after)
              for g in range(4)]
        F[dram.name] = sh
        return w, sh

    for d_ in SH:
        F[d_.name] = None

    def kgen(i):
        od, ch = jobs[i]
        cs = slice(ch * 128, (ch + 1) * 128)
        tdr = c.dma(c.act, dr[0:1, :], A["hyena_d_2"][0, od:od + 1, cs], rsem, F["dr"])
        ev = []
        for g in range(8):
            r, rf = dring.take()
            td = c.dma(c.sp, DEC[:, r, :].rearrange("p (a b) -> p a b", b=128),
                       A["k_dec"][:, 4 * g:4 * g + 4, cs], dsem_[r], rf)
            b, bf = c.banks.take()
            for j in range(4):
                n2 = 4 * g + j
                for h in range(2):
                    rr = slice(64 * h, 64 * h + 64)
                    t = c.mm(c.P[b][rr, j * 128:(j + 1) * 128], G[rr, n2, :], WP[rr, od, cs], True, True, bf,
                             sig=(j == 3 and h == 1))
            e = c.tt(c.dve, flat(KT[:, 4 * g:4 * g + 4, :]), c.P[b][:, :], DEC[:, r, :], ALU.mult, t, td, F["KT"])
            c.banks.give(b, e)
            dring.give(r, e)
            if g == 0:
                e = c.tt(c.dve, KT[0:1, 0, :], KT[0:1, 0, :], dr[0:1, :], ALU.add, e, tdr)
                F["dr"] = e
            ev.append(e)
        out = []
        for g in range(8):
            b, bf = c.banks.take()
            t = c.mm(c.P[b][:, :], WK, flat(KT[:, 4 * g:4 * g + 4, :]), True, True, bf, ev[g], sig=True)
            e = c.act_(flat(AK[:, 4 * g:4 * g + 4, :]), c.P[b][:, :], ACT.Copy, t, F["AK"])
            c.banks.give(b, e)
            out.append(e)
        F["AK"], sh = shuffle(SH[0], KT, AK, ksh, out, t)
        return sh

    def kspec(i, sh):
        er, ei = [], []
        for g in range(8):
            b, bf = c.banks.take()
            for j in range(4):
                t = c.mm(c.P[b][:, j * 128:(j + 1) * 128], WX[:, 4 * g + j, 0:128], KT[:, 4 * g + j, :], True, True,
                         bf, sh[g // 2], sig=(j == 3))
            e1 = c.act_(flat(KR[0:64, 4 * g:4 * g + 4, :]), c.P[b][0:64, :], ACT.Copy, t, F["K"])
            e2 = c.act_(flat(KI[64:128, 4 * g:4 * g + 4, :]), c.P[b][64:128, :], ACT.Copy, t, F["K"])
            c.banks.give(b, e2)
            er.append(e1)
            ei.append(e2)
        F["KT"] = t
        d1 = c.dma(c.act, KR[64:128, :, :], KR[0:64, :, :], dup[0], er, F["K"])
        d2 = c.dma(c.sp, KI[0:64, :, :], KI[64:128, :, :], dup[1], ei, F["K"])
        e = c.cp(c.dve, KR[64:65, 0, :], KI[64:65, 0, :], d1, ei[0])
        e = c.ms(c.dve, KI[64:65, 0, :], 0.0, e, d2)
        e2 = c.ms(c.dve, KI[0:1, 0, :], 0.0, d2)
        for g in range(8):
            kt[g] = [d1, d2, e, e2]

    def da(i):
        od, ch = jobs[i]
        if od == 0:
            utok[i] = c.dma(c.sp, U[:, i % 2, :], GD[8 + ch], usem[i % 2], ufree[i % 2])
        out = []
        for e_ in range(2):
            for jg in range(4):
                b, bf = c.banks.take()
                t = c.mm(c.P[b][:, :], WA[:, e_, :], U[:, i % 2, jg * 512:(jg + 1) * 512], True, True, bf, utok[i],
                         sig=True)
                n2 = 16 * e_ + 4 * jg
                if jg % 2:
                    e = c.act_(flat(AD[:, n2:n2 + 4, :]), c.P[b][:, :], ACT.Copy, t, F["AD"])
                else:
                    e = c.cp(c.dve, flat(AD[:, n2:n2 + 4, :]), c.P[b][:, :], t, F["AD"])
                c.banks.give(b, e)
                out.append(e)
        ufree[i % 2] = t
        return out

    def dshuffle(out):
        F["AD"], sh = shuffle(SH[1], DD, AD, ash, out, F["DD"])
        return sh

    def db(i, sh):
        yt = []
        for g in range(8):
            b1, f1 = c.banks.take()
            b2, f2 = c.banks.take()
            for j in range(4):
                bk = 4 * g + j
                ps = slice(j * 128, (j + 1) * 128)
                c.mm(c.P[b1][:, ps], WX[:, bk, 0:128], DD[:, bk, :], True, True, f1, sh[g // 2])
                t = c.mm(c.P[b2][:, ps], WX[:, bk, 64:192], DD[:, bk, :], True, True, f2, sig=(j == 3))
            kr, ki = flat(KR[:, 4 * g:4 * g + 4, :]), flat(KI[:, 4 * g:4 * g + 4, :])
            e1 = c.tt(c.dve, kr, c.P[b1][:, :], kr, ALU.mult, t, kt[g])
            e2 = c.stt(ki, c.P[b2][:, :], sg[:, 0:1], ki, ALU.mult, ALU.mult, t)
            c.banks.give(b1, e1)
            c.banks.give(b2, e2)
            e3 = c.tt(c.pool, flat(DD[:, 4 * g:4 * g + 4, :]), kr, ki, ALU.add, e1, e2, t)
            yt.append(e3)
        F["K"] = e3
        return yt

    def binv(i, yt):
        out = []
        for g in range(8):
            b, bf = c.banks.take()
            for j in range(4):
                bk = 4 * g + j
                t = c.mm(c.P[b][:, j * 128:(j + 1) * 128], WI[:, bk, :], DD[:, bk, :], True, True, bf, yt[g],
                         sig=(j == 3))
            e = c.act_(flat(AK[:, 4 * g:4 * g + 4, :]), c.P[b][:, :], ACT.Copy, t, F["AK"])
            c.banks.give(b, e)
            out.append(e)
        F["DD"] = t
        F["AK"], sh = unshuffle(SH[2], T2, AK, bsh, out, F["T2"])
        return sh

    def ainv(i, sh):
        od, ch = jobs[i]
        tg_ = c.dma(c.sp, GT[:, :], GD[8 + 4 * (od + 1) + ch], gsem, F["GT"])
        ev = []
        for jg in range(4):
            b, bf = c.banks.take()
            for e_ in range(2):
                n2 = 16 * e_ + 4 * jg
                t = c.mm(c.P[b][:, :], WAI[:, e_, :], flat(T2[:, n2:n2 + 4, :]), e_ == 0, e_ == 1, bf, sh,
                         sig=(e_ == 1))
            e = c.tt(c.dve, U[:, i % 2, jg * 512:(jg + 1) * 512], c.P[b][:, :], GT[:, jg * 512:(jg + 1) * 512],
                     ALU.mult, t, tg_, ufree[i % 2])
            c.banks.give(b, e)
            ev.append(e)
        F["T2"] = t
        F["GT"] = e
        if od == 0:
            utok[i + 2] = ev
        else:
            ufree[i % 2] = c.dma(c.act, GD[4 + ch], U[:, i % 2, :], osem[ch % 2], ev)
            ytime[ch] = ufree[i % 2]

    ytime = [None] * 4
    kt = [None] * 8
    ks = kgen(0)
    dsh = dshuffle(da(0))
    kspec(0, ks)
    for i in range(8):
        if i < 7:
            ks = kgen(i + 1)
        yt = db(i, dsh)
        if i < 7:
            dout = da(i + 1)
        bs = binv(i, yt)
        if i < 7:
            dsh = dshuffle(dout)
            kspec(i + 1, ks)
        ainv(i, bs)
    c.fence()


def window_constants():
    q = np.arange(64)
    start = np.clip(q - 8, 0, 48)
    kc = np.arange(64)
    inside = (kc[None, :] >= start[:, None]) & (kc[None, :] < start[:, None] + 16)
    m = np.where(inside, 0.0, -1e30).astype(np.float32)
    s, t = np.arange(128)[:, None], np.arange(128)[None, :]
    same = s // 16 == t // 16
    pair = np.stack([same & (s <= t), same & (s >= t)]).astype(np.int32)
    reset = np.ones((1, S_LEN), np.float32)
    reset[0, ::128] = 0.0
    return {"k_flip": np.kron(np.eye(2), np.eye(64)[::-1]).astype(np.float32), "k_win": np.concatenate([m, m], 0), "k_pair": pair.transpose(1, 0, 2).copy(), "k_reset": reset}


def block3(c, A, X2, out, Y, GD, dbg, dump):
    R0, R1, R2 = c.R0, c.R1, c.R2
    HT = c.view(R1, 8, 2048)
    w_in = A["w_in_3"][0]
    b_in = c.col("b_in_3")
    ytok = {}
    attention(c, A, HT, w_in, b_in, Y, ytok)
    if dbg == "b3a":
        dump(Y[0:4], "o0")
        return
    recurrence(c, A, HT, w_in, b_in, Y, ytok)
    if dbg == "b3b":
        dump(Y[4:8], "o0")
        return
    YT = c.view(R1, 8, 2048)
    WO = c.view(R0, 8, 1024)
    o = R2
    X = c.view(o, 3, 1024)
    T = c.view(o + 3072, 2, 1024)
    bo, lg, lb = (c.view(o + 5120 + 1024 * i, 1024) for i in range(3))
    st = c.view(o + 8192, 2, 16)
    eps = c.view(o + 8224, 1)[:, :]
    te = c.ms(c.pool, eps, 1e-5)
    ly = [c.dma(c.sp if k % 2 else c.act, YT[:, k, :], Y[k], c.dsem_of(k)) for k in range(8)]
    two = [c.dma(c.sp, WO[:, k, :], A["w_out_3"][0][k * 128:(k + 1) * 128, :], c.dsem_of(8 + k)) for k in range(8)]
    tb = [c.dma(c.act, dst[:, :], rows_of(A, n).partition_broadcast(128), c.dsem_of(16 + i))
          for i, (dst, n) in enumerate(((bo, "b_out_3"), (lg, "ln_gain_3"), (lb, "ln_bias_3")))]
    xring, tring = Ring(3), Ring(2)
    xsem = [c.dsem_of(20 + i) for i in range(3)]
    osem = [c.dsem_of(23 + i) for i in range(3)]
    alpha = 2.0 ** 0.25

    def epilogue(i, bb, t, rf):
        r, xf = xring.take()
        q, tf = tring.take()
        X_, T_, s = X[:, r, :], T[:, q, :], st[:, q, :]
        tx = c.dma(c.sp, X_, X2[i * 128:(i + 1) * 128, :], xsem[r], xf, c.x2tok[i])
        for h in range(2):
            sl = slice(h * 512, (h + 1) * 512)
            e = c.tt(c.dve, T_[:, sl], c.P[bb[h]][:, :], bo[:, sl], ALU.add, t, tb, tf)
            c.banks.give(bb[h], e)
        e = c.stt(X_, X_, alpha, T_, ALU.mult, ALU.add, e, tx)
        for h in range(2):
            o_, a_ = s[:, 6 * h:6 * h + 6], X_[:, h * 512:(h + 1) * 512]
            e1 = c.dve.do(lambda en, o_=o_, a_=a_: en.bn_stats(o_, a_), e)
        o_, a_ = s[:, 12:14], s[:, 0:12]
        e1 = c.dve.do(lambda en: en.bn_aggr(o_, a_), e1)
        v = s[:, 14:15]
        e2 = c.act_(v, s[:, 13:14], ACT.Ln, e1, te, bias=eps)
        e2 = c.act_(v, v, ACT.Exp, e2, scale=-0.5)
        e3 = c.ts(c.dve, T_, X_, s[:, 12:13], v, ALU.subtract, ALU.mult, e2, e1)
        e4 = c.tt(c.pool, T_, T_, lg[:, :], ALU.mult, e3, tb)
        e5 = c.tt(c.pool, X_, T_, lb[:, :], ALU.add, e4, e3)
        d = c.dma(c.act, out[i * 128:(i + 1) * 128, :], X_, osem[r], e5)
        xring.give(r, d)
        tring.give(q, e5)
        return e5

    out_stage(c, 8, lambda i, k: YT[:, k, i * 128:(i + 1) * 128], lambda i: [ly, two], WO, None, epilogue,
              lambda i, t: None, None, None, None)


def attention(c, A, HT, w_in, b_in, Y, ytok):
    R0, R2 = c.R0, c.R2
    V, VO = c.view(R0, 16, 512), c.view(R0 + 8192, 16, 512)
    wr = WRing(c, R2, 4)
    o = R2 + 4096
    QK = c.view(o, 2, 2048)
    SG = c.view(o + 4096, 2048)
    YS = c.view(o + 6144, 3, 512)
    BT = c.view(o + 7680, 2, 960)
    E = c.view(o + 9600, 3, 512)
    PT = c.view(o + 11136, 3, 512)
    win = c.view(o + 12672, 64)
    st = c.view(o + 12736, 3, 4)
    flip = c.view(o + 12752, 128)
    tflip = c.dma(c.act, flip[:, :], A["k_flip"], c.dsem_of(9))
    vb = c.view(o + 7680, 512)
    PR = c.view(o + 9600, 128)
    c.banks = Ring(6)
    obank = Ring(2)
    tvb = c.dma(c.act, vb[:, :], A["b_in_3"][0, 1024:1536].partition_broadcast(128), c.dsem_of(0))
    twin = c.dma(c.act, win[:, :], A["k_win"], c.dsem_of(1))
    sl = [wr.load(w_in, 1024 + q * 128) for q in range(4)]
    wt = [t for _, t in sl]
    vt = []
    for i in range(16):
        b, bf = c.banks.take()
        for k in range(8):
            t = c.mm(c.P[b][:, :], HT[:, k, i * 128:(i + 1) * 128], wr.W[:, 0:4, k * 128:(k + 1) * 128], k == 0, k == 7,
                     bf, wt, sig=(k == 7))
        e = c.tt(c.dve, V[:, i, :], c.P[b][:, :], vb[:, :], ALU.add, t, tvb)
        c.banks.give(b, e)
        vt.append(e)
    for s, _ in sl:
        wr.ring.give(s, t)
    tvo = [c.dma(c.act, VO[0:64, 0:15, :], V[64:128, 0:15, :], c.dsem_of(2), vt),
           c.dma(c.act, VO[64:128, 0:15, :], V[0:64, 1:16, :], c.dsem_of(3), vt)]
    RD = c.nc.dram_tensor("rpb_rows", (120, 128), F32, kind="Internal").ap()
    t = c.ms(c.pool, PR[0:120, :], 0.0)
    t = c.dma(c.act, PR[0:120, 48:79], A["rpb_3"][0].rearrange("h a b -> (h a) b"), c.dsem_of(4), t)
    trd = c.dma(c.act, RD, PR[0:120, :], c.dsem_of(5), t)
    bsem = [c.dsem_of(6 + i) for i in range(4)]
    ysem = [c.dsem_of(10 + i) for i in range(3)]
    bfree, qkfree = [[vt], [vt]], [None, None, None]
    ering, pring, yring = Ring(3), Ring(3), Ring(3)
    for i in range(3):
        ering.give(i, trd)
    scale = 64 ** -0.5
    sgfree = None
    for pr in range(4):
        bt = BT[:, pr % 2, :].rearrange("p (a b) -> p a b", b=64)
        tbs = []
        for hh in range(2):
            src = bass.AP(RD.tensor, (2 * pr + hh) * 15 * 128, [[1, 64], [128, 15], [1, 64]])
            tbs.append(c.dma(c.act, bt[64 * hh:64 * hh + 64, :, :], src, bsem[2 * (pr % 2) + hh], trd, bfree[pr % 2]))
        tfl = []
        for a, n in ((0, 8), (8, 7)):
            b, bf = c.banks.take()
            t = c.mm(c.P[b][:, 0:n * 64], flip[:, :], BT[:, pr % 2, a * 64:(a + n) * 64], True, True, bf, tbs, tflip,
                     sig=True)
            tfl.append((a, n, b, t))
        for a, n, b, t in tfl:
            tbt = c.tt(c.dve, bt[:, a:a + n, :], c.P[b][:, 0:n * 64].rearrange("p (a b) -> p a b", b=64),
                       win[:, :].unsqueeze(1).to_broadcast([128, n, 64]), ALU.add, t, twin)
            c.banks.give(b, tbt)
        tqk = []
        for q in range(2):
            s, tw = wr.load(w_in, q * 512 + pr * 128)
            for tb in range(4):
                b, t = proj_cm(c, wr, s, tw, HT, tb, None)
                e = c.act_(QK[:, q, tb * 512:(tb + 1) * 512], c.P[b][:, :], ACT.Identity, t, qkfree[q],
                           bias=b_in[:, 4 * q + pr:4 * q + pr + 1])
                c.banks.give(b, e)
                tqk.append(e)
            wr.ring.give(s, t)
        s, tw = wr.load(w_in, 1536 + pr * 128)
        tsg = []
        for tb in range(4):
            b, t = proj_cm(c, wr, s, tw, HT, tb, None)
            e = c.act_(SG[:, tb * 512:(tb + 1) * 512], c.P[b][:, :], ACT.Silu, t, sgfree,
                       bias=b_in[:, 12 + pr:13 + pr])
            c.banks.give(b, e)
            tsg.append(e)
        wr.ring.give(s, t)
        ytok[pr] = []
        stage = {}

        def scores(r):
            r0 = min(max(r - 4, 0), 24)
            b, bf = c.banks.take()
            for hh in range(2):
                rr = slice(64 * hh, 64 * hh + 64)
                t = c.mm(c.P[b][rr, :], QK[rr, 0, r * 64:(r + 1) * 64], QK[rr, 1, r0 * 64:r0 * 64 + 512], True, True,
                         bf, tqk, sig=(hh == 1))
            stage["qk"] = t
            d0 = r0 - r + 7
            k, ef = ering.take()
            x = E[:, k, :]
            s_ = st[:, k, :]
            e = c.stt(x.rearrange("p (a b) -> p a b", b=64), c.P[b][:, :].rearrange("p (a b) -> p a b", b=64), scale,
                      bt[:, d0:d0 + 8, :], ALU.mult, ALU.add, t, ef, tbt)
            c.banks.give(b, e)
            e = c.dve.do(lambda en: en.tensor_reduce(s_[:, 0:1], x, AXX, ALU.max, negate=True), e)
            e = c.act_(x, x, ACT.Exp, e, bias=s_[:, 0:1], accum=s_[:, 1:2])
            e = c.recip(s_[:, 2:3], s_[:, 1:2], e)
            e = c.ts(c.dve, x, x, s_[:, 2:3], None, ALU.mult, None, e)
            stage[("p", r)] = (k, e)
            stage["bt"] = e

        def turn(r):
            k, e = stage.pop(("p", r))
            b, bf = c.banks.take()
            for j in range(4):
                t = c.tr(c.P[b][:, j * 128:(j + 1) * 128], E[:, k, j * 128:(j + 1) * 128], c.ident, bf, e, sig=(j == 3))
            ering.give(k, t)
            k, pf = pring.take()
            e = c.act_(PT[:, k, :], c.P[b][:, :], ACT.Copy, t, pf)
            c.banks.give(b, e)
            stage[("t", r)] = (k, e)

        def values(r):
            r0 = min(max(r - 4, 0), 24)
            if r % 8 == 0:
                stage["ob"] = obank.take()
            ob, of = stage["ob"]
            k, e = stage.pop(("t", r))
            vv = VO if r0 % 2 else V
            for hh in range(2):
                h = 2 * pr + hh
                for j in range(4):
                    t = c.mm(c.P[6 + ob][64 * hh:64 * hh + 64, (r % 8) * 64:(r % 8) * 64 + 64],
                             vv[:, r0 // 2 + j, h * 64:(h + 1) * 64], PT[:, k, j * 128 + 64 * hh:j * 128 + 64 * hh + 64],
                             j == 0, j == 3, of, e, vt, tvo, sig=(hh == 1 and j == 3))
            pring.give(k, t)
            if r % 8 == 7:
                tb = r // 8
                y, yf = yring.take()
                e = c.tt(c.dve, YS[:, y, :], c.P[6 + ob][:, :], SG[:, tb * 512:(tb + 1) * 512], ALU.mult, t, tsg, yf)
                obank.give(ob, e)
                d = c.dma(c.act, Y[pr][:, tb * 512:(tb + 1) * 512], YS[:, y, :], ysem[y], e)
                yring.give(y, d)
                ytok[pr].append(d)
                stage["sg"] = e

        for r in range(34):
            if r < 32:
                scores(r)
            if 1 <= r < 33:
                turn(r - 1)
            if r >= 2:
                values(r - 2)
        bfree[pr % 2] = stage["bt"]
        qkfree = [stage["qk"], stage["qk"]]
        sgfree = stage["sg"]
    c.fence()


def recurrence(c, A, HT, w_in, b_in, Y, ytok):
    c.banks = Ring(4)
    OB = [4, 5, 6, 7]
    o = [c.R0]

    def al(n):
        if o[0] <= c.R1 < o[0] + n:
            o[0] = c.R2
        o[0] += n
        return o[0] - n

    n = 2048
    Q, FG, KK, BB, WW = (c.view(al(n), n) for _ in range(5))
    AR = [c.view(al(n), n) for _ in range(2)]
    K32 = [c.view(al(n), n)]
    K32.append(c.view(al(n), n))
    VH = c.view(al(n), 16, 128)
    O = c.view(al(n), n)
    SS = c.view(al(n), 16, 128)
    wr = WRing(c, al(3072), 3)
    AT = c.view(al(1024), 2, 512)
    KDT = c.view(al(1024), 2, 512)
    lbv = c.view(al(64), 64)
    dec = c.view(al(16), 16)
    vb = c.view(al(128), 128)
    reset = c.view(al(2048), 2048)
    tr0 = c.dma(c.sp, reset[:, :], A["k_reset"][0, :].partition_broadcast(128), c.dsem_of(2))
    tl = []
    for d, nm in enumerate(("lb_fwd_logits_3", "lb_bwd_logits_3")):
        l = c.col(nm)
        a = 32 * d
        m, e0, e1, lo = (lbv[:, a + 4 * i:a + 4 * i + 4] for i in range(4))
        t = c.tt(c.dve, m, l[:, 0:4], l[:, 4:8], ALU.max, c.t_par)
        t0 = c.tt(c.dve, e0, l[:, 0:4], m, ALU.subtract, t)
        t1 = c.tt(c.dve, e1, l[:, 4:8], m, ALU.subtract, t)
        t0 = c.act_(e0, e0, ACT.Exp, t0)
        t1 = c.act_(e1, e1, ACT.Exp, t1)
        t = c.tt(c.dve, m, e0, e1, ALU.add, t0, t1)
        t = c.recip(m, m, t)
        t = c.tt(c.dve, lo, e0, m, ALU.mult, t)
        t = c.ts(c.dve, lbv[:, a + 16:a + 20], lo, -1.0, 1.0, ALU.mult, ALU.add, t)
        tl.append(t)
    tz = [c.ms(c.pool, K32[0][:, :], 0.0), c.ms(c.pool, K32[1][:, :], 0.0)]
    c.act.wait(tl)
    gain = c.col("hg_norm_gain_3")
    vsem = c.dsem_of(0)
    v3 = lambda v, m: v[:, :].rearrange("p (n x) -> p n x", x=m)
    for hd in range(4):
        c.fence()
        tvb = c.dma(c.act, vb[:, :], A["b_in_3"][0, 3584 + hd * 128:3584 + hd * 128 + 128].partition_broadcast(128), vsem)
        s, tw = wr.load(w_in, 2048 + hd * 128)
        tq = []
        for tb in range(4):
            b, t = proj_cm(c, wr, s, tw, HT, tb, None)
            e = c.act_(Q[:, tb * 512:(tb + 1) * 512], c.P[b][:, :], ACT.Identity, t, bias=b_in[:, 16 + hd:17 + hd])
            c.banks.give(b, e)
            tq.append(e)
        wr.ring.give(s, t)
        s, tw = wr.load(w_in, 3584 + hd * 128)
        tv = []
        for g in range(4):
            b, bf = c.banks.take()
            for j in range(4):
                i = 4 * g + j
                for k in range(8):
                    t = c.mm(c.P[b][:, j * 128:(j + 1) * 128], HT[:, k, i * 128:(i + 1) * 128],
                             wr.W[:, s, k * 128:(k + 1) * 128], k == 0, k == 7, bf, tw, sig=(j == 3 and k == 7))
            e = c.tt(c.dve, VH[:, 4 * g:4 * g + 4, :], c.P[b][:, :].rearrange("p (a b) -> p a b", b=128),
                     vb[:, :].unsqueeze(1).to_broadcast([128, 4, 128]), ALU.add, t, tvb)
            c.banks.give(b, e)
            tv.append(e)
        wr.ring.give(s, t)
        for d in range(2):
            c.fence()
            fwd = d == 0
            s, tw = wr.load(w_in, 2560 + 512 * d + hd * 128)
            tf = []
            for tb in range(4):
                b, t = proj_cm(c, wr, s, tw, HT, tb, None)
                e = c.act_(FG[:, tb * 512:(tb + 1) * 512], c.P[b][:, :], ACT.Sigmoid, t,
                           bias=b_in[:, 20 + 4 * d + hd:21 + 4 * d + hd])
                c.banks.give(b, e)
                tf.append(e)
            wr.ring.give(s, t)
            a = 32 * d
            t = c.ts(c.dve, FG[:, :], FG[:, :], lbv[:, a + 16 + hd:a + 17 + hd], lbv[:, a + 12 + hd:a + 13 + hd],
                     ALU.mult, ALU.add, tf, tl)
            tk = c.ts(c.dve, KK[:, :], FG[:, :], -1.0, 1.0, ALU.mult, ALU.add, t)
            tg = c.act_(FG[:, :], FG[:, :], ACT.Ln, t, tk)
            tb_ = c.dve.do(lambda en: en.tensor_tensor_scan(BB[:, :], reset[:, :], FG[:, :], 0.0, ALU.mult, ALU.add), tg, tr0)
            if fwd:
                W, tw_ = BB, tb_
            else:
                W = WW
                tw_ = c.tt(c.dve, WW[:, :], FG[:, :], BB[:, :], ALU.subtract, tb_)
            op = ALU.subtract if fwd else ALU.add
            tdec = c.act_(dec[:, :], v3(BB, 128)[:, :, 127], ACT.Exp, tb_)
            zt = [c.mm(c.P[OB[g]][:, :], c.zb[:, 0:128], c.zb[:, :], True, False, c.t_const, sig=True)
                  for g in range(4)]
            afree = [None, None]
            for lv, B in enumerate((128, 64, 32)):
                h = B // 2
                ar = AR[lv % 2]
                qs, ks = (slice(h, B), slice(0, h)) if fwd else (slice(0, h), slice(h, B))
                nb = n // B
                ref = v3(BB, B)[:, :, h - 1:h].to_broadcast([128, nb, B])
                x = v3(ar, B)
                kd = x if B > 32 else v3(K32[d], 32)
                e = c.tt(c.dve, x, v3(W, B), ref, op, tw_, afree[lv % 2])
                e2 = c.act_(kd[:, :, ks], x[:, :, ks], ACT.Exp, e, scale=-1.0)
                e1 = c.act_(x[:, :, qs], x[:, :, qs], ACT.Exp, e)
                e2 = c.tt(c.pool, kd[:, :, ks], kd[:, :, ks], v3(KK, B)[:, :, ks], ALU.mult, e2, tk, tz)
                e1 = c.tt(c.dve, x[:, :, qs], x[:, :, qs], v3(Q, B)[:, :, qs], ALU.mult, e1, tq)
                for ci in range(16):
                    for bl in range(128 // B):
                        blk = ci * (128 // B) + bl
                        k0 = bl * B + ks.start if B > 32 else bl * B
                        m = h if B > 32 else 32
                        q0 = bl * B + qs.start
                        lhs = kd[:, blk, ks] if B > 32 else kd[:, blk, :]
                        t = c.mm(c.P[OB[ci // 4]][k0:k0 + m, (ci % 4) * 128 + q0:(ci % 4) * 128 + q0 + h], lhs,
                                 x[:, blk, qs], False, False, e1, e2, zt,
                                 sig=(ci == 15 and bl == 128 // B - 1))
                afree[lv % 2] = t
            toff = [c.mm(c.P[OB[g]][:, :], c.zb[:, 0:128], c.zb[:, :], False, True, sig=True) for g in range(4)]
            QD, KD = AR
            ref = v3(BB, 16)[:, :, 7:8].to_broadcast([128, n // 16, 16])
            e = c.tt(c.dve, v3(QD, 16), v3(W, 16), ref, op, afree)
            e2 = c.act_(KD[:, :], QD[:, :], ACT.Exp, e, afree, scale=-1.0)
            e1 = c.act_(QD[:, :], QD[:, :], ACT.Exp, e, e2)
            e2 = c.tt(c.pool, KD[:, :], KD[:, :], KK[:, :], ALU.mult, e2)
            e1 = c.tt(c.dve, QD[:, :], QD[:, :], Q[:, :], ALU.mult, e1)
            last = v3(BB, 128)[:, :, 127:128].to_broadcast([128, 16, 128])
            if fwd:
                e = c.tt(c.dve, v3(FG, 128), v3(W, 128), last, ALU.subtract, tb_)
                f2 = c.act_(FG[:, :], FG[:, :], ACT.Exp, e, scale=-1.0)
                f1 = c.act_(WW[:, :], W[:, :], ACT.Exp, tw_)
            else:
                f2 = c.act_(FG[:, :], W[:, :], ACT.Exp, tw_, scale=-1.0)
                e = c.tt(c.dve, v3(WW, 128), v3(W, 128), last, ALU.add, f2, c.dve.last())
                f1 = c.act_(WW[:, :], WW[:, :], ACT.Exp, e)
            f2 = c.tt(c.pool, FG[:, :], FG[:, :], KK[:, :], ALU.mult, f2)
            f1 = c.tt(c.dve, WW[:, :], WW[:, :], Q[:, :], ALU.mult, f1)
            order = list(range(16)) if fwd else list(range(15, -1, -1))
            aring, kring = Ring(2), Ring(2)
            ts_ = {}
            groups = [order[4 * i:4 * i + 4] for i in range(4)]
            pend = None

            def outputs(g, grp, ar_, ta):
                b, bf = c.banks.take()
                for ci in grp:
                    ps = slice((ci % 4) * 128, (ci % 4) * 128 + 128)
                    first = ci == order[0]
                    if not first:
                        c.mm(c.P[b][:, ps], SS[:, ci, :], WW[:, ci * 128:(ci + 1) * 128], True, False, bf, f1, ts_[ci])
                    t = c.mm(c.P[b][:, ps], VH[:, ci, :], AT[:, ar_, (ci % 4) * 128:(ci % 4) * 128 + 128], first, True,
                             bf, tv, ta, sig=(ci == grp[-1]))
                aring.give(ar_, t)
                sl = slice(g * 512, (g + 1) * 512)
                if fwd:
                    e = c.act_(O[:, sl], c.P[b][:, :], ACT.Copy, t)
                else:
                    e = c.tt(c.dve, O[:, sl], O[:, sl], c.P[b][:, :], ALU.add, t)
                c.banks.give(b, e)

            for grp in groups:
                g = grp[0] // 4
                b, bf = c.banks.take()
                for j in range(4):
                    sl = slice((4 * g + j) * 128, (4 * g + j + 1) * 128)
                    t = c.mm(c.P[b][:, j * 128:(j + 1) * 128], KD[:, sl], QD[:, sl], True, True, bf, e1, e2, sig=(j == 3))
                r, rf = aring.take()
                e = c.act_(AT[:, r, :], c.P[OB[g]][:, :], ACT.Copy, toff[g], rf)
                a_, m_, p_ = (AT[:, r, :].rearrange("p (a b) -> p a b", b=128),
                              c.pair[:, d, :].unsqueeze(1).to_broadcast([128, 4, 128]),
                              c.P[b][:, :].rearrange("p (a b) -> p a b", b=128))
                ta = c.dve.do(lambda en, a_=a_, m_=m_, p_=p_: en.copy_predicated(a_, m_, p_), e, t)
                c.banks.give(b, ta)
                b, bf = c.banks.take()
                for j, ci in enumerate(grp):
                    t = c.tr(c.P[b][:, j * 128:(j + 1) * 128], FG[:, ci * 128:(ci + 1) * 128], c.ident, bf, f2,
                             sig=(j == 3))
                kr_, kf = kring.take()
                tkd = c.act_(KDT[:, kr_, :], c.P[b][:, :], ACT.Copy, t, kf)
                c.banks.give(b, tkd)
                if pend is not None:
                    outputs(*pend)
                b, bf = c.banks.take()
                for j, ci in enumerate(grp):
                    t = c.mm(c.P[b][:, j * 128:(j + 1) * 128], KDT[:, kr_, j * 128:(j + 1) * 128], VH[:, ci, :], True,
                             True, bf, tkd, tv, sig=(j == 3))
                kring.give(kr_, t)
                e = None
                for j, ci in enumerate(grp):
                    if ci == order[15]:
                        continue
                    nx = ci + 1 if fwd else ci - 1
                    u = c.P[b][:, j * 128:(j + 1) * 128]
                    if ci == order[0]:
                        e = c.cp(c.dve, SS[:, nx, :], u, t)
                    else:
                        e = c.stt(SS[:, nx, :], SS[:, ci, :], dec[:, ci:ci + 1], u, ALU.mult, ALU.add, t, ts_[ci], tdec)
                    ts_[nx] = e
                c.banks.give(b, e)
                pend = (g, grp, r, ta)
            outputs(*pend)
        c.fence()
        s, tw = wr.load(w_in, 4096 + hd * 128)
        ytok[4 + hd] = []
        ysem = [c.dsem_of(4 + i) for i in range(2)]
        yf = [None, None]
        for tb in range(4):
            sl = slice(tb * 512, (tb + 1) * 512)
            sq, rs, sg, yo = AR[0][:, sl], AR[1][:, sl], WW[:, sl], O[:, sl]
            b, t = proj_cm(c, wr, s, tw, HT, tb, None)
            eg = c.act_(sg, c.P[b][:, :], ACT.Silu, t, bias=b_in[:, 32 + hd:33 + hd])
            c.banks.give(b, eg)
            e = c.act_(sq, yo, ACT.Square)
            b, bf = c.banks.take()
            t = c.mm(c.P[b][:, :], c.ones, sq, True, True, bf, e, sig=True)
            e = rsqrt(c, rs, c.P[b][:, :], 1.0 / 128, t)
            c.banks.give(b, e)
            e = c.stt(yo, yo, gain[:, hd:hd + 1], rs, ALU.mult, ALU.mult, e)
            e = c.tt(c.dve, yo, yo, sg, ALU.mult, e, eg)
            ytok[4 + hd].append(c.dma(c.act, Y[4 + hd][:, sl], yo, ysem[tb % 2], e))
        wr.ring.give(s, t)
    c.fence()


def program(nc, A, out, dbg=None, dbg_out=None):
    with ExitStack() as ctx:
        c = setup(nc, ctx)
        c.top = 0

        def take(n):
            c.top += n
            assert c.top <= 2300
            return c.top - n

        c.take = take
        c.wsems = [c.dsem() for _ in range(8)]
        pool_ = {}

        def dsem_of(i):
            if i not in pool_:
                pool_[i] = c.dsem()
            return pool_[i]

        c.dsem_of = dsem_of
        c.ident = c.view(take(128), 128)[:, :]
        c.ones = c.view(take(128), 128)[:, :]
        c.eps = c.view(take(1), 1)[:, :]
        c.gate = c.view(take(1024), 1024)[:, :]
        c.R0 = 2300
        c.R1 = c.R0 + 16384
        c.R2 = c.R1 + 16384
        c.t_const = [c.dma(c.sp, c.ident, A["k_ident"], c.dsem()),
                     c.ms(c.dve, c.ones, 1.0), c.ms(c.dve, c.eps, EPS), c.ms(c.dve, c.zb[:, :], 0.0),
                     c.dma(c.sp, c.pair[:, :, :], A["k_pair"], c.dsem())]
        for e in (c.pe, c.act, c.dve, c.pool):
            e.wait(c.t_const)
        X1 = nc.dram_tensor("x1_rows", (S_LEN, D), F32, kind="Internal").ap()
        X2 = nc.dram_tensor("x2_rows", (S_LEN, D), F32, kind="Internal").ap()
        Y = nc.dram_tensor("y_tiles", (16, 128, S_LEN), F32, kind="Internal").ap()
        GD = nc.dram_tensor("g_tiles", (24, 128, S_LEN), F32, kind="Internal").ap()

        def dump(ap, name):
            c.fence()
            if dbg_out is not None:
                c.dma(c.sp, dbg_out[name], ap, c.dsem())

        def finish():
            c.fence()
            block = ctx.enter_context(nc.Block())

            @block.sync
            def _(e):
                c.sp.emit(e)

            @block.scalar
            def _(e):
                c.act.emit(e)

            @block.vector
            def _(e):
                c.dve.emit(e)

            @block.gpsimd
            def _(e):
                c.pool.emit(e)

            @block.tensor
            def _(e):
                c.pe.emit(e)

        HT = block1(c, A, X1, Y, GD, dbg)
        if dbg in ("h", "b1"):
            dump(HT, "o0")
            if dbg == "b1":
                dump(X1, "o1")
            return finish()
        block2(c, A, HT, X1, X2, Y, GD, dbg, dump)
        if dbg is not None and dbg.startswith("b2"):
            return finish()
        block3(c, A, X2, out, Y, GD, dbg, dump)
        finish()


def constants():
    k = {"k_ident": np.eye(128, dtype=np.float32)}
    k.update(transform_constants())
    k.update(window_constants())
    return k


NAMES = ["x", "c", "w_ada", "b_ada", "norm_g", "w_in", "conv_w", "conv_b", "conv_ln_g", "conv_ln_b", "sg_ln_g",
         "sg_ln_b", "w_s", "b_s", "w_out", "final_g", "pre_norm_g_2", "w_in_2", "conv_w_2", "conv_b_2",
         "filt_w1_2", "filt_b1_2", "filt_w2_2", "filt_b2_2", "filt_w3_2", "filt_b3_2", "filt_freq_2",
         "filt_w_out_2", "hyena_d_2", "pool_w_2", "pool_scale_2", "norm_h_g_2", "norm_p_g_2", "w_out_2",
         "post_norm_g_2", "w_in_3", "b_in_3", "rpb_3", "lb_fwd_logits_3", "lb_bwd_logits_3", "hg_norm_gain_3",
         "w_out_3", "b_out_3", "ln_gain_3", "ln_bias_3"]


def kernel(**inputs):
    import concourse.bacc as bacc
    from concourse.bass_utils import run_bass_kernel_spmd

    nc = bacc.Bacc("TRN2", target_bir_lowering=False, num_devices=1)
    arrays, A = {}, {}
    for name in NAMES:
        arrays[f"in_{name}"] = np.ascontiguousarray(inputs[name])
    for name, a in constants().items():
        arrays[f"in_{name}"] = a
    for name, a in arrays.items():
        A[name[3:]] = nc.dram_tensor(name, a.shape, mybir.dt.from_np(a.dtype), kind="ExternalInput").ap()
    out = nc.dram_tensor("out_rows", (S_LEN, D), F32, kind="ExternalOutput").ap()
    program(nc, A, out)
    r = run_bass_kernel_spmd(nc, [arrays], core_ids=[0])
    return r.results[0]["out_rows"].reshape(1, S_LEN, D)
```

```python
import math
from contextlib import ExitStack

import numpy as np

import concourse.bass as bass
from concourse import mybir

F32 = mybir.dt.float32
F32R = mybir.dt.float32r
ACT = mybir.ActivationFunctionType
ALU = mybir.AluOpType
AXX = mybir.AxisListType.X

S_LEN = 2048
D = 1024
NT = 16
EPS = 1e-6


class Engine:

    def __init__(self, sem):
        self.sem, self.n, self.queue, self.seen = sem, 0, [], {}

    def wait(self, *after):
        for t in after:
            if t is None:
                continue
            if isinstance(t, list):
                self.wait(*t)
                continue
            sem, v = t
            if self.seen.get(sem.name, 0) < v:
                self.seen[sem.name] = v
                self.queue.append((0, sem, v))

    def do(self, f, *after, sig=True):
        self.wait(*after)
        if sig:
            self.n += 1
            self.queue.append((1, f, self.sem))
            return (self.sem, self.n)
        self.queue.append((1, f, None))
        return None

    def last(self):
        return (self.sem, self.n)

    def emit(self, eng):
        for kind, a, b in self.queue:
            if kind == 0:
                eng.wait_ge(a, b)
            elif kind == 1:
                i = a(eng)
                if b is not None:
                    i.then_inc(b, 1)
            else:
                a(eng).then_inc(b, 16)


class DmaSem:

    def __init__(self, sem):
        self.sem, self.n = sem, 0

    def last(self):
        return (self.sem, 16 * self.n)


class Ring:

    def __init__(self, n):
        self.n, self.at, self.free = n, 0, [None] * n

    def take(self):
        i = self.at % self.n
        self.at += 1
        f = self.free[i]
        return i, f

    def give(self, i, *tokens):
        self.free[i] = list(tokens)


class Ctx:
    pass


def setup(nc, ctx):
    c = Ctx()
    c.nc = nc
    c.nsem = 0

    def sem(name):
        return ctx.enter_context(nc.semaphore(name))

    def dsem():
        c.nsem += 1
        d = DmaSem(sem(f"d{c.nsem}"))
        c.dsems.append(d)
        return d

    c.dsems = []
    c.dsem = dsem
    c.pe, c.act, c.dve, c.pool, c.sp = (Engine(sem(n)) for n in ("s_pe", "s_act", "s_dve", "s_pool", "s_sp"))
    c.NF = 52688
    c.pair = ctx.enter_context(nc.sbuf_tensor("pair", [128, 2, 128], mybir.dt.int32))
    c.zb = ctx.enter_context(nc.sbuf_tensor("zeros", [128, 512], mybir.dt.bfloat16))
    base = (int(nc.sbuf_base) + 31) // 32 * 32
    c.named = {}
    c.P = [ctx.enter_context(nc.psum_tensor(f"ps{i}", [128, 512], F32)) for i in range(8)]
    c.banks = Ring(8)

    def dma(eng, out, in_, ds, *after, slow=False):
        prev = ds.last() if ds.n else None
        eng.wait(*after)
        eng.wait(prev)
        ds.n += 1
        eng.queue.append((2, lambda e: e.dma_start(out, in_, allow_slow_non_contiguous=slow), ds.sem))
        return ds.last()

    def mm(out, lhsT, rhs, start, stop, *after, sig=False):
        return c.pe.do(lambda e: e.matmul(out, lhsT, rhs, start=start, stop=stop), *after, sig=sig)

    def tr(out, in_, ident, *after, sig=False):
        return c.pe.do(lambda e: e.transpose(out, in_, ident), *after, sig=sig)

    def act(out, in_, func, *after, scale=None, bias=None, accum=None):
        kw = {}
        if scale is not None:
            kw["scale"] = scale
        if bias is not None:
            kw["bias"] = bias
        if accum is not None:
            kw["accum_out"] = accum
        return c.act.do(lambda e: e.activation(out, in_, func, **kw), *after)

    def tt(eng, out, a, b, op, *after):
        return eng.do(lambda e: e.tensor_tensor(out, a, b, op), *after)

    def ts(eng, out, a, s1, s2, op0, op1, *after):
        if op1 is None:
            return eng.do(lambda e: e.tensor_scalar(out, a, s1, None, op0), *after)
        return eng.do(lambda e: e.tensor_scalar(out, a, s1, s2, op0, op1), *after)

    def stt(out, a, s, b, op0, op1, *after):
        return c.dve.do(lambda e: e.scalar_tensor_tensor(out, a, s, b, op0, op1), *after)

    def cp(eng, out, a, *after):
        return eng.do(lambda e: e.tensor_copy(out, a), *after)

    def ms(eng, out, v, *after):
        return eng.do(lambda e: e.memset(out, v), *after)

    def recip(out, a, *after):
        return c.dve.do(lambda e: e.reciprocal(out, a), *after)

    c.dma, c.mm, c.tr, c.act_, c.tt, c.ts, c.stt, c.cp, c.ms, c.recip = dma, mm, tr, act, tt, ts, stt, cp, ms, recip

    def view(off, *dims, r=False):
        n = 1
        for d in dims:
            n *= d
        assert off + n <= c.NF, (off, dims)
        key = (off, n, r)
        if key not in c.named:
            c.named[key] = nc.alloc_sbuf_tensor_at(f"v{off}_{n}{'r' if r else ''}", [128, n], F32R if r else F32,
                                                   offset=base + 4 * off, align_bytes=4)
        v = c.named[key][:, :]
        if len(dims) == 2:
            return v.rearrange("p (a b) -> p a b", b=dims[1])
        if len(dims) == 3:
            return v.rearrange("p (a b c) -> p a b c", b=dims[1], c=dims[2])
        return v

    c.view = view

    def fence():
        toks = [e.last() for e in (c.pe, c.act, c.dve, c.pool, c.sp) if e.n] + [d.last() for d in c.dsems if d.n]
        for e in (c.pe, c.act, c.dve, c.pool, c.sp):
            e.wait(*toks)

    c.fence = fence
    return c


def rsqrt(c, out, in_, scale, *after):
    t = c.act_(out, in_, ACT.Ln, *after, scale=scale, bias=c.eps[:in_.shape[0], :])
    return c.act_(out, out, ACT.Exp, t, scale=-0.5)


class Split:

    def __init__(self, c, off, n, tiles):
        self.c, self.tiles, self.n = c, tiles, n
        self.raw = c.view(off, 2, 1024)
        self.H = c.view(off + 2048, n, 2048, r=True)
        self.rawring, self.ring = Ring(2), Ring(n)
        self.sems = [c.wsems[i] for i in range(2)]
        self.loaded, self.ready, self.nl, self.ns, self.ng = [], [], 0, 0, 0

    def load(self):
        if self.nl >= len(self.tiles):
            return
        dram, col = self.tiles[self.nl]
        self.nl += 1
        i, free = self.rawring.take()
        dst = self.raw[:, i, :].rearrange("p (k n) -> p k n", k=8)
        src = dram[:, col:col + 128].rearrange("(k p) n -> p k n", p=128)
        self.loaded.append((i, self.c.dma(self.c.sp, dst, src, self.sems[i], free)))

    def split(self):
        if self.ns >= len(self.tiles):
            return
        if self.ns >= self.nl:
            self.load()
        c = self.c
        i, t = self.loaded[self.ns]
        self.ns += 1
        s, free = self.ring.take()
        hi, lo = self.H[:, s, 0:1024], self.H[:, s, 1024:2048]
        e = c.act_(hi, self.raw[:, i, :], ACT.Copy, t, free)
        e = c.tt(c.pool, lo, self.raw[:, i, :], hi, ALU.subtract, e, t)
        self.rawring.give(i, e)
        self.ready.append((s, e))

    def get(self, ahead=1):
        n = self.ng
        self.ng += 1
        while self.ns <= n + ahead and self.ns < len(self.tiles):
            self.split()
            self.load()
        return self.ready[n]


def ht_views(c):
    c.HH = [c.view(c.R0 + 8192 * tb, 8, 512, r=True) for tb in range(4)]
    c.HL = [c.view(c.R0 + 8192 * tb + 4096, 8, 512, r=True) for tb in range(4)]


def proj(c, W, slot, wtok, tb):
    b, free = c.banks.take()
    for k in range(8):
        wh, wl = W.H[:, slot, k * 128:(k + 1) * 128], W.H[:, slot, 1024 + k * 128:1024 + (k + 1) * 128]
        c.mm(c.P[b][:, :], wh, c.HH[tb][:, k, :], k == 0, False, free, wtok, c.ht_tok[tb])
        c.mm(c.P[b][:, :], wh, c.HL[tb][:, k, :], False, False)
        t = c.mm(c.P[b][:, :], wl, c.HH[tb][:, k, :], False, k == 7, sig=(k == 7))
    return b, t


def proj_rows(c, W, slots, toks, i, b, at, free):
    n = len(slots)
    s0 = slots[0]
    tb, j = i // 4, (i % 4) * 128
    out = c.P[b][:, at:at + 128 * n]
    for k in range(8):
        hh, hl = c.HH[tb][:, k, j:j + 128], c.HL[tb][:, k, j:j + 128]
        wh = W.H[:, s0:s0 + n, k * 128:(k + 1) * 128]
        wl = W.H[:, s0:s0 + n, 1024 + k * 128:1024 + (k + 1) * 128]
        c.mm(out, hh, wh, k == 0, False, free, toks, c.ht_tok[tb])
        c.mm(out, hh, wl, False, False)
        t = c.mm(out, hl, wh, False, k == 7, sig=(k == 7))
    return t


def make_ht(c, rows, rstd, scale, bias, tmp, *after, mid=None, midtok=None):
    c.ht_tok = [[] for _ in range(4)]
    tring = Ring(4)
    done = []
    for tb in range(4):
        if mid is not None:
            mid(tb)
        xs = []
        for j in range(4):
            v, t = rows(4 * tb + j, done)
            if rstd is not None:
                i = 4 * tb + j
                t = c.ts(c.dve, v, v, rstd[:, i:i + 1], None, ALU.mult, None, t, *after)
            xs.append((v, t))
        for k in range(8):
            b, free = c.banks.take()
            for j in range(4):
                t = c.tr(c.P[b][:, j * 128:(j + 1) * 128], xs[j][0][:, k * 128:(k + 1) * 128], c.ident, free, xs[j][1],
                         sig=(j == 3))
            hi, lo = c.HH[tb][:, k, :], c.HL[tb][:, k, :]
            if bias is not None:
                r, rf = tring.take()
                e0 = c.ts(c.dve, tmp[:, r, :], c.P[b][:, :], scale[:, k:k + 1], bias[:, k:k + 1], ALU.mult, ALU.add, t,
                          rf, *after)
                c.banks.give(b, e0)
                e = c.act_(hi, tmp[:, r, :], ACT.Copy, e0, midtok, *after)
                e = c.tt(c.pool if k % 2 else c.dve, lo, tmp[:, r, :], hi, ALU.subtract, e, e0)
                tring.give(r, e)
            elif scale is not None:
                e = c.act_(hi, c.P[b][:, :], ACT.Copy, t, *after, scale=scale[:, k:k + 1])
                e = c.stt(lo, c.P[b][:, :], scale[:, k:k + 1], hi, ALU.mult, ALU.subtract, e, t)
                c.banks.give(b, e)
            else:
                e = c.act_(hi, c.P[b][:, :], ACT.Copy, t, *after)
                e = c.tt(c.dve, lo, c.P[b][:, :], hi, ALU.subtract, e, t)
                c.banks.give(b, e)
            c.ht_tok[tb].append(e)
        done.append(t)
    return done


def rows_from(c, X, xtok, off, sems):
    XV = c.view(off, 8, 1024)

    def rows(i, done):
        free = done[i // 4 - 2] if i >= 8 else None
        t = c.dma(c.act if i % 2 else c.sp, XV[:, i % 8, :], X[i * 128:(i + 1) * 128, :], sems[i % 8], free, xtok[i])
        return XV[:, i % 8, :], t

    return rows


class OutWeights:

    def __init__(self, c, dram, off, KT, raw, sems):
        self.c, self.dram, self.raw, self.sems = c, dram, raw, sems
        self.WO = c.view(off, KT, 2048, r=True)
        self.ring, self.at, self.toks = Ring(len(sems)), {}, []

    def load(self, k, *after):
        r, rf = self.ring.take()
        self.at[k] = (r, self.c.dma(self.c.sp, self.raw[:, r, :], self.dram[k * 128:(k + 1) * 128, :], self.sems[r], rf,
                                    *after), after)

    def split(self, k):
        c, WO = self.c, self.WO
        r, t, after = self.at.pop(k)
        e = c.act_(WO[:, k, 0:1024], self.raw[:, r, :], ACT.Copy, t, *after)
        e = c.tt(c.pool if k % 2 else c.dve, WO[:, k, 1024:2048], self.raw[:, r, :], WO[:, k, 0:1024], ALU.subtract, e)
        self.ring.give(r, e)
        self.toks.append(e)


def load_wo(c, dram, off, KT, raw, sems):
    w = OutWeights(c, dram, off, KT, raw, sems)
    for k in range(KT):
        w.load(k)
        w.split(k)
    return w.WO, w.toks


def out_tile(c, KT, yh, yl, ytoks, WO, wtoks, mid=None):
    bb = []
    for h in range(2):
        b, free = c.banks.take()
        for k in range(KT):
            wh, wl = WO[:, k, h * 512:(h + 1) * 512], WO[:, k, 1024 + h * 512:1024 + (h + 1) * 512]
            c.mm(c.P[b][:, :], yh(k), wh, k == 0, False, free, ytoks(k), wtoks[k])
            c.mm(c.P[b][:, :], yh(k), wl, False, False)
            t = c.mm(c.P[b][:, :], yl(k), wh, False, k == KT - 1, sig=(k == KT - 1))
        bb.append(b)
        if h == 0 and mid is not None:
            mid()
    return bb, t


PROWS1 = [("c", 8), ("norm_g", 8), ("conv_b", 8), ("conv_ln_g", 8), ("conv_ln_b", 8), ("pre_norm_g_2", 8),
          ("conv_b_2", 12), ("pool_scale_2", 4), ("norm_h_g_2", 4), ("norm_p_g_2", 4), ("conv_w_2", 36)]
PROWS2 = [("b_in_3", 36), ("hg_norm_gain_3", 4), ("lb_fwd_logits_3", 8), ("lb_bwd_logits_3", 8),
          ("b_ada", 24), ("sg_ln_g", 8), ("sg_ln_b", 8)]


def parameters(c, A, off):
    raw = c.view(off, 4, 128)
    c.cols = {}
    toks = [c.ms(c.dve, raw[:, :, :], 0.0)]
    tk = []

    def rows(tile, at, ap):
        n = ap.shape[0]
        tk.append(c.dma(c.act, raw[at:at + n, tile, :], ap, c.dsem(), *toks))

    at = 0
    for name, n in PROWS1:
        a = A[name]
        while len(a.shape) > 1:
            letters = " ".join("abcd"[:len(a.shape)])
            a = a.rearrange(f"{letters} -> ({letters})")
        rows(0, at, a.rearrange("(r p) -> r p", p=128))
        c.cols[name] = (0, at, n)
        at += n
    at = 0
    for name, n in PROWS2:
        a = A[name]
        while len(a.shape) > 1:
            letters = " ".join("abcd"[:len(a.shape)])
            a = a.rearrange(f"{letters} -> ({letters})")
        rows(1, at, a.rearrange("(r p) -> r p", p=128))
        c.cols[name] = (1, at, n)
        at += n
    cw = A["conv_w"].rearrange("l w o (t p) -> (l w o t) p", p=128)
    rows(2, 0, cw[0:124, :])
    rows(3, 0, cw[124:248, :])
    b, free = c.banks.take()
    for t in range(4):
        last = c.tr(c.P[b][:, t * 128:(t + 1) * 128], raw[:, t, :], c.ident, free, tk, c.t_const, sig=(t == 3))
    done = c.cp(c.dve, c.pcol[:, :, :].rearrange("p a b -> p (a b)"), c.P[b][:, :], last)
    c.banks.give(b, done)
    c.t_par = done

    def col(name):
        t, a, n = c.cols[name]
        return c.pcol[:, t, a:a + n]

    def convw(j, ch):
        r = j * 8 + ch
        return c.pcol[:, 2 + r // 124, r % 124:r % 124 + 1]

    c.col, c.convw = col, convw


def rows_of(A, name):
    a = A[name]
    if len(a.shape) == 2:
        return a[0, :]
    return a


def block1(c, A, X1, Y, GD):
    R0, R2 = c.R0, c.R2
    w_in, w_ada = A["w_in"][0], A["w_ada"][0]
    x = A["x"][0]
    ss, rstd = c.view(c.take(16), 16), c.view(c.take(16), 16)
    ms, cs = c.view(c.take(16), 16), c.view(c.take(8), 8)
    rowv = [c.view(R0 + 3 * 8192 + i * 1024, 1024) for i in range(8)] + \
           [c.view(R2 + 10240 + i * 1024, 1024) for i in range(8)]
    wa = c.view(R0, 6, 8, 512)
    parameters(c, A, R2 + 2048 + 3 * 2048)
    xt = [c.dma(c.act, rowv[i], x[i * 128:(i + 1) * 128, :], c.dsem()) for i in range(16)]
    tw = [c.dma(c.sp, wa[:, n, :, :], w_ada[:, n * 512:(n + 1) * 512].rearrange("(k p) n -> p k n", p=128), c.dsem())
          for n in range(6)]
    W = Split(c, R2, 4, [(w_in, col * 128) for ch in range(8) for col in (8 + ch, ch, 16 + ch, 40 + ch, 24 + ch)] +
              [(w_in, 4096 + g * 128) for g in range(8)])
    W.load()
    W.load()
    tcs = c.act_(cs, c.col("c"), ACT.Silu, c.t_par)
    junk = c.view(R2 + 2048 + 2 * 2048, 1024)
    tj = None
    for i in range(16):
        tj = c.act_(junk, rowv[i], ACT.Square, xt[i], tj, accum=ss[:, i:i + 1])
    trs = rsqrt(c, rstd, ss, 1.0 / D, tj)
    xs = [c.ts(c.dve, rowv[i], rowv[i], rstd[:, i:i + 1], None, ALU.mult, None, trs) for i in range(16)]
    srow = c.view(R2 + 2048, 2048)
    ba = c.col("b_ada")
    sbank, sf = c.banks.take()
    for n in range(4):
        b, bf = c.banks.take()
        for k in range(8):
            t = c.mm(c.P[b][0:1, :], cs[:, k:k + 1], wa[:, n, k, :], k == 0, k == 7, bf, tcs, tw[n], sig=(k == 7))
        e = c.act_(srow[0:1, n * 512:(n + 1) * 512], c.P[b][0:1, :], ACT.Copy, t)
        c.banks.give(b, e)
        for q in range(4):
            tm = c.mm(c.P[sbank][:, 4 * n + q:4 * n + q + 1], srow[0:1, (4 * n + q) * 128:(4 * n + q + 1) * 128],
                      c.ones[0:1, 0:1], True, True, sf, e, c.t_const, sig=True)
    t0 = c.tt(c.dve, ms, c.P[sbank][:, 0:16], ba[:, 0:16], ALU.add, tm, c.t_par)
    c.banks.give(sbank, t0)
    t0 = c.stt(ms[:, 8:16], ms[:, 8:16], 1.0, c.col("norm_g"), ALU.add, ALU.mult, t0)
    W.ring.give(0, tm)
    tgm = []
    grow, brow = c.view(R2 + 2048 + 2048, 1024), c.view(R2 + 2048 + 2048 + 1024, 1024)
    tbr = c.dma(c.sp, brow[0:1, :], A["b_ada"][0:1, 2048:3072], c.dsem())
    GR = c.nc.dram_tensor("gate_row", (1024,), F32, kind="Internal").ap()

    def gate_row(tb):
        if tb != 2:
            return
        for n in range(2):
            b, bf = c.banks.take()
            for k in range(8):
                t = c.mm(c.P[b][0:1, :], cs[:, k:k + 1], wa[:, 4 + n, k, :], k == 0, k == 7, bf, tcs, tw[4 + n],
                         sig=(k == 7))
            e = c.tt(c.dve, grow[0:1, n * 512:(n + 1) * 512], c.P[b][0:1, :], brow[0:1, n * 512:(n + 1) * 512],
                     ALU.add, t, tbr)
            c.banks.give(b, e)
            tgm.append(t)
        tgm.append(c.dma(c.sp, GR.rearrange("(o n) -> o n", o=1), grow[0:1, :], c.dsem(), e))

    tmp = c.view(R2 + 2048 + 2 * 2048, 4, 512)
    make_ht(c, lambda i, done: (rowv[i], xs[i]), None, ms[:, 8:16], ms[:, 0:8], tmp, t0, tj, mid=gate_row, midtok=tgm)
    tht = c.ht_tok[3][-8:]
    tgr = tgm[-1]
    W.ring.give(1, tgr)
    W.ring.give(2, tht, tj)
    W.ring.give(3, c.t_par)

    o = R2 + 10240
    AP = [c.view(o, 2080), c.view(o + 2080, 2080)]
    CV = c.view(o + 4160, 2048)
    sgt = c.view(o + 6208, 2, 512)
    ost = c.view(o + 7232, 2, 512)
    sring, oring = Ring(2), Ring(2)
    oring.give(0, tht)
    oring.give(1, tht)
    osem, cvsem = [c.dsem_of(i) for i in range(2)], [c.dsem_of(2 + i) for i in range(2)]
    pads = [c.ms(c.pool, AP[q][:, a:b], 0.0, tht) for q in range(2) for a, b in ((0, 15), (2063, 2080))]
    apfree = [None, None]
    cvfree = [None, None]
    cvtok, gtok, utok, vtok = [None] * 8, {}, {}, {}
    cb = c.col("conv_b")
    jobs = []

    def conv(ch, parts):
        a = AP[ch % 2]
        dd = []
        for h in range(2):
            v = CV[:, h * 1024:(h + 1) * 1024]
            t = c.ts(c.dve, v, a[:, h * 1024:(h + 1) * 1024], c.convw(0, ch), cb[:, ch:ch + 1], ALU.mult, ALU.add,
                     parts, cvfree[h])
            yield
            for j in range(1, 31):
                t = c.stt(v, a[:, h * 1024 + j:(h + 1) * 1024 + j], c.convw(j, ch), v, ALU.mult, ALU.add, t)
                yield
            cvfree[h] = c.dma(c.sp, Y[ch][:, h * 1024:(h + 1) * 1024], v, cvsem[h], t)
            dd.append(cvfree[h])
        apfree[ch % 2] = t
        cvtok[ch] = dd

    def background(n):
        while jobs and n:
            if next(jobs[0], 0) == 0:
                jobs.pop(0)
            n -= 1

    for ch in range(8):
        sg, tg_ = W.get()
        sa, ta_ = W.get()
        a = AP[ch % 2]
        parts = []
        for tb in range(4):
            b, t = proj(c, W, sg, tg_, tb)
            r, rf = sring.take()
            e = c.act_(sgt[:, r, :], c.P[b][:, :], ACT.Sigmoid, t, rf, tht)
            c.banks.give(b, e)
            background(4)
            b, t = proj(c, W, sa, ta_, tb)
            e = c.tt(c.dve, a[:, 15 + tb * 512:15 + (tb + 1) * 512], c.P[b][:, :], sgt[:, r, :], ALU.mult,
                     t, e, apfree[ch % 2], pads)
            c.banks.give(b, e)
            sring.give(r, e)
            parts.append(e)
            background(4)
        W.ring.give(sg, t)
        W.ring.give(sa, t)
        while jobs:
            background(1)
        jobs.append(conv(ch, parts))
        s, tw_ = W.get()
        for tb in range(4):
            b, t = proj(c, W, s, tw_, tb)
            r, rf = oring.take()
            e = c.act_(ost[:, r, :], c.P[b][:, :], ACT.Silu, t, rf)
            c.banks.give(b, e)
            gtok[(ch, tb)] = c.dma(c.act, GD[ch][:, tb * 512:(tb + 1) * 512], ost[:, r, :], osem[r], e)
            oring.give(r, gtok[(ch, tb)])
            background(4)
        W.ring.give(s, t)
        sg, tg_ = W.get()
        su, tu_ = W.get()
        for tb in range(4):
            b, t = proj(c, W, sg, tg_, tb)
            r, rf = sring.take()
            e = c.act_(sgt[:, r, :], c.P[b][:, :], ACT.Silu, t, rf)
            c.banks.give(b, e)
            background(2)
            b, t = proj(c, W, su, tu_, tb)
            r2, rf2 = oring.take()
            e = c.tt(c.dve, ost[:, r2, :], c.P[b][:, :], sgt[:, r, :], ALU.mult, t, e, rf2)
            c.banks.give(b, e)
            sring.give(r, e)
            utok[(ch, tb)] = c.dma(c.act, Y[8 + ch][:, tb * 512:(tb + 1) * 512], ost[:, r2, :], osem[r2], e)
            oring.give(r2, utok[(ch, tb)])
            background(2)
        W.ring.give(sg, t)
        W.ring.give(su, t)
    VR = c.nc.dram_tensor("v_rows", (S_LEN, D), F32, kind="Internal").ap()
    bst = c.view(c.take(384), 16, 24)
    mv, rs = c.view(c.take(32), 16, 2), c.view(c.take(16), 16)
    OW = OutWeights(c, A["w_out"][0], R0, 16, c.view(R2 + 12288, 4, 1024), [c.dsem_of(4 + i) for i in range(4)])
    for g in range(4):
        s0, t0_ = W.get()
        s1, t1_ = W.get(2)
        for i in range(0, 16, 2):
            b, bf = c.banks.take()
            for h in range(2):
                t = proj_rows(c, W, [s0, s1], [t0_, t1_], i + h, b, 256 * h, bf)
            r, rf = oring.take()
            e = c.act_(ost[:, r, :], c.P[b][:, :], ACT.Copy, t, rf)
            for h in range(2):
                o_, a_ = bst[:, i + h, 6 * g:6 * g + 6], ost[:, r, h * 256:(h + 1) * 256]
                e2 = c.dve.do(lambda en, o_=o_, a_=a_: en.bn_stats(o_, a_), e)
            c.banks.give(b, e)
            d = c.dma(c.act, VR[i * 128:(i + 2) * 128, g * 256:(g + 1) * 256].rearrange("(i p) n -> p i n", p=128),
                      ost[:, r, :].rearrange("p (i n) -> p i n", n=256), osem[r], e)
            oring.give(r, d, e2)
            vtok[(g, i)] = d
            background(6)
            if g == 3 and i % 4 == 0 and i:
                for k in range(i - 4, i):
                    OW.split(k)
            if g == 3 and i % 4 == 2:
                for k in range(i - 2, i + 2):
                    OW.load(k, t, apfree, cvtok)
        W.ring.give(s0, t)
        W.ring.give(s1, t)
    while jobs:
        background(1)

    o = R2
    LD = c.view(o, 4, 1024)
    fg, gate, BT, wsT = c.view(o + 4096, 1024), c.view(o + 5120, 1024), c.view(o + 6144, 8, 128), \
        c.view(o + 7168, 8, 128)
    X, T = c.view(o + 16384, 1024), c.view(o + 17408, 1024)
    WO, two = OW.WO, OW.toks
    first = [c.pe.last(), c.dve.last(), c.act.last(), c.pool.last(), [vtok[(3, i)] for i in range(12, 16, 2)]]
    for i in range(16):
        o_, a_ = mv[:, i, :], bst[:, i, :]
        tmv = c.dve.do(lambda e, o_=o_, a_=a_: e.bn_aggr(o_, a_), first)
    trs = rsqrt(c, rs, mv[:, :, 1:2].rearrange("p a b -> p (a b)"), 1.0, tmv)
    tfg = c.dma(c.act, fg, A["final_g"].partition_broadcast(128), c.dsem_of(8), first)
    tgt = c.dma(c.act, gate, GR.partition_broadcast(128), c.dsem_of(9), first, tgr)
    tbs = c.dma(c.act, BT, A["b_s"][0].partition_broadcast(128), c.dsem_of(10), first)
    wsr = X.rearrange("p (a b) -> p a b", b=128)
    tws = c.dma(c.act, wsr, A["w_s"][0].rearrange("h p q -> p h q"), c.dsem_of(11), first)
    twt = []
    for g in range(2):
        b, bf = c.banks.take()
        for j in range(4):
            txf = c.tr(c.P[b][:, j * 128:(j + 1) * 128], wsr[:, 4 * g + j, :], c.ident, bf, tws, sig=(j == 3))
        e = c.act_(wsT[:, 4 * g:4 * g + 4, :].rearrange("p a b -> p (a b)"), c.P[b][:, :], ACT.Copy, txf)
        c.banks.give(b, e)
        twt.append(e)
    lgc, lbc = c.col("sg_ln_g"), c.col("sg_ln_b")
    tbt = []
    for g in range(2):
        b, bf = c.banks.take()
        t = c.mm(c.P[b][:, :], c.ones, wsT[:, 4 * g:4 * g + 4, :], True, True, bf, twt[g], sig=True)
        for j in range(4):
            h = 4 * g + j
            e = c.stt(BT[:, h, :], c.P[b][:, j * 128:(j + 1) * 128], lbc[:, h:h + 1], BT[:, h, :], ALU.mult, ALU.add,
                      t, tbs)
            tbt.append(e)
        c.banks.give(b, e)
    glg, glb = c.col("conv_ln_g"), c.col("conv_ln_b")
    ldsem = [c.dsem_of(12 + i) for i in range(4)]
    xsem, x1sem = c.dsem_of(16), c.dsem_of(17)
    ldfree = [first] * 4
    yfree = [first, [first, two]]
    x1tok, st = {}, {}
    s2 = c.view(c.take(32), 2, 16)
    loads = {}

    def load(i):
        sl = slice(i * 128, (i + 1) * 128)
        cm = "k p t -> p k t"
        tb = i // 4
        srcs = [(Y[0:8, :, sl].rearrange(cm), cvtok), (GD[0:8, :, sl].rearrange(cm), [gtok[(k, tb)] for k in range(8)]),
                (VR[sl, :], [vtok[(g, i - i % 2)] for g in range(4)]),
                (Y[8:16, :, sl].rearrange(cm), [utok[(k, tb)] for k in range(8)])]
        tl = []
        for q, (src, dep) in enumerate(srcs):
            dst = LD[:, q, :] if q == 2 else LD[:, q, :].rearrange("p (k t) -> p k t", k=8)
            tl.append(c.dma(c.sp, dst, src, ldsem[q], ldfree[q], dep))
        loads[i] = tl

    def prep_a(i):
        tcv, tga, tv, tug = loads[i]
        q = i % 2
        o = R2 + 8192 + 4096 * q
        cv = LD[:, 0, :]
        sq, red = c.view(o + 1024, 1024), c.view(o + 3072, 256)
        e = c.act_(sq, cv, ACT.Square, tcv, yfree[q])
        e1 = c.dve.do(lambda en: en.tensor_reduce(red[:, 0:128], cv.rearrange("p (k t) -> p t k", k=8), AXX, ALU.add),
                      tcv, yfree[q])
        e2 = c.dve.do(lambda en: en.tensor_reduce(red[:, 128:256], sq.rearrange("p (k t) -> p t k", k=8), AXX,
                                                  ALU.add), e)
        v = LD[:, 2, :]
        e3 = c.ts(c.dve, v, v, mv[:, i, 0:1], rs[:, i:i + 1], ALU.subtract, ALU.mult, tv, trs)
        st[i] = (e2, e3)

    def prep_pe(i):
        e2, e3 = st[i]
        q = i % 2
        red = c.view(R2 + 8192 + 4096 * q + 3072, 256)
        b, bf = c.banks.take()
        t = c.mm(c.P[b][:, 0:256], c.ones, red, True, True, bf, e2, sig=True)
        bb = []
        for g in range(2):
            b2, bf = c.banks.take()
            for j in range(4):
                h = 4 * g + j
                t2 = c.mm(c.P[b2][:, j * 128:(j + 1) * 128], LD[:, 2, h * 128:(h + 1) * 128], wsT[:, h, :], True, True,
                          bf, e3, twt, sig=(j == 3))
            bb.append(b2)
        st[i] = (b, t, bb, t2)

    def prep_b(i):
        b, t, bb, t2 = st[i]
        tcv, tga, tv, tug = loads[i]
        q = i % 2
        o = R2 + 8192 + 4096 * q
        mu, rsd = c.view(o + 3328, 128), c.view(o + 3456, 128)
        yh, yl = c.view(o, 2, 1024, r=True), c.view(o + 2048, 2, 1024, r=True)
        cv, ga, vb, ug = (LD[:, k, :] for k in range(4))
        v3 = lambda a: a.rearrange("p (k t) -> p k t", k=8)
        e1 = c.ts(c.dve, mu, c.P[b][:, 0:128], 1.0 / D, None, ALU.mult, None, t)
        e2 = c.act_(rsd, mu, ACT.Square, e1)
        e3 = c.stt(rsd, c.P[b][:, 128:256], 1.0 / D, rsd, ALU.mult, ALU.subtract, e2, t)
        c.banks.give(b, e3)
        e4 = c.ts(c.dve, rsd, rsd, 0.0, None, ALU.max, None, e3)
        e5 = rsqrt(c, rsd, rsd, 1.0, e4)
        a = c.tt(c.dve, v3(cv), v3(cv), mu.unsqueeze(1).to_broadcast([128, 8, 128]), ALU.subtract, e1, tcv)
        for h in range(8):
            g, j = h // 4, h % 4
            s = c.stt(vb[:, h * 128:(h + 1) * 128], c.P[bb[g]][:, j * 128:(j + 1) * 128], lgc[:, h:h + 1], BT[:, h, :],
                      ALU.mult, ALU.add, t2, tbt)
            if j == 3:
                c.banks.give(bb[g], s)
        a = c.tt(c.dve, v3(cv), v3(cv), rsd.unsqueeze(1).to_broadcast([128, 8, 128]), ALU.mult, a, e5)
        u = c.tt(c.pool, ug, ug, vb, ALU.mult, s, tug)
        for k in range(8):
            ck = cv[:, k * 128:(k + 1) * 128]
            e = c.act_(ck, ck, ACT.Silu, a, scale=glg[:, k:k + 1], bias=glb[:, k:k + 1])
        w = c.tt(c.dve, cv, cv, ga, ALU.mult, e, tga)
        h1 = c.act_(yh[:, 1, :], ug, ACT.Copy, u, a)
        l1 = c.tt(c.pool, yl[:, 1, :], ug, yh[:, 1, :], ALU.subtract, h1, a)
        h0 = c.act_(yh[:, 0, :], cv, ACT.Copy, w, yfree[q])
        l0 = c.tt(c.dve, yl[:, 0, :], cv, yh[:, 0, :], ALU.subtract, h0)
        ldfree[0], ldfree[1], ldfree[2], ldfree[3] = [l0, h0], w, u, [l1, h1]
        return yh, yl, [l0, h0], [l1, h1]

    load(0)
    prep_a(0)
    prep_pe(0)
    ready = prep_b(0)
    for k in range(12, 16):
        OW.split(k)
    xfree, tfree = [twt, txf], None
    for i in range(16):
        yh, yl, r0, r1 = ready
        if i < 15:
            load(i + 1)
            prep_a(i + 1)
        tx = c.dma(c.sp, X, x[i * 128:(i + 1) * 128, :], xsem, xfree)
        bb, t = out_tile(c, 16, lambda k: yh[:, k // 8, (k % 8) * 128:(k % 8) * 128 + 128],
                         lambda k: yl[:, k // 8, (k % 8) * 128:(k % 8) * 128 + 128],
                         lambda k: r0 if k < 8 else r1, WO, two, lambda: prep_pe(i + 1) if i < 15 else None)
        yfree[i % 2] = [yfree[i % 2], t] if i < 2 else t
        if i < 15:
            ready = prep_b(i + 1)
        for h in range(2):
            e = c.tt(c.dve, T[:, h * 512:(h + 1) * 512], c.P[bb[h]][:, :], gate[:, h * 512:(h + 1) * 512], ALU.mult, t,
                     tfree, tgt, first)
            c.banks.give(bb[h], e)
        e = c.tt(c.pool, X, X, T, ALU.add, e, tx)
        s = s2[:, 0, i:i + 1]
        e1 = c.act_(T, X, ACT.Square, e, accum=s)
        e1 = rsqrt(c, s, s, 1.0 / D, e1)
        e = c.stt(X, X, s, fg, ALU.mult, ALU.mult, e1, tfg)
        x1tok[i] = c.dma(c.act, X1[i * 128:(i + 1) * 128, :], X, x1sem, e)
        tfree = c.act_(T, X, ACT.Square, e, accum=s2[:, 1, i:i + 1])
        xfree = [x1tok[i], tfree]
    rsqrt(c, c.rstd2, s2[:, 1, :], 1.0 / D, tfree)
    c.x1tok = [x1tok[i] for i in range(16)]
    c.fence()


TWO_PI = 2 * math.pi
MAGIC = 12582912.0


def transform_constants():
    k = {}
    n1 = np.arange(128)[:, None]
    wk = np.zeros((128, 128))
    wai = np.zeros((128, 64))
    m1 = np.arange(64)
    for j in range(64):
        a = TWO_PI * ((n1[:, 0] * j) % 128) / 128
        b = TWO_PI * ((m1 * j) % 128) / 128
        if j == 0:
            wk[:, 0] = 1.0
            wk[:, 1] = np.where(n1[:, 0] % 2 == 0, 1.0, -1.0)
            wai[0] = 1.0 / 4096
            wai[1] = np.where(m1 % 2 == 0, 1.0, -1.0) / 4096
        else:
            wk[:, 2 * j] = np.cos(a)
            wk[:, 2 * j + 1] = -np.sin(a)
            wai[2 * j] = 2 * np.cos(b) / 4096
            wai[2 * j + 1] = -2 * np.sin(b) / 4096
    k["k_wk"] = wk
    wa = np.zeros((128, 2, 128))
    wb = np.zeros((128, 2, 128))
    for e in range(2):
        wa[e::2, e, :] = wk[:64]
        wb[:, e, e::2] = wai
    k["k_wa"] = wa.reshape(128, 256)
    k["k_wai"] = wb.reshape(128, 256)
    wx = np.zeros((128, 32, 3, 2, 32))
    wi = np.zeros((2, 2, 32, 32, 2, 2, 32))
    n2 = np.arange(32)[:, None]
    k2 = np.arange(32)[None, :]
    for b in range(32):
        for q in range(2):
            j = 2 * b + q
            re, im = slice(64 * q, 64 * q + 32), slice(64 * q + 32, 64 * q + 64)
            if j:
                th = TWO_PI * ((n2 * (j + 128 * k2)) % 4096) / 4096
                cs, sn = np.cos(th), np.sin(th)
                wx[re, b, 0, q], wx[im, b, 0, q] = cs, sn
                wx[re, b, 1, q], wx[im, b, 1, q] = -sn, cs
                wi[0, q, :, b, q, 0, :], wi[1, q, :, b, q, 0, :] = cs.T, -sn.T
                wi[0, q, :, b, q, 1, :], wi[1, q, :, b, q, 1, :] = sn.T, cs.T
                continue
            n = np.arange(32)
            alt = np.where(n % 2 == 0, 1.0, -1.0)
            wx[re, 0, 0, 0, 0] = 1.0
            wx[re, 0, 1, 0, 0] = alt
            wi[0, 0, 0, 0, 0, 0, :] = 1.0
            wi[1, 0, 0, 0, 0, 0, :] = alt
            for v in range(1, 32):
                f = 128 * v if v < 16 else 64 + 128 * (v - 16)
                row, cc = (re, 0) if v < 16 else (im, 1)
                th = TWO_PI * ((n * f) % 4096) / 4096
                wx[row, 0, 0, 0, v] = np.cos(th)
                wx[row, 0, 1, 0, v] = -np.sin(th)
                wi[0, 0, v, 0, 0, cc, :] = 2 * np.cos(th)
                wi[1, 0, v, 0, 0, cc, :] = -2 * np.sin(th)
    wx[:, :, 2] = wx[:, :, 0]
    k["k_wx"] = wx.reshape(128, 6144)
    k["k_wi"] = wi.reshape(128, 4096)
    sg = np.ones((128, 1))
    sg[0:64] = -1.0
    k["k_sg"] = sg
    L = S_LEN
    f32 = np.float32
    t = np.linspace(0.0, 1.0, L, dtype=f32)[:, None]
    ang = f32(2.0 * math.pi) * np.arange(L, dtype=f32)[:, None] / f32(L)
    bands = np.linspace(1e-4, 15, 16, dtype=f32)[None, :]
    z = np.concatenate([t, np.cos(bands * ang), -np.sin(bands * ang)], axis=-1).astype(f32)
    i = np.arange(64)
    tf = np.stack([32 * i + n for n in range(32)])
    tb = np.stack([2048 - n - 32 * i for n in range(32)])
    k["k_z"] = np.concatenate([z[tf.reshape(-1)].T, z[np.minimum(tb, L - 1).reshape(-1)].T], 0)
    max_decay = math.log(1e-2) / 0.3
    min_decay = math.log(1e-2) / 1.5
    deltas = np.linspace(min_decay, max_decay, 512, dtype=f32)
    dec = np.exp(-t * np.abs(deltas)[None, :]).astype(f32)
    dec = np.concatenate([dec, np.zeros((1, 512), f32)], 0)
    k["k_dec"] = np.concatenate([dec[tf.T], dec[tb.T]], 0)
    ec = np.ones((4, 16))
    for g, w in enumerate((2, 4, 8, 16)):
        for q in range(8):
            if q < w // 2:
                ec[g, q] = w / (q + w // 2)
            tt_ = L - 8 + q
            cnt = min(tt_ + w // 2 - 1, L - 1) - (tt_ - w // 2) + 1
            ec[g, 8 + q] = w / cnt
    k["k_ec"] = ec
    return {n: np.ascontiguousarray(v, dtype=np.float32) for n, v in k.items()}


def block2(c, A, X1, X2, Y, GD):
    R0, R2 = c.R0, c.R2
    c.top = c.base
    w_in = A["w_in_2"][0]
    cols = [16, 17, 20, 18, 21, 19, 22, 12, 23, 13, 14, 15] + list(range(12))
    W = Split(c, R2, 3, [(w_in, q * 128) for q in cols])
    W.load()
    W.load()
    o = R2 + 8192
    make_ht(c, rows_from(c, X1, c.x1tok, o, [c.dsem_of(i) for i in range(8)]), c.rstd2, c.col("pre_norm_g_2"), None,
            None)
    tht = [t for l in c.ht_tok for t in l[-2:]]
    B = [c.view(o + 2064 * i, 2064) for i in range(4)]
    ost = c.view(o + 8256, 4, 512)
    ec = c.view(o + 10304, 4, 16)
    pw = c.view(c.take(512), 4, 128)
    tpw = c.dma(c.sp, pw[:, :, :], A["pool_w_2"][0].rearrange("g c d -> c g d"), c.dsem_of(8))
    tec = c.dma(c.sp, ec[:, :, :], A["k_ec"].partition_broadcast(128), c.dsem_of(9), tht)
    pads = [c.ms(c.pool, u[:, a:b], 0.0, tht) for u in B[:2] for a, b in ((0, 8), (2056, 2064))]
    oring = Ring(4)
    for i in range(4):
        oring.give(i, tht)
    osem = [c.dsem_of(10 + i) for i in range(4)]
    ufree = [None, None]
    ytok, ztok = {}, {}
    ps = c.col("pool_scale_2")
    Sa, Sb = B[2], B[3]
    pend = None

    def pool_out(g, tp_):
        s, tw = W.get()
        ytok[4 + g] = []
        for tb in range(4):
            b, t = proj(c, W, s, tw, tb)
            r, rf = oring.take()
            e = c.act_(ost[:, r, :], c.P[b][:, :], ACT.Silu, t, rf)
            c.banks.give(b, e)
            b, bf = c.banks.take()
            t2 = c.mm(c.P[b][:, :], pw[:, g, :], B[g % 2][:, 8 + tb * 512:8 + (tb + 1) * 512], True, True, bf, tp_,
                      tpw, sig=True)
            e = c.stt(ost[:, r, :], c.P[b][:, :], ps[:, g:g + 1], ost[:, r, :], ALU.mult, ALU.mult, t2, e)
            c.banks.give(b, e)
            d = c.dma(c.sp, Y[4 + g][:, tb * 512:(tb + 1) * 512], ost[:, r, :], osem[r], e)
            ytok[4 + g].append(d)
            oring.give(r, d)
        W.ring.give(s, t)
        ufree[g % 2] = t2

    for g in range(4):
        w = 2 << g
        u = B[g % 2]
        s, tw = W.get()
        tu = []
        for tb in range(4):
            b, t = proj(c, W, s, tw, tb)
            e = c.act_(u[:, 8 + tb * 512:8 + (tb + 1) * 512], c.P[b][:, :], ACT.Copy, t, ufree[g % 2], pads, tht)
            c.banks.give(b, e)
            tu.append(e)
        W.ring.give(s, t)
        t = c.tt(c.dve, Sa[:, 1:2064], u[:, 0:2063], u[:, 1:2064], ALU.add, tu, c.dve.last())
        cur, nxt, lo, hi, d = Sa, Sb, 1, 2063, 1
        for _ in range(g):
            t = c.tt(c.dve, nxt[:, lo + d:hi - d + 1], cur[:, lo:hi - 2 * d + 1], cur[:, lo + 2 * d:hi + 1], ALU.add, t)
            cur, nxt, lo, hi, d = nxt, cur, lo + d, hi - d, 2 * d
        t = c.tt(c.dve, cur[:, 8:16], cur[:, 8:16], ec[:, g, 0:8], ALU.mult, t, tec)
        t = c.tt(c.dve, cur[:, 2048:2056], cur[:, 2048:2056], ec[:, g, 8:16], ALU.mult, t)
        t = c.stt(u[:, 8:2056], cur[:, 8:2056], 1.0 / w, u[:, 8:2056], ALU.mult, ALU.subtract, t)
        if pend is not None:
            pool_out(*pend)
        pend = (g, t)
    for q in range(4):
        s, tw = W.get()
        ztok[q] = []
        for tb in range(4):
            b, t = proj(c, W, s, tw, tb)
            r, rf = oring.take()
            e = c.act_(ost[:, r, :], c.P[b][:, :], ACT.Silu, t, rf)
            c.banks.give(b, e)
            d = c.dma(c.sp, GD[q][:, tb * 512:(tb + 1) * 512], ost[:, r, :], osem[r], e)
            ztok[q].append(d)
            oring.give(r, d)
        W.ring.give(s, t)
        if q == 0:
            pool_out(*pend)
    TT, ST = B[2][:, 0:2048], B[3][:, 0:2048]
    pads = [c.ms(c.pool, p[:, a:b], 0.0, ufree, c.dve.last()) for p in B[:2] for a, b in ((0, 1), (2049, 2052))]
    pfree, sfree = [ufree, ufree], c.dve.last()
    ssem = c.dsem_of(14)
    cb2 = c.col("conv_b_2")
    cw2 = c.col("conv_w_2")
    pend, tfree = None, None

    def to_time(n, tc_):
        nonlocal sfree
        tv = TT.rearrange("p (n j) -> p n j", j=16)
        ev = []
        for jg in range(4):
            b, bf = c.banks.take()
            for jj in range(4):
                t = c.tr(c.P[b][:, jj * 128:(jj + 1) * 128], tv[:, :, 4 * jg + jj], c.ident, bf, tc_, sig=(jj == 3))
            e = c.act_(ST[:, 512 * jg:512 * jg + 512], c.P[b][:, :], ACT.Copy, t, sfree)
            c.banks.give(b, e)
            ev.append(e)
        sfree = c.dma(c.sp, GD[8 + n], ST, ssem, ev)
        return t

    for n in range(12):
        q = n % 2
        P_ = B[q]
        s, tw = W.get()
        ev = []
        for tb in range(4):
            b, t = proj(c, W, s, tw, tb)
            e = c.act_(P_[:, 1 + tb * 512:1 + (tb + 1) * 512], c.P[b][:, :], ACT.Copy, t, pfree[q], pads)
            c.banks.give(b, e)
            ev.append(e)
        W.ring.give(s, t)
        if pend is not None:
            tfree = to_time(*pend)
        t = c.ts(c.dve, TT, P_[:, 1:2049], cw2[:, 12 + n:13 + n], cb2[:, n:n + 1], ALU.mult, ALU.add, ev, tfree,
                 c.dve.last())
        t = c.stt(TT, P_[:, 0:2048], cw2[:, n:n + 1], TT, ALU.mult, ALU.add, t)
        t = c.stt(TT, P_[:, 2:2050], cw2[:, 24 + n:25 + n], TT, ALU.mult, ALU.add, t)
        pfree[q] = t
        pend = (n, t)
    to_time(*pend)
    c.fence()
    hyena(c, A, GD)
    R1 = R0 + 16384
    YT = c.view(R1, 8, 2048)
    UT, ZT = c.view(R2, 2, 2048), c.view(R2 + 4096, 2, 2048)
    ly = {}
    ycm = []
    for q in range(4):
        r = q % 2
        rf = ycm[q - 2] if q >= 2 else None
        t1 = c.dma(c.sp, UT[:, r, :], GD[4 + q], c.dsem_of(40 + r), rf)
        t2 = c.dma(c.act, ZT[:, r, :], GD[q], c.dsem_of(42 + r), rf)
        es = []
        for jg in range(4):
            b, bf = c.banks.take()
            for jj in range(4):
                j = 4 * jg + jj
                t = c.tr(c.P[b][:, jj * 128:(jj + 1) * 128], UT[:, r, j * 128:(j + 1) * 128], c.ident, bf, t1,
                         sig=(jj == 3))
            a3 = "p (n j) -> p j n"
            e = c.tt(c.dve, YT[:, q, :].rearrange(a3, j=16)[:, 4 * jg:4 * jg + 4, :],
                     c.P[b][:, :].rearrange("p (j n) -> p j n", j=4),
                     ZT[:, r, :].rearrange(a3, j=16)[:, 4 * jg:4 * jg + 4, :], ALU.mult, t, t2)
            c.banks.give(b, e)
            es.append(e)
        ycm.append(es)
        ly[q] = es
    for k in range(4, 8):
        ly[k] = c.dma(c.sp, YT[:, k, :], Y[k], c.dsem_of(k))
    sq, sm, rs = c.view(R2, 4, 512), c.view(R2 + 2048, 2, 512), c.view(R2 + 3072, 2, 512)
    X, TD, pg = c.view(R2 + 8192, 2, 1024), [c.view(R2 + 10240, 1024), c.view(R2 + 4096, 1024)], c.view(R2 + 11264, 1024)
    YP = [(c.view(R2 + 12288 + 2048 * q, 1024, r=True), c.view(R2 + 13312 + 2048 * q, 1024, r=True)) for q in range(2)]
    st = c.view(c.take(16), 16)
    def weights():
        return load_wo(c, A["w_out_2"][0], R0, 8, c.view(R2 + 8192, 4, 1024), [c.dsem_of(32 + i) for i in range(4)])

    qring, mring = Ring(4), Ring(2)
    yat = {}
    ready = {}
    yfree = [None, None]

    def norm(tb):
        sl = slice(tb * 512, (tb + 1) * 512)
        last = []
        for grp in range(2):
            m, mf = mring.take()
            gain = c.col("norm_h_g_2" if grp == 0 else "norm_p_g_2")
            tp = None
            for k in range(4):
                r, rf = qring.take()
                e = c.act_(sq[:, r, :], YT[:, 4 * grp + k, sl], ACT.Square, ly[4 * grp + k], rf, ycm)
                if k == 0:
                    tp = c.cp(c.pool, sm[:, m, :], sq[:, r, :], e, mf, ycm)
                else:
                    tp = c.tt(c.pool, sm[:, m, :], sm[:, m, :], sq[:, r, :], ALU.add, e, tp)
                qring.give(r, tp)
            b, bf = c.banks.take()
            t = c.mm(c.P[b][:, :], c.ones, sm[:, m, :], True, True, bf, tp, sig=True)
            e = rsqrt(c, rs[:, m, :], c.P[b][:, :], 1.0 / 512, t, mf, ycm)
            c.banks.give(b, e)
            for k in range(4):
                v = YT[:, 4 * grp + k, sl]
                e2 = c.stt(v, v, gain[:, k:k + 1], rs[:, m, :], ALU.mult, ALU.mult, e, ly[4 * grp + k])
                last.append(e2)
            mring.give(m, t, e2)
        yat[tb] = last

    def prep(i):
        q = i % 2
        yh, yl = YP[q]
        v = YT[:, :, i * 128:(i + 1) * 128]
        h3 = lambda a: a.rearrange("p (k t) -> p k t", k=8)
        e = c.act_(h3(yh), v, ACT.Copy, yat[i // 4], yfree[q])
        e1 = c.tt(c.pool, h3(yl), v, h3(yh), ALU.subtract, e)
        ready[i] = [e, e1]

    xring, xsem = Ring(2), [c.dsem_of(9 + i) for i in range(2)]
    x2sem = [c.dsem_of(11 + i) for i in range(2)]
    norm(0)
    prep(0)
    WO, two = weights()
    prep(1)
    norm(1)
    tpg = c.dma(c.act, pg, A["post_norm_g_2"][0, :].partition_broadcast(128), c.dsem_of(8), two)
    x2tok, tfs = {}, [two, [two, ycm]]
    for i in range(16):
        yh, yl = YP[i % 2]
        bb, t = out_tile(c, 8, lambda k: yh[:, k * 128:(k + 1) * 128], lambda k: yl[:, k * 128:(k + 1) * 128],
                         lambda k: ready[i], WO, two)
        yfree[i % 2] = t
        if i + 2 < 16:
            prep(i + 2)
        if i in (2, 6):
            norm(i // 4 + 2)
        r, xf = xring.take()
        X_, T, tf = X[:, r, :], TD[i % 2], tfs[i % 2]
        tx = c.dma(c.sp, X_, X1[i * 128:(i + 1) * 128, :], xsem[r], xf, two)
        s = st[:, 4 * r:4 * r + 2]
        e1 = c.act_(T[:, 0:512], c.P[bb[0]][:, :], ACT.Square, t, tf, xf, accum=s[:, 0:1])
        e1 = c.act_(T[:, 512:1024], c.P[bb[1]][:, :], ACT.Square, t, accum=s[:, 1:2])
        s1 = st[:, 4 * r + 2:4 * r + 3]
        e1 = c.tt(c.dve, s1, s[:, 0:1], s[:, 1:2], ALU.add, e1, xf)
        e1 = rsqrt(c, s1, s1, 1.0 / D, e1)
        for h in range(2):
            e = c.stt(T[:, h * 512:(h + 1) * 512], c.P[bb[h]][:, :], s1, pg[:, h * 512:(h + 1) * 512], ALU.mult,
                      ALU.mult, e1, tpg)
            c.banks.give(bb[h], e)
        e = c.tt(c.pool, X_, X_, T[:, :], ALU.add, e, tx)
        tfs[i % 2] = e
        x2tok[i] = c.dma(c.act, X2[i * 128:(i + 1) * 128, :], X_, x2sem[r], e)
        xring.give(r, e, x2tok[i])
    c.x2tok = [x2tok[i] for i in range(16)]
    c.fence()


def hyena(c, A, GD):
    o = [c.R0]
    flat = lambda v: v.rearrange("p a b -> p (a b)")

    def al(n):
        o[0] += n
        return o[0] - n

    G = c.view(al(2048), 32, 64)
    KT = c.view(al(4096), 32, 128)
    AK = c.view(al(4096), 32, 128)
    KR = c.view(al(4096), 32, 128)
    KI = c.view(al(4096), 32, 128)
    AD = c.view(al(4096), 32, 128)
    DD = c.view(al(4096), 32, 128)
    T2 = c.view(al(4096), 32, 128)
    WX = c.view(al(6144), 32, 192)
    WI = c.view(al(4096), 32, 128)
    WP = c.view(al(1024), 2, 512)
    DEC = c.view(al(1024), 2, 512)
    U = c.view(al(4096), 2, 2048)
    GT = c.view(al(2048), 2048)
    WK, WA = c.view(al(128), 128), c.view(al(256), 2, 128)
    WAI = c.view(al(256), 2, 128)
    dr = c.view(al(128), 128)
    sg = c.view(al(1), 1)
    fc = c.view(al(8), 8)
    ld = []
    n_ = [0]

    def load(dst, src):
        n_[0] += 1
        ld.append(c.dma(c.sp if n_[0] % 2 else c.act, dst, src, c.dsem_of(n_[0] - 1), slow=True))

    Z = c.view(c.R0 + 2048, 2048)
    H = [c.view(c.R0 + 2048 + 4096, 2048), c.view(c.R0 + 2048 + 8192, 2048)]
    Q = c.view(c.R0 + 2048 + 12288, 2048)
    WF = c.view(c.R0 + 2048 + 16384, 3, 128)
    z0 = c.ms(c.pool, WF[:, :, :], 0.0)
    c.sp.wait(z0)
    c.act.wait(z0)
    load(Z[0:66, :], A["k_z"])
    for h in range(2):
        load(WF[33 * h:33 * h + 33, 0, 64 * h:64 * h + 64], A["filt_w1_2"][0])
        load(WF[64 * h:64 * h + 64, 1, 64 * h:64 * h + 64], A["filt_w2_2"][0])
        load(WF[64 * h:64 * h + 64, 2, 64 * h:64 * h + 64], A["filt_w3_2"][0])
        for q, nm in enumerate(("filt_freq_2", "filt_b1_2", "filt_b2_2", "filt_b3_2")):
            load(fc[64 * h:64 * h + 64, q:q + 1], A[nm].rearrange("l n -> n l"))
        load(WP[64 * h:64 * h + 64, :, :],
             A["filt_w_out_2"][0].rearrange("k (o d n) -> k o d n", o=2, d=2)[:, :, h, :])
    load(WK, A["k_wk"])
    load(flat(WA), A["k_wa"])
    load(flat(WAI), A["k_wai"])
    load(sg, A["k_sg"])
    big = [c.dma(c.sp, WX[:, :, :].rearrange("p a b -> p (a b)"), A["k_wx"], c.dsem_of(34)),
           c.dma(c.act, WI[:, :, :].rearrange("p a b -> p (a b)"), A["k_wi"], c.dsem_of(35))]
    c.pe.wait(ld)
    c.dve.wait(ld)
    c.act.wait(ld)
    tfb = c.ts(c.dve, fc[:, 4:7], fc[:, 1:4], fc[:, 0:1], None, ALU.mult, None, ld)
    src, kk, th = Z, 66, None
    tg = None
    for layer in range(3):
        dst = H[layer % 2]
        new = []
        for tb in range(4):
            sl = slice(tb * 512, (tb + 1) * 512)
            b, bf = c.banks.take()
            t = c.mm(c.P[b][:, :], WF[0:kk, layer, :], src[0:kk, sl], True, True, bf, th, sig=True)
            d = dst[:, sl]
            q = Q[:, sl]
            e = c.ts(c.dve, d, c.P[b][:, :], fc[:, 0:1], fc[:, 4 + layer:5 + layer], ALU.mult, ALU.add, t, tfb, th)
            c.banks.give(b, e)
            e2 = c.ts(c.dve, q, d, 1.0 / TWO_PI, MAGIC, ALU.mult, ALU.add, e)
            e2 = c.ts(c.dve, q, q, MAGIC, None, ALU.subtract, None, e2)
            hi = float(np.float32(6.28125))
            mid = float(np.float32(TWO_PI - 6.28125))
            lo = float(np.float32(TWO_PI - 6.28125 - float(np.float32(TWO_PI - 6.28125))))
            for v in (hi, mid, lo):
                e2 = c.stt(d, q, -v, d, ALU.mult, ALU.add, e2)
            e2 = c.ts(c.dve, d, d, 3.1415925, -3.1415925, ALU.min, ALU.max, e2)
            if layer < 2:
                new.append(c.act_(d, d, ACT.Sin, e2))
            else:
                new.append(c.act_(G[:, tb * 8:(tb + 1) * 8, :].rearrange("p a b -> p (a b)"), d, ACT.Sin, e2))
        src, kk, th = dst, 128, new
    tg = th
    c.fence()

    jobs = [(0, 0), (0, 1), (1, 0), (1, 1), (0, 2), (0, 3), (1, 2), (1, 3)]
    dring = Ring(2)
    dsem_ = [c.dsem_of(i) for i in range(2)]
    usem = [c.dsem_of(2 + i) for i in range(2)]
    gsem, rsem, osem, dup = c.dsem_of(4), c.dsem_of(5), [c.dsem_of(6 + i) for i in range(2)], [c.dsem_of(8 + i) for i in range(2)]
    ksh = [c.dsem_of(10 + i) for i in range(8)]
    ash = [c.dsem_of(18 + i) for i in range(8)]
    bsh = [c.dsem_of(26 + i) for i in range(8)]
    F = {n: None for n in ("KT", "AK", "K", "AD", "DD", "T2", "dr", "GT")}
    ufree = [None, None]
    utok = {}
    SH = [c.nc.dram_tensor(f"sh{i}", (32, 128, 128), F32, kind="Internal").ap() for i in range(3)]

    def shuffle(dram, dst, src, sems, out, *after):
        rows = dram.rearrange("b q n -> (b q) n").rearrange("(p m) n -> p m n", m=32)
        w = [c.dma(c.act, rows[:, 8 * g:8 * g + 8, :], src[:, 8 * g:8 * g + 8, :], sems[g], out[2 * g:2 * g + 2], F[dram.name])
             for g in range(4)]
        sh = [c.dma(c.sp, dst[:, 8 * g:8 * g + 8, :], dram[8 * g:8 * g + 8, :, :].rearrange("b q n -> q b n"),
                    sems[4 + g], w, *after) for g in range(4)]
        F[dram.name] = sh
        return w, sh

    def unshuffle(dram, dst, src, sems, out, *after):
        rows = dram.rearrange("b q n -> (b q) n").rearrange("(p m) n -> p m n", m=32)
        w = [c.dma(c.act, dram[8 * g:8 * g + 8, :, :].rearrange("b q n -> q b n"), src[:, 8 * g:8 * g + 8, :], sems[g],
                   out[2 * g:2 * g + 2], F[dram.name]) for g in range(4)]
        sh = [c.dma(c.sp, dst[:, 8 * g:8 * g + 8, :], rows[:, 8 * g:8 * g + 8, :], sems[4 + g], w, *after)
              for g in range(4)]
        F[dram.name] = sh
        return w, sh

    for d_ in SH:
        F[d_.name] = None

    def kgen(i):
        od, ch = jobs[i]
        cs = slice(ch * 128, (ch + 1) * 128)
        tdr = c.dma(c.act, dr[0:1, :], A["hyena_d_2"][0, od:od + 1, cs], rsem, F["dr"])
        ev = []
        for g in range(8):
            r, rf = dring.take()
            td = c.dma(c.sp, DEC[:, r, :].rearrange("p (a b) -> p a b", b=128),
                       A["k_dec"][:, 4 * g:4 * g + 4, cs], dsem_[r], rf)
            b, bf = c.banks.take()
            for j in range(4):
                n2 = 4 * g + j
                for h in range(2):
                    rr = slice(64 * h, 64 * h + 64)
                    t = c.mm(c.P[b][rr, j * 128:(j + 1) * 128], G[rr, n2, :], WP[rr, od, cs], True, True, bf,
                             sig=(j == 3 and h == 1))
            e = c.tt(c.dve, flat(KT[:, 4 * g:4 * g + 4, :]), c.P[b][:, :], DEC[:, r, :], ALU.mult, t, td, F["KT"])
            c.banks.give(b, e)
            dring.give(r, e)
            if g == 0:
                e = c.tt(c.dve, KT[0:1, 0, :], KT[0:1, 0, :], dr[0:1, :], ALU.add, e, tdr)
                F["dr"] = e
            ev.append(e)
        out = []
        for g in range(8):
            b, bf = c.banks.take()
            t = c.mm(c.P[b][:, :], WK, flat(KT[:, 4 * g:4 * g + 4, :]), True, True, bf, ev[g], sig=True)
            e = c.act_(flat(AK[:, 4 * g:4 * g + 4, :]), c.P[b][:, :], ACT.Copy, t, F["AK"])
            c.banks.give(b, e)
            out.append(e)
        F["AK"], sh = shuffle(SH[0], KT, AK, ksh, out, t)
        return sh

    def kspec(i, sh):
        er, ei = [], []
        for g in range(8):
            b, bf = c.banks.take()
            for j in range(4):
                t = c.mm(c.P[b][:, j * 128:(j + 1) * 128], WX[:, 4 * g + j, 0:128], KT[:, 4 * g + j, :], True, True,
                         bf, sh[g // 2], sig=(j == 3))
            e1 = c.act_(flat(KR[0:64, 4 * g:4 * g + 4, :]), c.P[b][0:64, :], ACT.Copy, t, F["K"])
            e2 = c.act_(flat(KI[64:128, 4 * g:4 * g + 4, :]), c.P[b][64:128, :], ACT.Copy, t, F["K"])
            c.banks.give(b, e2)
            er.append(e1)
            ei.append(e2)
        F["KT"] = t
        d1 = c.dma(c.act, KR[64:128, :, :], KR[0:64, :, :], dup[0], er, F["K"])
        d2 = c.dma(c.sp, KI[0:64, :, :], KI[64:128, :, :], dup[1], ei, F["K"])
        e = c.cp(c.dve, KR[64:65, 0, :], KI[64:65, 0, :], d1, ei[0])
        e = c.ms(c.dve, KI[64:65, 0, :], 0.0, e, d2)
        e2 = c.ms(c.dve, KI[0:1, 0, :], 0.0, d2)
        for g in range(8):
            kt[g] = [d1, d2, e, e2]

    def da(i):
        od, ch = jobs[i]
        if od == 0:
            utok[i] = c.dma(c.sp, U[:, i % 2, :], GD[8 + ch], usem[i % 2], ufree[i % 2])
        out = []
        for e_ in range(2):
            for jg in range(4):
                b, bf = c.banks.take()
                t = c.mm(c.P[b][:, :], WA[:, e_, :], U[:, i % 2, jg * 512:(jg + 1) * 512], True, True, bf, utok[i],
                         sig=True)
                n2 = 16 * e_ + 4 * jg
                if jg % 2:
                    e = c.act_(flat(AD[:, n2:n2 + 4, :]), c.P[b][:, :], ACT.Copy, t, F["AD"])
                else:
                    e = c.cp(c.dve, flat(AD[:, n2:n2 + 4, :]), c.P[b][:, :], t, F["AD"])
                c.banks.give(b, e)
                out.append(e)
        ufree[i % 2] = t
        return out

    def dshuffle(out):
        F["AD"], sh = shuffle(SH[1], DD, AD, ash, out, F["DD"])
        return sh

    def db(i, sh):
        yt = []
        for g in range(8):
            b1, f1 = c.banks.take()
            b2, f2 = c.banks.take()
            for j in range(4):
                bk = 4 * g + j
                ps = slice(j * 128, (j + 1) * 128)
                c.mm(c.P[b1][:, ps], WX[:, bk, 0:128], DD[:, bk, :], True, True, f1, sh[g // 2])
                t = c.mm(c.P[b2][:, ps], WX[:, bk, 64:192], DD[:, bk, :], True, True, f2, sig=(j == 3))
            kr, ki = flat(KR[:, 4 * g:4 * g + 4, :]), flat(KI[:, 4 * g:4 * g + 4, :])
            e1 = c.tt(c.dve, kr, c.P[b1][:, :], kr, ALU.mult, t, kt[g])
            e2 = c.stt(ki, c.P[b2][:, :], sg[:, 0:1], ki, ALU.mult, ALU.mult, t)
            c.banks.give(b1, e1)
            c.banks.give(b2, e2)
            e3 = c.tt(c.pool, flat(DD[:, 4 * g:4 * g + 4, :]), kr, ki, ALU.add, e1, e2, t)
            yt.append(e3)
        F["K"] = e3
        return yt

    def binv(i, yt):
        out = []
        for g in range(8):
            b, bf = c.banks.take()
            for j in range(4):
                bk = 4 * g + j
                t = c.mm(c.P[b][:, j * 128:(j + 1) * 128], WI[:, bk, :], DD[:, bk, :], True, True, bf, yt[g],
                         sig=(j == 3))
            e = c.act_(flat(AK[:, 4 * g:4 * g + 4, :]), c.P[b][:, :], ACT.Copy, t, F["AK"])
            c.banks.give(b, e)
            out.append(e)
        F["DD"] = t
        F["AK"], sh = unshuffle(SH[2], T2, AK, bsh, out, F["T2"])
        return sh

    def ainv(i, sh):
        od, ch = jobs[i]
        tg_ = c.dma(c.sp, GT[:, :], GD[8 + 4 * (od + 1) + ch], gsem, F["GT"])
        ev = []
        for jg in range(4):
            b, bf = c.banks.take()
            for e_ in range(2):
                n2 = 16 * e_ + 4 * jg
                t = c.mm(c.P[b][:, :], WAI[:, e_, :], flat(T2[:, n2:n2 + 4, :]), e_ == 0, e_ == 1, bf, sh,
                         sig=(e_ == 1))
            e = c.tt(c.dve, U[:, i % 2, jg * 512:(jg + 1) * 512], c.P[b][:, :], GT[:, jg * 512:(jg + 1) * 512],
                     ALU.mult, t, tg_, ufree[i % 2])
            c.banks.give(b, e)
            ev.append(e)
        F["T2"] = t
        F["GT"] = e
        if od == 0:
            utok[i + 2] = ev
        else:
            ufree[i % 2] = c.dma(c.act, GD[4 + ch], U[:, i % 2, :], osem[ch % 2], ev)
            ytime[ch] = ufree[i % 2]

    ytime = [None] * 4
    kt = [None] * 8
    ks = kgen(0)
    dsh = dshuffle(da(0))
    kspec(0, ks)
    for i in range(8):
        if i < 7:
            ks = kgen(i + 1)
        yt = db(i, dsh)
        if i < 7:
            dout = da(i + 1)
        bs = binv(i, yt)
        if i < 7:
            dsh = dshuffle(dout)
            kspec(i + 1, ks)
        ainv(i, bs)
    c.fence()


def window_constants():
    q = np.arange(64)
    start = np.clip(q - 8, 0, 48)
    kc = np.arange(64)
    inside = (kc[None, :] >= start[:, None]) & (kc[None, :] < start[:, None] + 16)
    m = np.where(inside, 0.0, -1e30).astype(np.float32)
    s, t = np.arange(128)[:, None], np.arange(128)[None, :]
    same = s // 16 == t // 16
    pair = np.stack([same & (s <= t), same & (s >= t)]).astype(np.int32)
    reset = np.ones((1, 512), np.float32)
    reset[0, ::128] = 0.0
    return {"k_flip": np.kron(np.eye(2), np.eye(64)[::-1]).astype(np.float32), "k_win": np.concatenate([m, m], 0), "k_pair": pair.transpose(1, 0, 2).copy(), "k_reset": reset}


def block3(c, A, X2, out, Y, GD):
    R0, R2 = c.R0, c.R2
    KB = c.nc.dram_tensor("kb_tiles", (24, 128, S_LEN), F32, kind="Internal").ap()
    VR = c.nc.dram_tensor("va_rows", (S_LEN, 512), F32, kind="Internal").ap()
    IR = c.nc.dram_tensor("ih_rows", (S_LEN, 512), F32, kind="Internal").ap()
    tok = project3(c, A, X2, GD, KB, VR, IR)
    c.fence()
    mix3(c, A, Y, GD, KB, VR, IR)
    c.fence()
    output3(c, A, X2, out, Y)


def project3(c, A, X2, GD, KB, VR, IR):
    R2 = c.R2
    w_in = A["w_in_3"][0]
    b_in = c.col("b_in_3")
    cols = []
    for hd in range(4):
        cols += [2560 // 128 + hd, hd, 3072 // 128 + hd, 4 + hd, 12 + hd, 16 + hd, 32 + hd]
    cols += [28, 29, 30, 31, 8, 9, 10, 11]
    W = Split(c, R2, 4, [(w_in, q * 128) for q in cols])
    W.load()
    W.load()
    make_ht(c, rows_from(c, X2, c.x2tok, R2 + 10240, [c.dsem_of(i) for i in range(8)]), None, None, None, None)
    tht = [t for l in c.ht_tok for t in l[-2:]]
    o = R2 + 10240
    ost = c.view(o, 2, 512)
    FG, KK, BB, WW = (c.view(o + 1024 + 1024 * i, 2, 512) for i in range(4))
    reset = c.view(o + 5120, 512)
    vb = c.view(o + 5632, 2, 512)
    lbv = c.view(o + 6656, 64)
    tr0 = c.dma(c.sp, reset, A["k_reset"][0, :].partition_broadcast(128), c.dsem_of(8), tht)
    tvb = [c.dma(c.sp, vb[:, i, :], A["b_in_3"][0, a:a + 512].partition_broadcast(128), c.dsem_of(9 + i), tht)
           for i, a in enumerate((3584, 1024))]
    tl = []
    for d, nm in enumerate(("lb_fwd_logits_3", "lb_bwd_logits_3")):
        l = c.col(nm)
        a = 32 * d
        m, e0, e1, lo = (lbv[:, a + 4 * i:a + 4 * i + 4] for i in range(4))
        t = c.tt(c.dve, m, l[:, 0:4], l[:, 4:8], ALU.max, c.t_par, tht)
        t0 = c.tt(c.dve, e0, l[:, 0:4], m, ALU.subtract, t)
        t1 = c.tt(c.dve, e1, l[:, 4:8], m, ALU.subtract, t)
        t0 = c.act_(e0, e0, ACT.Exp, t0)
        t1 = c.act_(e1, e1, ACT.Exp, t1)
        t = c.tt(c.dve, m, e0, e1, ALU.add, t0, t1)
        t = c.recip(m, m, t)
        t = c.tt(c.dve, lo, e0, m, ALU.mult, t)
        t = c.ts(c.dve, lbv[:, a + 16:a + 20], lo, -1.0, 1.0, ALU.mult, ALU.add, t)
        tl.append(t)
    oring, fring = Ring(2), Ring(2)
    oring.give(0, tht)
    oring.give(1, tht)
    fring.give(0, tht)
    fring.give(1, tht)
    osem = [c.dsem_of(11 + i) for i in range(2)]
    fsem = [[c.dsem_of(13 + 3 * i + j) for j in range(3)] for i in range(2)]

    def plain(dst, func, bcol):
        s, tw = W.get()
        for tb in range(4):
            b, t = proj(c, W, s, tw, tb)
            r, rf = oring.take()
            e = c.act_(ost[:, r, :], c.P[b][:, :], func, t, rf, bias=b_in[:, bcol:bcol + 1])
            c.banks.give(b, e)
            oring.give(r, c.dma(c.sp, dst[:, tb * 512:(tb + 1) * 512], ost[:, r, :], osem[r], e))
        W.ring.give(s, t)

    def forget(hd, d):
        s, tw = W.get()
        a = 32 * d
        for tb in range(4):
            sl = slice(tb * 512, (tb + 1) * 512)
            b, t = proj(c, W, s, tw, tb)
            r, rf = fring.take()
            f, k, bb, w = FG[:, r, :], KK[:, r, :], BB[:, r, :], WW[:, r, :]
            e = c.act_(f, c.P[b][:, :], ACT.Sigmoid, t, rf, bias=b_in[:, 20 + 4 * d + hd:21 + 4 * d + hd])
            c.banks.give(b, e)
            e = c.ts(c.dve, f, f, lbv[:, a + 16 + hd:a + 17 + hd], lbv[:, a + 12 + hd:a + 13 + hd], ALU.mult, ALU.add,
                     e, tl)
            ek = c.ts(c.dve, k, f, -1.0, 1.0, ALU.mult, ALU.add, e, rf)
            dd = [c.dma(c.sp, KB[4 * d + hd][:, sl], k, fsem[r][0], ek)]
            e = c.act_(f, f, ACT.Ln, e, ek)
            eb = c.dve.do(lambda en, bb=bb, f=f: en.tensor_tensor_scan(bb, reset, f, 0.0, ALU.mult, ALU.add), e, tr0)
            dd.append(c.dma(c.sp, KB[8 + 4 * d + hd][:, sl], bb, fsem[r][1], eb))
            if d:
                ew = c.tt(c.dve, w, f, bb, ALU.subtract, eb)
                dd.append(c.dma(c.sp, KB[16 + hd][:, sl], w, fsem[r][2], ew))
                eb = ew
            fring.give(r, dd, eb)
        W.ring.give(s, t)

    for hd in range(4):
        forget(hd, 0)
        plain(GD[hd], ACT.Identity, hd)
        forget(hd, 1)
        plain(GD[4 + hd], ACT.Identity, 4 + hd)
        plain(GD[8 + hd], ACT.Silu, 12 + hd)
        plain(GD[12 + hd], ACT.Identity, 16 + hd)
        plain(GD[16 + hd], ACT.Silu, 32 + hd)
    for q in range(2):
        dst = (IR, VR)[q]
        for g in range(2):
            s0, t0 = W.get()
            s1, t1 = W.get(2)
            for i in range(0, 16, 2):
                b, bf = c.banks.take()
                for h in range(2):
                    t = proj_rows(c, W, [s0, s1], [t0, t1], i + h, b, 256 * h, bf)
                r, rf = oring.take()
                e = c.tt(c.dve, ost[:, r, :].rearrange("p (i n) -> p i n", n=256),
                         c.P[b][:, :].rearrange("p (i n) -> p i n", n=256),
                         vb[:, q, g * 256:(g + 1) * 256].unsqueeze(1).to_broadcast([128, 2, 256]), ALU.add, t, tvb, rf)
                c.banks.give(b, e)
                oring.give(r, c.dma(c.sp, dst[i * 128:(i + 2) * 128, g * 256:(g + 1) * 256]
                                    .rearrange("(i p) n -> p i n", p=128),
                                    ost[:, r, :].rearrange("p (i n) -> p i n", n=256), osem[r], e))
            W.ring.give(s0, t)
            W.ring.give(s1, t)


def mix3(c, A, Y, GD, KB, VR, IR):
    att = attention(c, A, c.R0, 0, Y, GD, VR)
    rec = recurrence(c, A, c.R0 + 23636, 40, Y, GD, KB, IR)
    na, nr = 141, 220
    a = r = 0
    live = [True, True]
    while any(live):
        if live[0] and (a * nr <= r * na or not live[1]):
            live[0] = next(att, "end") != "end"
            a += 1
        elif live[1]:
            live[1] = next(rec, "end") != "end"
            r += 1


def attention(c, A, off, sem0, Y, GD, VR):
    o = [off]

    def al(n):
        o[0] += n
        return o[0] - n

    V, VO = c.view(al(2048), 16, 128), c.view(al(2048), 16, 128)
    QB = [c.view(al(4096), 32, 128) for _ in range(2)]
    K = [c.view(al(2048), 2048) for _ in range(2)]
    SG = c.view(al(512), 1, 512)
    YS = c.view(al(1024), 2, 512)
    BT = c.view(al(1920), 2, 960)
    E = c.view(al(2048), 4, 512)
    PT = c.view(al(1536), 3, 512)
    win = c.view(al(64), 64)
    st = c.view(al(16), 4, 4)
    flip = c.view(al(128), 128)
    PR = E[:, 0, 0:128]
    banks, OBANK = Ring(3), 3
    S = lambda i: c.dsem_of(sem0 + i)
    tflip = c.dma(c.act, flip, A["k_flip"], S(0))
    twin = c.dma(c.act, win, A["k_win"], S(1))
    RD = c.nc.dram_tensor("rpb_rows", (120, 128), F32, kind="Internal").ap()
    t = c.ms(c.pool, PR[0:120, :], 0.0)
    t = c.dma(c.act, PR[0:120, 48:79], A["rpb_3"][0].rearrange("h a b -> (h a) b"), S(2), t)
    trd = c.dma(c.act, RD, PR[0:120, :], S(3), t)
    zq = [c.ms(c.dve, QB[i][:, :, :], 0.0) for i in range(2)]
    bfree, qkfree, sgfree = [None, None], [None, None], None
    ofree = None
    ering, pring, yring = Ring(4), Ring(3), Ring(2)
    for i in range(4):
        ering.give(i, trd)
    scale = 64 ** -0.5
    early, late, tv0, tv1 = {}, {}, {}, {}

    def early_loads(pr):
        pp = pr % 2
        bt = BT[:, pp, :].rearrange("p (a b) -> p a b", b=64)
        tbs = []
        for hh in range(2):
            src = bass.AP(RD.tensor, (2 * pr + hh) * 15 * 128, [[1, 64], [128, 15], [1, 64]])
            tbs.append(c.dma(c.sp, bt[64 * hh:64 * hh + 64, :, :], src, S(4 + hh), trd, bfree[pp]))
        tqk = [c.dma(c.sp, QB[pp][64 * hh:64 * hh + 64, :, 64 * hh:64 * hh + 64],
                     GD[pr][64 * hh:64 * hh + 64, :].rearrange("p (r q) -> p r q", q=64), S(6 + 2 * pp + hh), qkfree[pp],
                     zq) for hh in range(2)]
        tqk.append(c.dma(c.sp, K[pp], GD[4 + pr], S(10 + pp), qkfree[pp]))
        early[pr] = (tbs, tqk)

    def value_loads(pr, half, free):
        cs = slice(pr * 128, (pr + 1) * 128)
        lo, n, no = (0, 8, 8) if half == 0 else (8, 8, 7)
        return [c.dma(c.sp, V[:, lo:lo + n, :], VR[128 * lo:128 * (lo + n), cs].rearrange("(n p) x -> p n x", p=128),
                      S(12 + 6 * half), free),
                c.dma(c.sp, VO[:, lo:lo + no, :],
                      VR[64 + 128 * lo:64 + 128 * (lo + no), cs].rearrange("(n p) x -> p n x", p=128),
                      S(13 + 6 * half), free)]

    def biases(pr):
        pp = pr % 2
        bt = BT[:, pp, :].rearrange("p (a b) -> p a b", b=64)
        tfl = []
        for a, n in ((0, 8), (8, 7)):
            b, bf = banks.take()
            t = c.mm(c.P[b][:, 0:n * 64], flip, BT[:, pp, a * 64:(a + n) * 64], True, True, bf, early[pr][0], tflip,
                     sig=True)
            tfl.append((a, n, b, t))
        for a, n, b, t in tfl:
            tbt = c.tt(c.dve, bt[:, a:a + n, :], c.P[b][:, 0:n * 64].rearrange("p (a b) -> p a b", b=64),
                       win.unsqueeze(1).to_broadcast([128, n, 64]), ALU.add, t, twin)
            banks.give(b, tbt)
        late[pr] = tbt

    early_loads(0)
    tv0[0] = value_loads(0, 0, None)
    tv1[0] = value_loads(0, 1, None)
    biases(0)
    yield
    for pr in range(4):
        pp = pr % 2
        bt = BT[:, pp, :].rearrange("p (a b) -> p a b", b=64)
        qb, kk = QB[pp], K[pp]
        tqk, tbt = early[pr][1], late[pr]
        stage = {}

        def scores(r):
            r0 = min(max(r - 4, 0), 24)
            b, bf = banks.take()
            t = c.mm(c.P[b][:, :], qb[:, r, :], kk[:, r0 * 64:r0 * 64 + 512], True, True, bf, tqk, sig=True)
            stage["qk"] = t
            d0 = r0 - r + 7
            k, ef = ering.take()
            x = E[:, k, :]
            s_ = st[:, k, :]
            e = c.stt(x.rearrange("p (a b) -> p a b", b=64), c.P[b][:, :].rearrange("p (a b) -> p a b", b=64), scale,
                      bt[:, d0:d0 + 8, :], ALU.mult, ALU.add, t, ef, tbt)
            banks.give(b, e)
            e = c.dve.do(lambda en: en.tensor_reduce(s_[:, 0:1], x, AXX, ALU.max, negate=True), e)
            e = c.act_(x, x, ACT.Exp, e, bias=s_[:, 0:1], accum=s_[:, 1:2])
            stage[("e", r)] = (k, e)

        def divide(r):
            k, e = stage.pop(("e", r))
            x, s_ = E[:, k, :], st[:, k, :]
            e = c.recip(s_[:, 2:3], s_[:, 1:2], e)
            e = c.ts(c.dve, x, x, s_[:, 2:3], None, ALU.mult, None, e)
            stage[("p", r)] = (k, e)
            stage["bt"] = e

        def turn(r):
            k, e = stage.pop(("p", r))
            b, bf = banks.take()
            for j in range(4):
                t = c.tr(c.P[b][:, j * 128:(j + 1) * 128], E[:, k, j * 128:(j + 1) * 128], c.ident, bf, e, sig=(j == 3))
            ering.give(k, t)
            k, pf = pring.take()
            e = c.act_(PT[:, k, :], c.P[b][:, :], ACT.Copy, t, pf)
            banks.give(b, e)
            stage[("t", r)] = (k, e)

        def values(r):
            nonlocal ofree, sgfree
            r0 = min(max(r - 4, 0), 24)
            tb = r // 8
            if r % 8 == 0:
                stage["sg"] = c.dma(c.sp, SG[:, 0, :], GD[8 + pr][:, tb * 512:(tb + 1) * 512], S(14), sgfree)
            k, e = stage.pop(("t", r))
            vv = VO if r0 % 2 else V
            for hh in range(2):
                for j in range(4):
                    t = c.mm(c.P[OBANK][64 * hh:64 * hh + 64, (r % 8) * 64:(r % 8) * 64 + 64],
                             vv[:, r0 // 2 + j, hh * 64:(hh + 1) * 64],
                             PT[:, k, j * 128 + 64 * hh:j * 128 + 64 * hh + 64],
                             j == 0, j == 3, ofree, e, tv0[pr], tv1[pr] if r0 > 8 else None, sig=(hh == 1 and j == 3))
            pring.give(k, t)
            stage["v"] = t
            if r % 8 == 7:
                y, yf = yring.take()
                e = c.tt(c.dve, YS[:, y, :], c.P[OBANK][:, :], SG[:, 0, :], ALU.mult, t, stage["sg"], yf)
                ofree = e
                sgfree = e
                yring.give(y, c.dma(c.sp, Y[pr][:, tb * 512:(tb + 1) * 512], YS[:, y, :], S(16 + y), e))

        for r in range(35):
            if r < 32:
                scores(r)
            if 1 <= r < 33:
                divide(r - 1)
            if 2 <= r < 34:
                turn(r - 2)
            if r >= 3:
                values(r - 3)
            if pr < 3 and r == 8:
                early_loads(pr + 1)
            if pr < 3 and r == 26:
                tv0[pr + 1] = value_loads(pr + 1, 0, stage["v"])
            if pr < 3 and r == 30:
                biases(pr + 1)
            yield
        bfree[pp] = stage["bt"]
        qkfree[pp] = stage["qk"]
        if pr < 3:
            tv1[pr + 1] = value_loads(pr + 1, 1, stage["v"])


def recurrence(c, A, off, sem0, Y, GD, KB, IR):
    o = [off]

    def al(n):
        o[0] += n
        return o[0] - n

    LQ, LK, LB, LW = (c.view(al(1024), 2, 512) for _ in range(4))
    X0, X1, X2, QD, KD, KE, QE = (c.view(al(1536), 3, 512) for _ in range(7))
    K32 = [c.view(al(1024), 2, 512) for _ in range(2)]
    VH = c.view(al(4096), 2, 16, 128)
    O = c.view(al(2048), 2048)
    AT, KDT = c.view(al(1024), 2, 512), c.view(al(1024), 2, 512)
    SS = c.view(al(1024), 8, 128)
    dec = c.view(al(12), 3, 4)
    NF = c.view(al(1536), 3, 512)
    OB, banks = 4, Ring(3)
    S = lambda i: c.dsem_of(sem0 + i)
    tz = [c.ms(c.pool, K32[0][:, :, :], 0.0), c.ms(c.pool, K32[1][:, :, :], 0.0)]
    gain = c.col("hg_norm_gain_3")
    v3 = lambda v, m: v.rearrange("p (n x) -> p n x", x=m)
    lring, ering, aring, kring = Ring(2), Ring(3), Ring(2), Ring(2)
    k32free = {}
    nfree = None
    obfree = None
    vfree, ofree = [None, None], {}
    ssfree = [None] * 8
    gsem = [S(20), S(21)]
    ysem = [S(22), S(23)]

    def take():
        i, f = banks.take()
        return 5 + i, f

    def give(b, *t):
        banks.give(b - 5, *t)

    units = [(hd, d, gi) for hd in range(4) for d in range(2) for gi in range(4)]
    L, EL, tvh, state = {}, {}, {}, {}
    pend = None

    def load(n):
        hd, d, gi = units[n]
        g = gi if d == 0 else 3 - gi
        sl = slice(g * 512, (g + 1) * 512)
        if d == 0 and gi == 0:
            tvh[hd] = c.dma(c.sp, VH[:, hd % 2, :, :], IR[:, hd * 128:(hd + 1) * 128].rearrange("(n p) x -> p n x", p=128),
                            S(24 + hd % 2), vfree[hd % 2])
        r, rf = lring.take()
        tq = c.dma(c.sp, LQ[:, r, :], GD[12 + hd][:, sl], S(4 * r), rf)
        tk = c.dma(c.sp, LK[:, r, :], KB[4 * d + hd][:, sl], S(4 * r + 1), rf)
        tb = c.dma(c.sp, LB[:, r, :], KB[8 + 4 * d + hd][:, sl], S(4 * r + 2), rf)
        tw = tb if d == 0 else c.dma(c.sp, LW[:, r, :], KB[16 + hd][:, sl], S(4 * r + 3), rf)
        L[n] = (r, tq, tk, tb, tw)

    def elements(n):
        hd, d, gi = units[n]
        fwd = d == 0
        r, tq, tk, tb, tw = L.pop(n)
        s, sf = ering.take()
        q, kk, bb = LQ[:, r, :], LK[:, r, :], LB[:, r, :]
        w = bb if fwd else LW[:, r, :]
        op = ALU.subtract if fwd else ALU.add
        lv = []
        for B, X in ((128, X0), (64, X1), (32, X2)):
            h = B // 2
            qs, ks = (slice(h, B), slice(0, h)) if fwd else (slice(0, h), slice(h, B))
            x = v3(X[:, s, :], B)
            kd = x if B > 32 else v3(K32[d][:, n % 2, :], 32)
            ref = v3(bb, B)[:, :, h - 1:h].to_broadcast([128, 512 // B, B])
            e = c.tt(c.dve, x, v3(w, B), ref, op, tw, tb, sf)
            e2 = c.act_(kd[:, :, ks], x[:, :, ks], ACT.Exp, e, sf, tz, k32free.get(n - 2), scale=-1.0)
            e1 = c.act_(x[:, :, qs], x[:, :, qs], ACT.Exp, e)
            e2 = c.tt(c.pool, kd[:, :, ks], kd[:, :, ks], v3(kk, B)[:, :, ks], ALU.mult, e2, tk)
            lv.append([B, x, kd, qs, ks, [e1, e2]])
        qd, kd, ke, qe = (v[:, s, :] for v in (QD, KD, KE, QE))
        ref = v3(bb, 16)[:, :, 7:8].to_broadcast([128, 32, 16])
        ed = c.tt(c.dve, v3(qd, 16), v3(w, 16), ref, op, sf)
        last = v3(bb, 128)[:, :, 127:128].to_broadcast([128, 4, 128])
        if fwd:
            el = c.tt(c.dve, v3(ke, 128), v3(w, 128), last, ALU.subtract, sf)
        else:
            el = c.tt(c.dve, v3(qe, 128), v3(w, 128), last, ALU.add, sf)
        for l in lv:
            B, x, _, qs, _, te = l
            te[0] = c.tt(c.dve, x[:, :, qs], x[:, :, qs], v3(q, B)[:, :, qs], ALU.mult, te[0], tq)
        yield
        e2 = c.act_(kd, qd, ACT.Exp, ed, sf, scale=-1.0)
        e1 = c.act_(qd, qd, ACT.Exp, ed, e2)
        if fwd:
            f2 = c.act_(ke, ke, ACT.Exp, el, scale=-1.0)
            f1 = c.act_(qe, w, ACT.Exp, sf, tw)
        else:
            f2 = c.act_(ke, w, ACT.Exp, sf, tw, scale=-1.0)
            f1 = c.act_(qe, qe, ACT.Exp, el)
        e2 = c.tt(c.pool, kd, kd, kk, ALU.mult, e2)
        f2 = c.tt(c.pool, ke, ke, kk, ALU.mult, f2)
        e1 = c.tt(c.dve, qd, qd, q, ALU.mult, e1)
        td = [e1, e2]
        f1 = c.tt(c.dve, qe, qe, q, ALU.mult, f1)
        fd = c.act_(dec[:, s, :], v3(bb, 128)[:, :, 127], ACT.Exp, sf)
        lring.give(r, e1, e2, f1, f2, fd)
        EL[n] = (s, lv, td, f1, f2, fd)

    def outputs(n, ar_, ta, states):
        nonlocal vfree
        hd, d, gi = units[n]
        s, f1 = states["s"], states["f1"]
        g = gi if d == 0 else 3 - gi
        order = range(4) if d == 0 else range(3, -1, -1)
        b, bf = take()
        for m, j in enumerate(order):
            ci = 4 * g + j
            ps = slice(j * 128, (j + 1) * 128)
            first = gi == 0 and m == 0
            if not first:
                sl_, st_ = states[j]
                c.mm(c.P[b][:, ps], SS[:, sl_, :], QE[:, s, ps], True, False, bf, f1, st_)
            t = c.mm(c.P[b][:, ps], VH[:, hd % 2, ci, :], AT[:, ar_, ps], first, True, bf, tvh[hd], ta, sig=True)
            if not first:
                ssfree[sl_] = t
        aring.give(ar_, t)
        ering.give(s, t)
        sl = slice(g * 512, (g + 1) * 512)
        if d == 0:
            e = c.act_(O[:, sl], c.P[b][:, :], ACT.Copy, t, ofree.get(g))
        else:
            e = c.tt(c.dve, O[:, sl], O[:, sl], c.P[b][:, :], ALU.add, t, state[("o", hd, g)])
        state[("o", hd, g)] = e
        give(b, e)
        if d == 1 and gi == 3:
            vfree[hd % 2] = t

    def products(n):
        nonlocal obfree, pend
        hd, d, gi = units[n]
        fwd = d == 0
        s, lv, td, f1, f2, fd = EL.pop(n)
        g = gi if fwd else 3 - gi
        c.mm(c.P[OB][:, :], c.zb[:, 0:128], c.zb[:, :], True, False, obfree, c.t_const)
        for B, x, kd, qs, ks, te in lv:
            h = B // 2
            for bl in range(512 // B):
                j, i = bl * B // 128, bl * B % 128
                k0 = i + ks.start if B > 32 else i
                m = h if B > 32 else 32
                lhs = kd[:, bl, ks] if B > 32 else kd[:, bl, :]
                q0 = bl * B + qs.start
                c.mm(c.P[OB][k0:k0 + m, q0:q0 + h], lhs, x[:, bl, qs], False, False, te)
        toff = c.mm(c.P[OB][:, :], c.zb[:, 0:128], c.zb[:, :], False, True, sig=True)
        k32free[n] = toff
        b, bf = take()
        for j in range(4):
            ps = slice(j * 128, (j + 1) * 128)
            t = c.mm(c.P[b][:, ps], KD[:, s, ps], QD[:, s, ps], True, True, bf, td, sig=(j == 3))
        r, rf = aring.take()
        obfree = c.act_(AT[:, r, :], c.P[OB][:, :], ACT.Copy, toff, rf)
        a_, m_, p_ = (AT[:, r, :].rearrange("p (a b) -> p a b", b=128),
                      c.pair[:, d, :].unsqueeze(1).to_broadcast([128, 4, 128]),
                      c.P[b][:, :].rearrange("p (a b) -> p a b", b=128))
        ta = c.dve.do(lambda en: en.copy_predicated(a_, m_, p_), obfree, t)
        give(b, ta)
        b, bf = take()
        for j in range(4):
            ps = slice(j * 128, (j + 1) * 128)
            t = c.tr(c.P[b][:, ps], KE[:, s, ps], c.ident, bf, f2, sig=(j == 3))
        kr_, kf = kring.take()
        tkd = c.act_(KDT[:, kr_, :], c.P[b][:, :], ACT.Copy, t, kf)
        give(b, tkd)
        yield
        if pend is not None:
            outputs(*pend)
        yield
        b, bf = take()
        for j in range(4):
            ci = 4 * g + j
            t = c.mm(c.P[b][:, j * 128:(j + 1) * 128], KDT[:, kr_, j * 128:(j + 1) * 128], VH[:, hd % 2, ci, :], True,
                     True, bf, tkd, tvh[hd], sig=(j == 3))
        kring.give(kr_, t)
        states = {"s": s, "f1": f1}
        e = None
        for m, j in enumerate(range(4) if fwd else range(3, -1, -1)):
            at = 4 * gi + m
            if at:
                states[j] = (at % 8, state["t"])
            if at == 15:
                continue
            u = c.P[b][:, j * 128:(j + 1) * 128]
            nx = (at + 1) % 8
            if at == 0:
                e = c.cp(c.dve, SS[:, nx, :], u, t, ssfree[nx])
            else:
                e = c.stt(SS[:, nx, :], SS[:, at % 8, :], dec[:, s, j:j + 1], u, ALU.mult, ALU.add, t, fd, state["t"],
                          ssfree[nx])
            state["t"] = e
        give(b, e)
        pend = (n, r, ta, states)

    def finish(hd):
        nonlocal nfree
        for tb in range(4):
            sl = slice(tb * 512, (tb + 1) * 512)
            sf = nfree
            sg, sq, rs = (NF[:, i, :] for i in range(3))
            yo = O[:, sl]
            tg = c.dma(c.sp, sg, GD[16 + hd][:, sl], gsem[tb % 2], sf)
            e = c.act_(sq, yo, ACT.Square, state[("o", hd, tb)], sf)
            b, bf = take()
            t = c.mm(c.P[b][:, :], c.ones, sq, True, True, bf, e, sig=True)
            e = rsqrt(c, rs, c.P[b][:, :], 1.0 / 128, t)
            give(b, e)
            yield
            e = c.stt(yo, yo, gain[:, hd:hd + 1], rs, ALU.mult, ALU.mult, e)
            e = c.tt(c.dve, yo, yo, sg, ALU.mult, e, tg)
            ofree[tb] = c.dma(c.sp, Y[4 + hd][:, sl], yo, ysem[tb % 2], e)
            nfree = [e, t]
            yield

    load(0)
    load(1)
    for _ in elements(0):
        yield
    for n in range(32):
        if n + 1 < 32:
            for _ in elements(n + 1):
                yield
        if n + 2 < 32:
            load(n + 2)
        yield
        for _ in products(n):
            yield
        yield
        if n % 8 == 0 and n:
            for _ in finish(n // 8 - 1):
                yield
    outputs(*pend)
    for _ in finish(3):
        yield


def output3(c, A, X2, out, Y):
    R0, R2 = c.R0, c.R2
    LD = c.view(R2, 2, 1024)
    YP = [(c.view(R2 + 2048 + 2048 * q, 1024, r=True), c.view(R2 + 3072 + 2048 * q, 1024, r=True)) for q in range(2)]
    o = R2 + 6144
    X = c.view(o, 3, 1024)
    T = c.view(o + 3072, 2, 1024)
    bo, lg, lb = (c.view(o + 5120 + 1024 * i, 1024) for i in range(3))
    st = c.view(o + 8192, 2, 16)
    eps = c.view(o + 8224, 1)
    te = c.ms(c.pool, eps, 1e-5)
    wraw = c.view(R0 + 16384, 4, 1024)
    WO, two = load_wo(c, A["w_out_3"][0], R0, 8, wraw, [c.dsem_of(i) for i in range(4)])
    tb = [c.dma(c.act, dst, rows_of(A, n).partition_broadcast(128), c.dsem_of(4 + i))
          for i, (dst, n) in enumerate(((bo, "b_out_3"), (lg, "ln_gain_3"), (lb, "ln_bias_3")))]
    xring, tring = Ring(3), Ring(2)
    xsem = [c.dsem_of(8 + i) for i in range(3)]
    osem = [c.dsem_of(11 + i) for i in range(3)]
    lsem = [c.dsem_of(14 + i) for i in range(2)]
    alpha = 2.0 ** 0.25
    lfree, yfree = [None, None], [None, None]
    ready = {}

    def prep(i):
        q = i % 2
        yh, yl = YP[q]
        t = c.dma(c.sp, LD[:, q, :].rearrange("p (k t) -> p k t", k=8),
                  Y[0:8, :, i * 128:(i + 1) * 128].rearrange("k p t -> p k t"), lsem[q], lfree[q])
        e = c.act_(yh, LD[:, q, :], ACT.Copy, t, yfree[q])
        e1 = c.tt(c.dve, yl, LD[:, q, :], yh, ALU.subtract, e, t)
        lfree[q] = e1
        ready[i] = [e, e1]

    prep(0)
    prep(1)
    for i in range(16):
        yh, yl = YP[i % 2]
        bb, t = out_tile(c, 8, lambda k: yh[:, k * 128:(k + 1) * 128], lambda k: yl[:, k * 128:(k + 1) * 128],
                         lambda k: ready[i], WO, two)
        yfree[i % 2] = t
        r, xf = xring.take()
        q, tf = tring.take()
        X_, T_, s = X[:, r, :], T[:, q, :], st[:, q, :]
        tx = c.dma(c.sp, X_, X2[i * 128:(i + 1) * 128, :], xsem[r], xf)
        for h in range(2):
            sl = slice(h * 512, (h + 1) * 512)
            e = c.tt(c.dve, T_[:, sl], c.P[bb[h]][:, :], bo[:, sl], ALU.add, t, tb, tf)
            c.banks.give(bb[h], e)
        e = c.stt(X_, X_, alpha, T_, ALU.mult, ALU.add, e, tx)
        for h in range(2):
            o_, a_ = s[:, 6 * h:6 * h + 6], X_[:, h * 512:(h + 1) * 512]
            e1 = c.dve.do(lambda en, o_=o_, a_=a_: en.bn_stats(o_, a_), e)
        o_, a_ = s[:, 12:14], s[:, 0:12]
        e1 = c.dve.do(lambda en, o_=o_, a_=a_: en.bn_aggr(o_, a_), e1)
        v = s[:, 14:15]
        e2 = c.act_(v, s[:, 13:14], ACT.Ln, e1, te, bias=eps)
        e2 = c.act_(v, v, ACT.Exp, e2, scale=-0.5)
        e3 = c.ts(c.dve, T_, X_, s[:, 12:13], v, ALU.subtract, ALU.mult, e2, e1)
        e4 = c.tt(c.pool, T_, T_, lg, ALU.mult, e3, tb)
        e5 = c.tt(c.pool, X_, T_, lb, ALU.add, e4, e3)
        d = c.dma(c.act, out[i * 128:(i + 1) * 128, :], X_, osem[r], e5)
        xring.give(r, d)
        tring.give(q, e5)
        if i + 2 < 16:
            prep(i + 2)


def program(nc, A, out):
    with ExitStack() as ctx:
        c = setup(nc, ctx)
        c.top = 0

        def take(n):
            c.top += n
            assert c.top <= 1330
            return c.top - n

        c.take = take
        c.wsems = [c.dsem() for _ in range(8)]
        pool_ = {}

        def dsem_of(i):
            if i not in pool_:
                pool_[i] = c.dsem()
            return pool_[i]

        c.dsem_of = dsem_of
        c.ident = c.view(take(128), 128)[:, :]
        c.ones = c.view(take(128), 128)[:, :]
        c.eps = c.view(take(1), 1)[:, :]
        c.rstd2 = c.view(take(16), 16)
        c.pcol = c.view(take(512), 4, 128)
        c.base = c.top
        c.R0 = 1330
        c.R1 = c.R0 + 16384
        c.R2 = c.R0 + 32768
        ht_views(c)
        c.t_const = [c.dma(c.sp, c.ident, A["k_ident"], c.dsem()),
                     c.ms(c.dve, c.ones, 1.0), c.ms(c.dve, c.eps, EPS), c.ms(c.dve, c.zb[:, :], 0.0),
                     c.dma(c.sp, c.pair[:, :, :], A["k_pair"], c.dsem())]
        for e in (c.pe, c.act, c.dve, c.pool):
            e.wait(c.t_const)
        X1 = nc.dram_tensor("x1_rows", (S_LEN, D), F32, kind="Internal").ap()
        X2 = nc.dram_tensor("x2_rows", (S_LEN, D), F32, kind="Internal").ap()
        Y = nc.dram_tensor("y_tiles", (16, 128, S_LEN), F32, kind="Internal").ap()
        GD = nc.dram_tensor("g_tiles", (24, 128, S_LEN), F32, kind="Internal").ap()

        def finish():
            c.fence()
            block = ctx.enter_context(nc.Block())

            @block.sync
            def _(e):
                c.sp.emit(e)

            @block.scalar
            def _(e):
                c.act.emit(e)

            @block.vector
            def _(e):
                c.dve.emit(e)

            @block.gpsimd
            def _(e):
                c.pool.emit(e)

            @block.tensor
            def _(e):
                c.pe.emit(e)

        block1(c, A, X1, Y, GD)
        block2(c, A, X1, X2, Y, GD)
        block3(c, A, X2, out, Y, GD)
        finish()


def constants():
    k = {"k_ident": np.eye(128, dtype=np.float32)}
    k.update(transform_constants())
    k.update(window_constants())
    return k


NAMES = ["x", "c", "w_ada", "b_ada", "norm_g", "w_in", "conv_w", "conv_b", "conv_ln_g", "conv_ln_b", "sg_ln_g",
         "sg_ln_b", "w_s", "b_s", "w_out", "final_g", "pre_norm_g_2", "w_in_2", "conv_w_2", "conv_b_2",
         "filt_w1_2", "filt_b1_2", "filt_w2_2", "filt_b2_2", "filt_w3_2", "filt_b3_2", "filt_freq_2",
         "filt_w_out_2", "hyena_d_2", "pool_w_2", "pool_scale_2", "norm_h_g_2", "norm_p_g_2", "w_out_2",
         "post_norm_g_2", "w_in_3", "b_in_3", "rpb_3", "lb_fwd_logits_3", "lb_bwd_logits_3", "hg_norm_gain_3",
         "w_out_3", "b_out_3", "ln_gain_3", "ln_bias_3"]


def kernel(**inputs):
    import concourse.bacc as bacc
    from concourse.bass_utils import run_bass_kernel_spmd

    nc = bacc.Bacc("TRN2", target_bir_lowering=False, num_devices=1)
    arrays, A = {}, {}
    for name in NAMES:
        arrays[f"in_{name}"] = np.ascontiguousarray(inputs[name])
    for name, a in constants().items():
        arrays[f"in_{name}"] = a
    for name, a in arrays.items():
        A[name[3:]] = nc.dram_tensor(name, a.shape, mybir.dt.from_np(a.dtype), kind="ExternalInput").ap()
    out = nc.dram_tensor("out_rows", (S_LEN, D), F32, kind="ExternalOutput").ap()
    program(nc, A, out)
    r = run_bass_kernel_spmd(nc, [arrays], core_ids=[0])
    return r.results[0]["out_rows"].reshape(1, S_LEN, D)
```
